# Optimizing a Trainium2 kernel written in Bass

```python
import math
import jax
import jax.numpy as jnp
from jax import lax
import numpy as np

'''Hybrid bidirectional encoder block: post-norm DeepNorm residuals with adaLN conditioning.

Inputs:  x (BATCH, SEQ, D_MODEL) float32, c (BATCH, D_MODEL) float32,
         positions (BATCH, SEQ) int32, plus per-layer weights stacked on a leading DEPTH axis.
Output:  (BATCH, SEQ, D_MODEL).

Per layer:
  token-mixing sub-layer: u = x * (1 + scale_c) + shift_c; one combined projection of u is split into
    (a) Hyena order-2 bidirectional long convolution branch (512 channels; implicit two-sided filters via rfft/irfft),
    (b) LongNet-style dilated sliding-window attention (3 dilation groups x 4 heads x 64 dims, partial rotary),
        the 3 groups combined per head slot by their softmax denominators,
    (c) two per-channel sigmoid branch gates;
    each branch is projected to D_MODEL, gated, summed, output-projected;
    x <- LN(alpha * x + (1 + gate_c) * mix)
  channel sub-layer: PEER product-key retrieval (8 heads, 128^2 single-neuron experts, top-16 per head);
    x <- LN(alpha * x + (1 + gate_c) * peer(x * (1 + scale_c) + shift_c))
'''

D_MODEL = 1024
BATCH = 1
SEQ = 1024
DEPTH = 1

HEAD_DIM = 64
HEADS_PER_GROUP = 4
DILATION_GROUPS = ((128, 1), (512, 4), (2048, 16))
N_GROUPS = len(DILATION_GROUPS)
ATTN_WIDTH = N_GROUPS * HEADS_PER_GROUP * HEAD_DIM
ATTN_OUT = HEADS_PER_GROUP * HEAD_DIM
ROPE_THETA = 500000.0
ROPE_DIM = HEAD_DIM // 4
NEG_BIG = -1e30

HYENA_WIDTH = D_MODEL // 2
HYENA_ORDER = 2
HYENA_EMB = 33
HYENA_BANDS = (HYENA_EMB - 1) // 2
HYENA_FILTER_HIDDEN = 64
HYENA_SHORT = 3
HYENA_DECAY_SHORT_PCT = 0.3
HYENA_DECAY_LONG_PCT = 1.5
HYENA_DECAY_TARGET = 1e-2
HYENA_FILTER_INIT = 0.05

PEER_HEADS = 8
PEER_NKEYS = 128
PEER_EXPERTS = PEER_NKEYS * PEER_NKEYS
PEER_KEY_DIM = 128
PEER_TOPK = 16
PEER_CHUNK = 128

N_BRANCH = 2
IN_WIDTH = (HYENA_ORDER + 1) * HYENA_WIDTH + 3 * ATTN_WIDTH + N_BRANCH * D_MODEL
DN_ALPHA = (2.0 * DEPTH) ** 0.25
DN_BETA = (8.0 * DEPTH) ** -0.25
ADA_INIT = 0.2
LN_EPS = 1e-5

kernel_name = 'hybrid_hyena_dilated_attn_peer_encoder'

def layer_norm(x, g, b):
    xf = x.astype(jnp.float32)
    mu = jnp.mean(xf, axis=-1, keepdims=True)
    var = jnp.mean(jnp.square(xf - mu), axis=-1, keepdims=True)
    y = (xf - mu) * lax.rsqrt(var + LN_EPS) * g.astype(jnp.float32) + b.astype(jnp.float32)
    return y.astype(x.dtype)

def short_conv(z, w, b):
    zp = jnp.pad(z, ((0, 0), (1, 1), (0, 0)))
    return zp[:, :-2] * w[0] + zp[:, 1:-1] * w[1] + zp[:, 2:] * w[2] + b

def hyena_filters(L, f1_w, f1_b, f1_freq, f2_w, f2_b, f2_freq, f3_w):
    f32 = jnp.float32
    t = jnp.linspace(0.0, 1.0, L, dtype=f32)[:, None]
    w = 2.0 * math.pi * jnp.arange(L, dtype=f32)[:, None] / L
    f = jnp.linspace(1e-4, HYENA_BANDS - 1, HYENA_BANDS, dtype=f32)[None, :]
    z = jnp.concatenate([t, jnp.cos(f * w), -jnp.sin(f * w)], axis=-1)
    h = jnp.sin(f1_freq.astype(f32) * (z @ f1_w.astype(f32) + f1_b.astype(f32)))
    h = jnp.sin(f2_freq.astype(f32) * (h @ f2_w.astype(f32) + f2_b.astype(f32)))
    h = (h @ f3_w.astype(f32)).reshape(L, 2, HYENA_ORDER, HYENA_WIDTH)
    max_decay = math.log(HYENA_DECAY_TARGET) / HYENA_DECAY_SHORT_PCT
    min_decay = math.log(HYENA_DECAY_TARGET) / HYENA_DECAY_LONG_PCT
    deltas = jnp.linspace(min_decay, max_decay, HYENA_WIDTH, dtype=f32)
    decay = jnp.exp(-t * jnp.abs(deltas)[None, :])
    h = h * decay[:, None, None, :]
    fwd, bwd = h[:, 0], h[:, 1]
    k2 = jnp.concatenate([fwd, jnp.zeros((1, HYENA_ORDER, HYENA_WIDTH), f32), bwd[:0:-1]], axis=0)
    return jnp.fft.rfft(k2, axis=0)

def long_conv(z, kf, bias):
    L = z.shape[1]
    zf = jnp.fft.rfft(z.astype(jnp.float32), n=2 * L, axis=1)
    y = jnp.fft.irfft(zf * kf[None], n=2 * L, axis=1)[:, :L]
    return (y + z.astype(jnp.float32) * bias.astype(jnp.float32)).astype(z.dtype)

def hyena_mixer(p_h, conv_w, conv_b, f1_w, f1_b, f1_freq, f2_w, f2_b, f2_freq, f3_w, bias):
    zc = short_conv(p_h, conv_w, conv_b)
    v, x1, x2 = jnp.split(zc, 3, axis=-1)
    K = hyena_filters(p_h.shape[1], f1_w, f1_b, f1_freq, f2_w, f2_b, f2_freq, f3_w)
    z = v
    for o, gate in enumerate((x1, x2)):
        z = gate * long_conv(z, K[:, o], bias[o])
    return z

def rotary(t, positions):
    f32 = jnp.float32
    inv = ROPE_THETA ** (-jnp.arange(0, ROPE_DIM, 2, dtype=f32) / ROPE_DIM)
    ang = positions.astype(f32)[..., None] * inv
    cos = jnp.cos(ang)[:, :, None, :]
    sin = jnp.sin(ang)[:, :, None, :]
    half = ROPE_DIM // 2
    t1 = t[..., :half].astype(f32)
    t2 = t[..., half:ROPE_DIM].astype(f32)
    out = jnp.concatenate([t1 * cos - t2 * sin, t2 * cos + t1 * sin, t[..., ROPE_DIM:].astype(f32)], axis=-1)
    return out.astype(t.dtype)

def dilated_window_attention(q, k, v, dilation, half):
    B, S, H, E = q.shape
    n = S // dilation
    blk = half
    nb = -(-n // blk)
    n_pad = nb * blk
    f32 = jnp.float32

    def to_blocks(t):
        t = t.reshape(B, n, dilation, H, E).transpose(0, 2, 1, 3, 4)
        t = jnp.pad(t, ((0, 0), (0, 0), (0, n_pad - n), (0, 0), (0, 0)))
        return t.reshape(B, dilation, nb, blk, H, E)

    def windows(t):
        tp = jnp.pad(t, ((0, 0), (0, 0), (1, 1), (0, 0), (0, 0), (0, 0)))
        return jnp.concatenate([tp[:, :, :-2], tp[:, :, 1:-1], tp[:, :, 2:]], axis=3)

    def from_blocks(t):
        t = t.reshape((B, dilation, n_pad) + t.shape[4:])[:, :, :n]
        t = jnp.swapaxes(t, 1, 2)
        return t.reshape((B, S) + t.shape[3:])

    qb = to_blocks(q).astype(f32) * (E ** -0.5)
    kw = windows(to_blocks(k)).astype(f32)
    vw = windows(to_blocks(v)).astype(f32)
    s = jnp.einsum('brnqhe,brnkhe->brnhqk', qb, kw)
    qi = jnp.arange(nb)[:, None] * blk + jnp.arange(blk)[None, :]
    kj = (jnp.arange(nb)[:, None] - 1) * blk + jnp.arange(3 * blk)[None, :]
    mask = (jnp.abs(qi[:, :, None] - kj[:, None, :]) <= half) & (kj[:, None, :] >= 0) & (kj[:, None, :] < n)
    mask = mask[None, None, :, None]
    s = jnp.where(mask, s, NEG_BIG)
    m = jnp.max(s, axis=-1)
    p = jnp.where(mask, jnp.exp(s - m[..., None]), 0.0)
    l = jnp.sum(p, axis=-1)
    acc = jnp.einsum('brnhqk,brnkhe->brnqhe', p, vw)
    acc = from_blocks(acc)
    m = from_blocks(jnp.swapaxes(m, 3, 4))
    l = from_blocks(jnp.swapaxes(l, 3, 4))
    return acc, m, l

def attention_mixer(qkv, positions):
    B, S, _ = qkv.shape
    qkv = qkv.reshape(B, S, 3, N_GROUPS * HEADS_PER_GROUP, HEAD_DIM)
    q = rotary(qkv[:, :, 0], positions)
    k = rotary(qkv[:, :, 1], positions)
    v = qkv[:, :, 2]
    accs, ms, ls = [], [], []
    for g, (window, dilation) in enumerate(DILATION_GROUPS):
        hs = slice(g * HEADS_PER_GROUP, (g + 1) * HEADS_PER_GROUP)
        a, m, l = dilated_window_attention(q[:, :, hs], k[:, :, hs], v[:, :, hs], dilation, window // (2 * dilation))
        accs.append(a)
        ms.append(m)
        ls.append(l)
    ms = jnp.stack(ms)
    wts = jnp.exp(ms - jnp.max(ms, axis=0, keepdims=True))
    num = jnp.sum(wts[..., None] * jnp.stack(accs), axis=0)
    den = jnp.sum(wts * jnp.stack(ls), axis=0)
    out = num / den[..., None]
    return out.reshape(B, S, ATTN_OUT).astype(qkv.dtype)

def peer(u, wq, keys, utab, vtab):
    B, S, D = u.shape
    T = B * S
    xt = u.reshape(T, D)
    q = (xt @ wq).reshape(T, PEER_HEADS, 2, PEER_KEY_DIM)
    s = jnp.einsum('thpe,hpke->thpk', q.astype(jnp.float32), keys.astype(jnp.float32))
    sv, si = lax.top_k(s, PEER_TOPK)
    cand = (sv[:, :, 0, :, None] + sv[:, :, 1, None, :]).reshape(T, PEER_HEADS, PEER_TOPK * PEER_TOPK)
    cidx = (si[:, :, 0, :, None] * PEER_NKEYS + si[:, :, 1, None, :]).reshape(T, PEER_HEADS, PEER_TOPK * PEER_TOPK)
    tv, ti = lax.top_k(cand, PEER_TOPK)
    eidx = jnp.take_along_axis(cidx, ti, axis=-1)
    g = jax.nn.softmax(tv, axis=-1)
    nc = T // PEER_CHUNK
    eidx = eidx.reshape(nc, PEER_CHUNK, PEER_HEADS * PEER_TOPK)
    g = g.reshape(nc, PEER_CHUNK, PEER_HEADS * PEER_TOPK)
    xc = xt.reshape(nc, PEER_CHUNK, D)

    def chunk(args):
        xb, ib, gb = args
        a = jnp.einsum('cd,ced->ce', xb, utab[ib]).astype(jnp.float32)
        coef = (gb * jax.nn.gelu(a, approximate=False)).astype(xb.dtype)
        return jnp.einsum('ce,ced->cd', coef, vtab[ib])

    return lax.map(chunk, (xc, eidx, g)).reshape(B, S, D)

def setup_inputs(seed: int = 0) -> dict:
    key = jax.random.key(seed)
    ks = jax.random.split(key, 32)
    f32 = jnp.float32

    def nrm(k, shape, scale):
        return jax.random.normal(k, shape, f32) * scale

    L, D, HW, HFH = DEPTH, D_MODEL, HYENA_WIDTH, HYENA_FILTER_HIDDEN
    return {
        'x': nrm(ks[0], (BATCH, SEQ, D), 1.0),
        'c': nrm(ks[1], (BATCH, D), 1.0),
        'positions': jnp.broadcast_to(jnp.arange(SEQ, dtype=jnp.int32)[None, :], (BATCH, SEQ)),
        'w_ada': nrm(ks[2], (L, D, 6 * D), ADA_INIT * D ** -0.5),
        'b_ada': nrm(ks[3], (L, 6 * D), 0.02),
        'w_in': nrm(ks[4], (L, D, IN_WIDTH), D ** -0.5),
        'hy_conv_w': nrm(ks[5], (L, HYENA_SHORT, 3 * HW), HYENA_SHORT ** -0.5),
        'hy_conv_b': nrm(ks[6], (L, 3 * HW), 0.02),
        'hy_f1_w': nrm(ks[7], (L, HYENA_EMB, HFH), HYENA_EMB ** -0.5),
        'hy_f1_b': nrm(ks[8], (L, HFH), 0.1),
        'hy_f1_freq': 1.0 + nrm(ks[9], (L, HFH), 0.01),
        'hy_f2_w': nrm(ks[10], (L, HFH, HFH), HFH ** -0.5),
        'hy_f2_b': nrm(ks[11], (L, HFH), 0.1),
        'hy_f2_freq': 1.0 + nrm(ks[12], (L, HFH), 0.01),
        'hy_f3_w': nrm(ks[13], (L, HFH, 2 * HYENA_ORDER * HW), HYENA_FILTER_INIT * HFH ** -0.5),
        'hy_bias': nrm(ks[14], (L, HYENA_ORDER, HW), 1.0),
        'w_branch_hyena': nrm(ks[15], (L, HW, D), HW ** -0.5),
        'w_branch_attn': nrm(ks[16], (L, ATTN_OUT, D), ATTN_OUT ** -0.5),
        'w_out': nrm(ks[17], (L, D, D), DN_BETA * D ** -0.5),
        'ln1_g': 1.0 + nrm(ks[18], (L, D), 0.01),
        'ln1_b': nrm(ks[19], (L, D), 0.01),
        'peer_wq': nrm(ks[20], (L, D, PEER_HEADS * 2 * PEER_KEY_DIM), D ** -0.5),
        'peer_keys': nrm(ks[21], (L, PEER_HEADS, 2, PEER_NKEYS, PEER_KEY_DIM), PEER_KEY_DIM ** -0.5),
        'peer_u': nrm(ks[22], (L, PEER_EXPERTS, D), D ** -0.5),
        'peer_v': nrm(ks[23], (L, PEER_EXPERTS, D), DN_BETA),
        'ln2_g': 1.0 + nrm(ks[24], (L, D), 0.01),
        'ln2_b': nrm(ks[25], (L, D), 0.01),
    }

def reference(x, c, positions, w_ada, b_ada, w_in, hy_conv_w, hy_conv_b, hy_f1_w, hy_f1_b, hy_f1_freq,
              hy_f2_w, hy_f2_b, hy_f2_freq, hy_f3_w, hy_bias, w_branch_hyena, w_branch_attn, w_out,
              ln1_g, ln1_b, peer_wq, peer_keys, peer_u, peer_v, ln2_g, ln2_b):
    hy_cols = (HYENA_ORDER + 1) * HYENA_WIDTH
    attn_cols = 3 * ATTN_WIDTH
    for l in range(DEPTH):
        ada = jax.nn.silu(c) @ w_ada[l] + b_ada[l]
        sh1, sc1, g1, sh2, sc2, g2 = jnp.split(ada[:, None, :], 6, axis=-1)

        u = x * (1.0 + sc1) + sh1
        proj = u @ w_in[l]
        p_h, p_qkv, p_gate = jnp.split(proj, [hy_cols, hy_cols + attn_cols], axis=-1)
        y_h = hyena_mixer(p_h, hy_conv_w[l], hy_conv_b[l], hy_f1_w[l], hy_f1_b[l], hy_f1_freq[l],
                          hy_f2_w[l], hy_f2_b[l], hy_f2_freq[l], hy_f3_w[l], hy_bias[l])
        y_a = attention_mixer(p_qkv, positions)
        gate_h, gate_a = jnp.split(jax.nn.sigmoid(p_gate), 2, axis=-1)
        merged = gate_h * (y_h @ w_branch_hyena[l]) + gate_a * (y_a @ w_branch_attn[l])
        x = layer_norm(DN_ALPHA * x + (1.0 + g1) * (merged @ w_out[l]), ln1_g[l], ln1_b[l])

        u2 = x * (1.0 + sc2) + sh2
        f = peer(u2, peer_wq[l], peer_keys[l], peer_u[l], peer_v[l])
        x = layer_norm(DN_ALPHA * x + (1.0 + g2) * f, ln2_g[l], ln2_b[l])
    return x


_drawn_inputs = setup_inputs


def setup_inputs(seed=0):
    import zlib

    import numpy as np

    out = dict(_drawn_inputs(seed))
    spreads = {}
    factors = {'hy_f1_freq': 7.466, 'hy_f2_freq': 7.204, 'ln2_g': 5.715, 'ln2_b': 5.61}
    for name, (base, spread) in spreads.items():
        noise = np.random.default_rng([zlib.crc32(name.encode()), seed]).standard_normal(out[name].shape)
        drawn = base * np.exp(spread * noise) if base else spread * noise
        out[name] = jnp.asarray(drawn.astype(out[name].dtype))
    for name, factor in factors.items():
        out[name] = (out[name] * factor).astype(out[name].dtype)
    return out
```

```python
import math
from contextlib import ExitStack

import numpy as np

import concourse.bass as bass
from concourse import mybir

F32 = mybir.dt.float32
F32R = mybir.dt.float32r
F16 = mybir.dt.float16
I32 = mybir.dt.int32
U32 = mybir.dt.uint32
ALU = mybir.AluOpType
ACT = mybir.ActivationFunctionType
AX = mybir.AxisListType.X

P = 128
SEQ = 1024
D = 1024
KT = D // P
HALF = 512
HW = 512
HEADS = 12
HD = 64
SLOTS = 4
ROPE = 8
PH = 8
NK = 128
TOPK = 16
ALPHA = 2.0 ** 0.25
EPS = 1e-5
NEG = -1e30
CM_TILES = (3 * HW + 2 * D) // P
HY_TILES = 3 * HW // P
QKV = 3 * HEADS * HD
QC = 384

MAGIC = 1.5 * 2.0 ** 23
TWO_PI = (6.28125, 0.0019340515136718750, 1.2556659146443102e-06)


class Chain:

    def __init__(self, eng, sem):
        self.eng, self.sem, self.base, self.n = eng, sem, 0, 0

    def link(self, ins, K=None):
        self.n += 1
        ins.then_inc(self.sem, 1)
        if K is None:
            self.eng.wait_ge(self.sem, self.base + self.n)
        else:
            hold(self.eng, K, self.sem, self.base + self.n)

    def loop(self, i, per):
        self.start, self.per = self.base + self.n, per
        self.base, self.n = self.start + i * per, 0

    def done(self, times):
        assert self.n == self.per, (self.n, self.per)
        self.base, self.n = self.start + times * self.per, 0


def hold(eng, K, sem, value):
    eng.wait_ge(sem, value)
    eng.sem_inc(K["passed"], 1)


def product3(nc, out, w, x, first, last):
    nc.tensor.matmul(out, w[0], x[0], start=first, stop=False)
    nc.tensor.matmul(out, w[0], x[1], start=False, stop=False)
    return nc.tensor.matmul(out, w[1], x[0], start=False, stop=last)


def cleared_sems(nc, ctx, prefix):
    used = []

    def clear():
        nc.clear_and_free_semaphores(used)
        nc.all_engine_barrier()

    def sem(name):
        used.append(nc.alloc_semaphore(name=prefix + name))
        return used[-1]

    ctx.callback(clear)
    return sem




def sine_prepare(nc, chain, out, turns, src, bias, freq):
    v = nc.vector
    chain.link(v.tensor_scalar(out, src, bias, freq, ALU.add, ALU.mult))
    wrap(nc, chain, out, turns)


def wrap(nc, chain, x, turns):
    v = nc.vector
    chain.link(v.tensor_scalar(turns, x, 1.0 / (2.0 * math.pi), MAGIC, ALU.mult, ALU.add))
    chain.link(v.tensor_scalar(turns, turns, -MAGIC, None, ALU.add))
    for part in TWO_PI:
        chain.link(v.scalar_tensor_tensor(out=x, in0=turns, scalar=-part, in1=x, op0=ALU.mult, op1=ALU.add))
    chain.link(v.tensor_scalar(x, x, -3.1415925, 3.1415925, ALU.max, ALU.min))


def stage_setup(nc, S, K, T):
    ctx = ExitStack()
    with ctx:
        sb = lambda n, s, d=F32: ctx.enter_context(nc.sbuf_tensor("su_" + n, s, d))
        sem = cleared_sems(nc, ctx, "su_")
        feats = sb("feats", [33, SEQ])
        f1w, f2w = sb("f1w", [33, 64]), sb("f2w", [64, 64])
        fvec = sb("fvec", [64, 4])
        arg, turns = sb("arg", [64, SEQ]), sb("turns", [64, SEQ])
        h1 = sb("h1", [64, SEQ])
        pos_i, pos = sb("pos_i", [P, KT], I32), sb("pos", [P, KT])
        inv = sb("inv", [P, ROPE])
        ang = sb("ang", [P, 2, KT, ROPE])
        ang_turns = sb("ang_turns", [P, 2, KT, ROPE])
        cc = sb("cc", [P, KT])
        ps = ctx.enter_context(nc.psum_tensor("su_ps", [64, 2, HALF], F32))
        loads, ready, layer, args_ok, hid = sem("loads"), sem("silu"), sem("layer"), sem("args"), sem("hidden")
        chain_s = sem("chain")
        act_s = sem("act")
        block = ctx.enter_context(nc.Block())

        @block.sync
        def _(sp):
            small = [
                (feats[:, :], T["feats"]), (f1w[:, :], T["f1_w"]), (f2w[:, :], T["f2_w"]),
                (K["f3w"][:, :], T["f3_w"]), (fvec[:, :], T["fvec"]), (pos_i[:, :], T["positions"]),
                (inv[:, :], T["inv"].partition_broadcast(P)), (cc[:, :], T["c"]), (K["ident"][:, :], T["ident"]),
                (K["ada_col"][:, :], T["b_col"]),
                (K["ada_row"][:, :, :], T["b_row"].partition_broadcast(P)),
            ]
            for dst, src in small:
                sp.dma_start(dst, src).then_inc(loads, 16)
            sp.wait_ge(loads, 16 * len(small))
            sp.sem_inc(ready, 1)

        @block.tensor
        def _(pe):
            pe.wait_ge(ready, 1)
            for h in range(2):
                last = nc.tensor.matmul(ps[:, h, :], f1w[:, :], feats[:, h * HALF:(h + 1) * HALF], start=True, stop=True)
            last.then_inc(layer, 1)
            pe.wait_ge(hid, 1)
            for h in range(2):
                last = nc.tensor.matmul(ps[:, h, :], f2w[:, :], h1[:, h * HALF:(h + 1) * HALF], start=True, stop=True)
            last.then_inc(layer, 1)

        @block.vector
        def _(dve):
            ch = Chain(dve, chain_s)
            flat = ps[:, :, :].rearrange("p a b -> p (a b)")
            dve.wait_ge(layer, 1)
            sine_prepare(nc, ch, arg[:, :], turns[:, :], flat, fvec[:, 0:1], fvec[:, 1:2])
            nc.vector.tensor_copy(pos[:, :], pos_i[:, :]).then_inc(args_ok, 1)
            dve.wait_ge(args_ok, 1)
            ch.link(nc.vector.tensor_tensor(ang[:, 1, :, :], pos[:, :].unsqueeze(2).to_broadcast([P, KT, ROPE]),
                                            inv[:, :].unsqueeze(1).to_broadcast([P, KT, ROPE]), ALU.mult))
            ch.link(nc.vector.tensor_scalar(ang[:, 0, :, :], ang[:, 1, :, :], 0.5, None, ALU.mult))
            wrap(nc, ch, ang[:, :, :, :].rearrange("p a b c -> p (a b c)"),
                 ang_turns[:, :, :, :].rearrange("p a b c -> p (a b c)"))
            nc.vector.tensor_copy(pos[:, :], pos_i[:, :]).then_inc(args_ok, 1)
            dve.wait_ge(layer, 2)
            dve.wait_ge(hid, 1)
            sine_prepare(nc, ch, arg[:, :], turns[:, :], flat, fvec[:, 2:3], fvec[:, 3:4])
            nc.vector.tensor_copy(pos[:, :], pos_i[:, :]).then_inc(args_ok, 1)
            dve.wait_ge(act_s, 2)
            sc = K["cos"][:, :, :].rearrange("p a b -> p (a b)")
            ch.link(nc.vector.tensor_tensor(sc, sc, sc, ALU.mult))
            ch.link(nc.vector.tensor_scalar(sc, sc, -2.0, 1.0, ALU.mult, ALU.add))
            ch.link(nc.vector.tensor_copy(K["silu_wide"][:, :, :], K["silu"][:, :].unsqueeze(2).to_broadcast([P, KT, P])))

        @block.scalar
        def _(act):
            act.wait_ge(args_ok, 1)
            nc.scalar.activation(h1[:, :], arg[:, :], ACT.Sin).then_inc(hid, 1)
            act.wait_ge(args_ok, 2)
            nc.scalar.activation(K["cos"][:, :, :], ang[:, 0, :, :], ACT.Sin)
            nc.scalar.activation(K["sin"][:, :, :], ang[:, 1, :, :], ACT.Sin)
            act.wait_ge(args_ok, 3)
            nc.scalar.activation(K["h2"][:, :], arg[:, :], ACT.Sin).then_inc(hid, 1)
            nc.scalar.activation(K["silu"][:, :], cc[:, :], ACT.Silu).then_inc(act_s, 2)


def stage_spectra(nc, S, K, T):
    ctx = ExitStack()
    with ctx:
        sb = lambda n, s, d=F32: ctx.enter_context(nc.sbuf_tensor("sp_" + n, s, d))
        sem = cleared_sems(nc, ctx, "sp_")
        decay = sb("decay", [P, KT, HW])
        fb = sb("fb", [P, 2, HW])
        pm = sb("pm", [P, 2, 2, HW])
        taps_h = sb("taps_h", [P, 2, KT, HW], F32R)
        taps_l = sb("taps_l", [P, 2, KT, HW], F32R)
        tab = sb("tab", [P, 2, 2, KT, P])
        tab_h = sb("tab_h", [P, 2, 2, KT, P], F32R)
        tab_l = sb("tab_l", [P, 2, 2, KT, P], F32R)
        spec = sb("spec", [P, 2, 2, HW])
        wada = sb("wada", [P, 2, KT, 256])
        hps = ctx.enter_context(nc.psum_tensor("sp_hps", [P, 2, HALF], F32))
        sps = ctx.enter_context(nc.psum_tensor("sp_sps", [P, 4, HALF], F32))
        aps = ctx.enter_context(nc.psum_tensor("sp_aps", [P, 2, HALF], F32))
        decay_in, taps_mm, pm_ok, hi_ok, lo_ok = sem("decay_in"), sem("taps_mm"), sem("pm_ok"), sem("hi_ok"), sem("lo_ok")
        tab_hi, tab_ok, spec_mm = sem("tab_hi"), sem("tab_ok"), sem("spec_mm")
        tab_in = [sem(f"tab_in{k}") for k in range(2)]
        stored = [sem(f"stored{k}") for k in range(2)]
        ada_in = [sem(f"ada_in{k}") for k in range(2)]
        cos_out, sin_out = sem("cos_out"), sem("sin_out")
        ada_mm, ada_out, chain_s = sem("ada_mm"), sem("ada_out"), sem("chain")
        block = ctx.enter_context(nc.Block())

        @block.sync
        def _(sp):
            sp.dma_start(decay[:, :, :], T["decay"]).then_inc(decay_in, 16)
            with sp.Fori(0, 2) as o:
                with sp.Fori(0, 2) as h:
                    for q in range(4):
                        n = o * KT + h * 4 + q
                        sp.wait_ge(tab_ok, n + 1)
                        sp.dma_start(tab[:, q % 2, :, :, :], T["tab0"][bass.ds(h * 4 + q, 1)][0]).then_inc(tab_in[q % 2], 16)
                        if q < 3:
                            m = (o * 2 + h) * 3 + q
                            sp.wait_ge(ada_mm, m + 1)
                            for c in range(2):
                                sp.dma_start(wada[:, c, :, :], T["w_ada"][bass.ds(m * 2 + c, 1)][0]).then_inc(ada_in[c], 16)

        @block.gpsimd
        def _(pool):
            pool.sem_inc(lo_ok, 2)
            pool.sem_inc(tab_ok, 2)
            with pool.Fori(0, 2) as o:
                for lt in range(KT):
                    n = o * KT + lt
                    pool.wait_ge(hi_ok, n + 1)
                    for j in range(2):
                        last = nc.gpsimd.tensor_tensor(taps_l[:, j, lt, :], pm[:, lt % 2, j, :],
                                                       taps_h[:, j, lt, :].bitcast(F32), ALU.subtract)
                    last.then_inc(lo_ok, 1)
                with pool.Fori(0, 2) as h:
                    for q in range(4):
                        n = o * KT + h * 4 + q
                        s = q % 2
                        pool.wait_ge(tab_in[s], 16 * (o * 4 + h * 2 + q // 2 + 1))
                        hold(pool, K, spec_mm, 2 * n + 2)
                        nc.gpsimd.tensor_copy(tab_h[:, s, :, :, :], tab[:, s, :, :, :]).then_inc(tab_hi, 1)
                        pool.wait_ge(tab_hi, n + 1)
                        nc.gpsimd.tensor_tensor(tab_l[:, s, :, :, :], tab[:, s, :, :, :],
                                                tab_h[:, s, :, :, :].bitcast(F32), ALU.subtract).then_inc(tab_ok, 1)

        @block.tensor
        def _(pe):
            pe.sem_inc(spec_mm, 4)
            pe.sem_inc(ada_mm, 1)
            with pe.Fori(0, 2) as o:
                for lt in range(KT):
                    hold(pe, K, chain_s, o * (KT + 1) + lt + 1 + (lt > 0))
                    for j in range(2):
                        last = nc.tensor.matmul(hps[:, j, :], K["h2"][:, lt * P:(lt + 1) * P],
                                                K["f3w"][:, bass.ds(o * HW + j * 2 * HW, HW)], start=True, stop=True)
                    last.then_inc(taps_mm, 1)
                hold(pe, K, lo_ok, (o + 1) * KT + 2)
                with pe.Fori(0, 2) as h:
                    for q in range(4):
                        n = o * KT + h * 4 + q
                        pe.wait_ge(tab_ok, n + 3)
                        pe.wait_ge(cos_out, n + 1)
                        pe.wait_ge(sin_out, n + 1)
                        for j in range(2):
                            for lt in range(KT):
                                last = product3(nc, sps[:, 2 * (q % 2) + j, :],
                                                (tab_h[:, q % 2, j, lt, :], tab_l[:, q % 2, j, lt, :]),
                                                (taps_h[:, j, lt, :], taps_l[:, j, lt, :]), lt == 0, lt == KT - 1)
                            last.then_inc(spec_mm, 1)
                        if q < 3:
                            m = (o * 2 + h) * 3 + q
                            pe.wait_ge(ada_out, m + 1)
                            for c in range(2):
                                pe.wait_ge(ada_in[c], 16 * (m + 1))
                                for ct in range(2 if q < 2 else 1):
                                    for k in range(KT):
                                        flags = dict(start=k == 0, stop=k == KT - 1)
                                        if q < 2:
                                            last = nc.tensor.matmul(aps[:, q % 2, 2 * c + ct:2 * c + ct + 1],
                                                                    wada[:, c, k, ct * P:(ct + 1) * P],
                                                                    K["silu"][:, k:k + 1], **flags)
                                        else:
                                            last = nc.tensor.matmul(aps[:, q % 2, c * 256:(c + 1) * 256],
                                                                    K["silu_wide"][:, k, :], wada[:, c, k, :], **flags)
                            last.then_inc(ada_mm, 1)

        @block.scalar
        def _(act):
            act.sem_inc(cos_out, 2)
            for s in range(2):
                act.sem_inc(stored[s], 16)
            with act.Fori(0, 2) as o:
                for lt in range(KT):
                    n = o * KT + lt
                    act.wait_ge(pm_ok, 2 * n + 2)
                    if lt == 0:
                        act.wait_ge(spec_mm, 2 * KT * o + 4)
                    nc.scalar.activation(taps_h[:, :, lt, :], pm[:, lt % 2, :, :], ACT.Copy).then_inc(hi_ok, 1)
                with act.Fori(0, 2) as h:
                    for q in range(4):
                        n, s = o * KT + h * 4 + q, q % 2
                        act.wait_ge(spec_mm, 2 * n + 5)
                        act.wait_ge(stored[s], 16 * (o * 4 + h * 2 + q // 2 + 1))
                        nc.scalar.activation(spec[:, s, 0, :], sps[:, 2 * s, :], ACT.Copy, scale=1.0 / SEQ).then_inc(cos_out, 1)
                        act.wait_ge(cos_out, n + 3)
                        act.wait_ge(sin_out, n + 3)
                        act.dma_start(S["spec"][bass.ds(o, 1), bass.ds(h * 4 + q, 1)][0][0],
                                      spec[:, s, :, :]).then_inc(stored[s], 16)
            for s in range(2):
                act.wait_ge(stored[s], 16 * (KT + 1))

        @block.vector
        def _(dve):
            v = nc.vector
            ch = Chain(dve, chain_s)
            dve.sem_inc(chain_s, 1)
            ch.n = 1
            dve.sem_inc(sin_out, 2)
            dve.sem_inc(ada_out, 1)
            dve.wait_ge(decay_in, 16)
            with dve.Fori(0, 2) as o:
                ch.loop(o, KT + 1)
                for lt in range(KT):
                    n = o * KT + lt
                    dve.wait_ge(taps_mm, n + 1)
                    ch.link(v.tensor_tensor(fb[:, :, :], hps[:, :, :], decay[:, lt, :].unsqueeze(1).to_broadcast([P, 2, HW]), ALU.mult))
                    if lt == 0:
                        ch.link(v.memset(fb[0:1, 1, :], 0.0))
                    dve.wait_ge(lo_ok, n + 1)
                    v.tensor_tensor(pm[:, lt % 2, 0, :], fb[:, 0, :], fb[:, 1, :], ALU.add).then_inc(pm_ok, 1)
                    v.tensor_tensor(pm[:, lt % 2, 1, :], fb[:, 0, :], fb[:, 1, :], ALU.subtract).then_inc(pm_ok, 1)
                    hold(dve, K, pm_ok, 2 * n + 2)
                with dve.Fori(0, 2) as h:
                    for q in range(4):
                        n, s = o * KT + h * 4 + q, q % 2
                        dve.wait_ge(spec_mm, 2 * n + 6)
                        dve.wait_ge(stored[s], 16 * (o * 4 + h * 2 + q // 2 + 1))
                        v.tensor_scalar(spec[:, s, 1, :], sps[:, 2 * s + 1, :], 1.0 / SEQ, None, ALU.mult).then_inc(sin_out, 1)
                        if q < 3:
                            g = o * 2 + h
                            m = g * 3 + q
                            dve.wait_ge(ada_mm, m + 2)
                            if q < 2:
                                col = K["ada_col"][:, bass.ds(g * 8 + 4 * q, 4)]
                                v.tensor_tensor(col, aps[:, q % 2, 0:4], col, ALU.add).then_inc(ada_out, 1)
                            else:
                                row = K["ada_row"][:, bass.ds(g, 1), :][:, 0, :]
                                v.scalar_tensor_tensor(out=row, in0=aps[:, q % 2, :], scalar=1.0, in1=row,
                                                       op0=ALU.add, op1=ALU.add).then_inc(ada_out, 1)
                
            ch.done(2)




def stage_project(nc, S, K, T):
    ctx = ExitStack()
    with ctx:
        sb = lambda n, s, d=F32: ctx.enter_context(nc.sbuf_tensor("pj_" + n, s, d))
        sem = cleared_sems(nc, ctx, "pj_")
        xk = sb("xk", [P, 2, SEQ])
        u_h, u_l = sb("u_h", [P, KT, SEQ], F32R), sb("u_l", [P, KT, SEQ], F32R)
        w = sb("w", [P, 2, KT, QC])
        w_h, w_l = sb("w_h", [P, 2, KT, QC], F32R), sb("w_l", [P, 2, KT, QC], F32R)
        out_c = sb("out_c", [P, 2, SEQ])
        out_q = sb("out_q", [P, 2, KT, QC])
        cps = ctx.enter_context(nc.psum_tensor("pj_cps", [P, 4, HALF], F32))
        qps = ctx.enter_context(nc.psum_tensor("pj_qps", [P, 4, HALF], F32))
        x_in = [sem(f"x_in{k}") for k in range(2)]
        w_in = [sem(f"w_in{k}") for k in range(2)]
        stored = [sem(f"stored{k}") for k in range(2)]
        q_stored = [sem(f"q_stored{k}") for k in range(2)]
        chain_s, u_ok, u_hi, u_lo, w_hi, w_ok = sem("chain"), sem("u_ok"), sem("u_hi"), sem("u_lo"), sem("w_hi"), sem("w_ok")
        cmm, act_out, dve_out, qmm, act_q, dve_q = sem("cmm"), sem("act_out"), sem("dve_out"), sem("qmm"), sem("act_q"), sem("dve_q")
        block = ctx.enter_context(nc.Block())
        CN, QN = CM_TILES, QKV // QC

        @block.sync
        def _(sp):
            for k in range(KT):
                if k >= 2:
                    sp.wait_ge(u_lo, k - 1)
                sp.dma_start(xk[:, k % 2, :], T["xT"][:, k, :]).then_inc(x_in[k % 2], 16)
            with sp.Fori(0, CN // 2) as i:
                for s in range(2):
                    sp.wait_ge(w_ok, 2 * i + s + 1)
                    sp.dma_start(w[:, s, :, 0:P], T["w_cm"][bass.ds(2 * i + s, 1)][0]).then_inc(w_in[s], 16)
            with sp.Fori(0, QN // 2) as i:
                for s in range(2):
                    sp.wait_ge(w_ok, 2 * i + s + 1 + CN)
                    sp.dma_start(w[:, s, :, :], T["w_qkv"][bass.ds(2 * i + s, 1)][0]).then_inc(w_in[s], 16)

        @block.gpsimd
        def _(pool):
            pool.sem_inc(w_ok, 2)

            def split(s, n, count, cols, read):
                pool.wait_ge(w_in[s], 16 * (count + 1))
                hold(pool, K, *read)
                nc.gpsimd.tensor_copy(w_h[:, s, :, 0:cols], w[:, s, :, 0:cols]).then_inc(w_hi, 1)
                pool.wait_ge(w_hi, n + 1)
                nc.gpsimd.tensor_tensor(w_l[:, s, :, 0:cols], w[:, s, :, 0:cols],
                                        w_h[:, s, :, 0:cols].bitcast(F32), ALU.subtract).then_inc(w_ok, 1)

            with pool.Fori(0, CN // 2) as i:
                for s in range(2):
                    n = 2 * i + s
                    split(s, n, i, P, (cmm, 2 * n + 2))
            pool.wait_ge(cmm, 4 + 2 * CN)
            with pool.Fori(0, QN // 2) as i:
                for s in range(2):
                    n = 2 * i + s
                    split(s, n + CN, i + CN // 2, QC, (qmm, KT * n + 1))

        @block.tensor
        def _(pe):
            pe.sem_inc(cmm, 4)
            pe.sem_inc(qmm, 1 + KT)
            pe.wait_ge(u_lo, KT)
            with pe.Fori(0, CN // 2) as i:
                for s in range(2):
                    n = 2 * i + s
                    pe.wait_ge(w_ok, n + 3)
                    pe.wait_ge(act_out, n + 1)
                    pe.wait_ge(dve_out, n + 1)
                    for h in range(2):
                        cut = slice(h * HALF, (h + 1) * HALF)
                        for k in range(KT):
                            last = product3(nc, cps[:, 2 * s + h, :], (w_h[:, s, k, 0:P], w_l[:, s, k, 0:P]),
                                            (u_h[:, k, cut], u_l[:, k, cut]), k == 0, k == KT - 1)
                        last.then_inc(cmm, 1)
            with pe.Fori(0, QN // 2) as i:
                for s in range(2):
                    n = 2 * i + s
                    pe.wait_ge(w_ok, n + 3 + CN)
                    for tt in range(KT):
                        done = act_q if tt % 2 == 0 else dve_q
                        pe.wait_ge(done, 4 * n + tt // 2 + 1)
                        cut = slice(tt * P, (tt + 1) * P)
                        for k in range(KT):
                            last = product3(nc, qps[:, tt % 4, 0:QC], (u_h[:, k, cut], u_l[:, k, cut]),
                                            (w_h[:, s, k, :], w_l[:, s, k, :]), k == 0, k == KT - 1)
                        last.then_inc(qmm, 1)

        @block.scalar
        def _(act):
            act.sem_inc(act_out, 2)
            act.sem_inc(act_q, 2)
            for s in range(2):
                act.sem_inc(stored[s], 16)
                act.sem_inc(q_stored[s], 16)
            for k in range(KT):
                act.wait_ge(u_ok, k + 1)
                nc.scalar.activation(u_h[:, k, :], xk[:, k % 2, :], ACT.Copy).then_inc(u_hi, 1)
            with act.Fori(0, CN // 2) as i:
                for s in range(2):
                    n = 2 * i + s
                    act.wait_ge(cmm, 2 * n + 5)
                    act.wait_ge(stored[s], 16 * (i + 1))
                    nc.scalar.activation(out_c[:, s, 0:HALF], cps[:, 2 * s, :], ACT.Copy).then_inc(act_out, 1)
                    act.wait_ge(act_out, n + 3)
                    act.wait_ge(dve_out, n + 3)
                    act.dma_start(S["cm"][bass.ds(n, 1)][0], out_c[:, s, :]).then_inc(stored[s], 16)
            with act.Fori(0, QN // 2) as i:
                for s in range(2):
                    n = 2 * i + s
                    act.wait_ge(q_stored[s], 16 * (i + 1))
                    for tt in range(0, KT, 2):
                        act.wait_ge(qmm, KT * n + tt + 2 + KT)
                        nc.scalar.activation(out_q[:, s, tt, :], qps[:, tt % 4, 0:QC], ACT.Copy).then_inc(act_q, 1)
                    act.wait_ge(act_q, 4 * n + 6)
                    act.wait_ge(dve_q, 4 * n + 6)
                    act.dma_start(S["qkv"].rearrange("(a p) n -> p a n", p=P)[:, :, bass.ds(n * QC, QC)],
                                  out_q[:, s, :, :]).then_inc(q_stored[s], 16)
            for s in range(2):
                act.wait_ge(stored[s], 16 * (CN // 2 + 1))
                act.wait_ge(q_stored[s], 16 * (QN // 2 + 1))

        @block.vector
        def _(dve):
            v = nc.vector
            ch = Chain(dve, chain_s)
            dve.sem_inc(dve_out, 2)
            dve.sem_inc(dve_q, 2)
            for a in (KT, 3 * KT):
                ch.link(v.tensor_scalar(K["ada_col"][:, a:a + KT], K["ada_col"][:, a:a + KT], 1.0, None, ALU.add))

            def low(k):
                dve.wait_ge(u_hi, k + 1)
                v.tensor_tensor(u_l[:, k, :], xk[:, k % 2, :], u_h[:, k, :].bitcast(F32), ALU.subtract).then_inc(u_lo, 1)

            for k in range(KT):
                dve.wait_ge(x_in[k % 2], 16 * (k // 2 + 1))
                v.tensor_scalar(xk[:, k % 2, :], xk[:, k % 2, :], K["ada_col"][:, KT + k:KT + k + 1],
                                K["ada_col"][:, k:k + 1], ALU.mult, ALU.add).then_inc(u_ok, 1)
                if k >= 1:
                    low(k - 1)
            low(KT - 1)
            with dve.Fori(0, CN // 2) as i:
                for s in range(2):
                    n = 2 * i + s
                    dve.wait_ge(cmm, 2 * n + 6)
                    dve.wait_ge(stored[s], 16 * (i + 1))
                    v.tensor_copy(out_c[:, s, HALF:SEQ], cps[:, 2 * s + 1, :]).then_inc(dve_out, 1)
            with dve.Fori(0, QN // 2) as i:
                for s in range(2):
                    n = 2 * i + s
                    dve.wait_ge(q_stored[s], 16 * (i + 1))
                    for tt in range(1, KT, 2):
                        dve.wait_ge(qmm, KT * n + tt + 2 + KT)
                        v.tensor_copy(out_q[:, s, tt, :], qps[:, tt % 4, 0:QC]).then_inc(dve_q, 1)


def stage_hyena(nc, S, K, T):
    ctx = ExitStack()
    with ctx:
        sb = lambda n, s, d=F32: ctx.enter_context(nc.sbuf_tensor("hy_" + n, s, d))
        sem = lambda n: ctx.enter_context(nc.semaphore("hy_" + n))
        yh = K["yh"]
        cw, cb, bias = sb("cw", [P, HY_TILES, 3]), sb("cb", [P, HY_TILES]), sb("bias", [P, 2, 4])
        raw = sb("raw", [P, SEQ])
        xg = K["big"][:, 4:8, :]
        z_h, z_l = sb("z_h", [P, KT, HW], F32R), sb("z_l", [P, KT, HW], F32R)
        y_h, y_l = sb("y_h", [P, KT, 2, HW], F32R), sb("y_l", [P, KT, 2, HW], F32R)
        tab = sb("tab", [P, 2, 2, SEQ])
        tab_h, tab_l = sb("tab_h", [P, 2, 2, SEQ], F32R), sb("tab_l", [P, 2, 2, SEQ], F32R)
        spec = sb("spec", [P, 2, 2, HW])
        prod, ytmp = sb("prod", [P, 2, HW]), sb("ytmp", [P, 2, HW])
        ps = ctx.enter_context(nc.psum_tensor("hy_ps", [P, 8, HALF], F32))
        small_in, v_in, raw_in, raw_used = sem("small_in"), sem("v_in"), sem("raw_in"), sem("raw_used")
        tab_in = [sem(f"tab_in{k}") for k in range(2)]
        spec_in = [sem(f"spec_in{k}") for k in range(2)]
        tab_hi, tab_ok, spec_used = sem("tab_hi"), sem("tab_ok"), sem("spec_used")
        z_ok, z_hi, z_lo, tp, fwd = sem("z_ok"), sem("z_hi"), sem("z_lo"), sem("tp"), sem("fwd")
        y_ok, y_hi, y_lo, inv, slab, chain_s = sem("y_ok"), sem("y_hi"), sem("y_lo"), sem("inv"), sem("slab"), sem("chain")
        block = ctx.enter_context(nc.Block())
        STEPS = 2 * KT

        @block.sync
        def _(sp):
            sp.dma_start(cw[:, :, :], T["conv_w"]).then_inc(small_in, 16)
            sp.dma_start(cb[:, :], T["conv_b"]).then_inc(small_in, 16)
            sp.dma_start(bias[:, :, :], T["hy_bias"]).then_inc(small_in, 16)
            for c in range(4):
                sp.dma_start(xg[:, c, :], S["cm"][c]).then_inc(v_in, 16)
            with sp.Fori(0, 2) as o:
                for j in range(STEPS):
                    sp.wait_ge(tab_ok, o * STEPS + j + 1)
                    src = T["tab1"][j].rearrange("p a b c -> p a (b c)") if j < KT else T["tab1_rows"][j - KT]
                    sp.dma_start(tab[:, j % 2, :, :], src).then_inc(tab_in[j % 2], 16)
                    if j < KT:
                        sp.wait_ge(spec_used, o * KT + j + 1)
                        sp.dma_start(spec[:, j % 2, :, :], S["spec"][bass.ds(o, 1), j][0]).then_inc(spec_in[j % 2], 16)
                    if j < 4:
                        sp.wait_ge(raw_used, o * 4 + j + 1)
                        sp.dma_start(raw[:, :], S["cm"][bass.ds(o * 4 + 4 + j, 1)][0]).then_inc(raw_in, 16)

        @block.gpsimd
        def _(pool):
            pool.sem_inc(tab_ok, 2)
            pool.sem_inc(y_lo, 1)

            def split_low(o, j):
                pool.wait_ge(tab_hi, o * STEPS + j + 1)
                nc.gpsimd.tensor_tensor(tab_l[:, j % 2, :, :], tab[:, j % 2, :, :],
                                        tab_h[:, j % 2, :, :].bitcast(F32), ALU.subtract).then_inc(tab_ok, 1)

            with pool.Fori(0, 2) as o:
                split_low(o, 0)
                for j in range(STEPS):
                    if j + 1 < STEPS:
                        split_low(o, j + 1)
                    if j < KT:
                        pool.wait_ge(y_hi, o * KT + j + 1)
                        nc.gpsimd.tensor_tensor(y_l[:, j, :, :], ytmp[:, :, :], y_h[:, j, :, :].bitcast(F32),
                                                ALU.subtract).then_inc(y_lo, 1)

        @block.tensor
        def _(pe):
            pe.sem_inc(slab, 2)
            with pe.Fori(0, 2) as o:
                pe.wait_ge(z_ok, o * 4 + 4)
                for tt in range(KT):
                    if tt >= 4:
                        pe.wait_ge(z_lo, o * KT + tt - 3)
                    for c in range(4):
                        last = nc.tensor.transpose(ps[:, 4 + tt % 4, c * P:(c + 1) * P],
                                                   yh[:, c, tt * P:(tt + 1) * P], K["ident"][:, :])
                    last.then_inc(tp, 1)
                hold(pe, K, z_lo, o * KT + KT)
                for j in range(KT):
                    s = j % 2
                    pe.wait_ge(tab_ok, o * STEPS + j + 3)
                    if j >= 2:
                        pe.wait_ge(y_ok, o * KT + j - 1)
                    for a in range(2):
                        for tt in range(KT):
                            cut = slice(tt * P, (tt + 1) * P)
                            last = product3(nc, ps[:, 2 * s + a, :], (tab_h[:, s, a, cut], tab_l[:, s, a, cut]),
                                            (z_h[:, tt, :], z_l[:, tt, :]), tt == 0, tt == KT - 1)
                        last.then_inc(fwd, 1)
                pe.wait_ge(y_ok, o * KT + KT)
                for j in range(KT):
                    s = j % 2
                    pe.wait_ge(tab_ok, o * STEPS + KT + j + 3)
                    pe.wait_ge(y_lo, o * KT + j + 2)
                    for c in range(4):
                        cc = slice(c * P, (c + 1) * P)
                        for h in range(2):
                            cut = slice(h * HALF, (h + 1) * HALF)
                            for a in range(2):
                                last = product3(nc, ps[:, 2 * c + h, :], (y_h[:, j, a, cc], y_l[:, j, a, cc]),
                                                (tab_h[:, s, a, cut], tab_l[:, s, a, cut]),
                                                j == 0 and a == 0, j == KT - 1 and a == 1)
                        if j == KT - 1 and c < 3:
                            last.then_inc(inv, 1)
                    last.then_inc(inv if j == KT - 1 else slab, 1)

        @block.scalar
        def _(act):
            def split_high(o, j):
                act.wait_ge(tab_in[j % 2], 16 * (o * KT + j // 2 + 1))
                if j < 2:
                    act.wait_ge(inv, 4 * o + 1)
                elif j <= KT + 1:
                    act.wait_ge(fwd, o * STEPS + 2 * (j - 1))
                else:
                    act.wait_ge(slab, o * (KT - 1) + j - KT - 1 + 2)
                nc.scalar.activation(tab_h[:, j % 2, :, :], tab[:, j % 2, :, :], ACT.Copy).then_inc(tab_hi, 1)

            act.sem_inc(inv, 1)
            with act.Fori(0, 2) as o:
                split_high(o, 0)
                for tt in range(KT):
                    act.wait_ge(tp, o * KT + tt + 1)
                    nc.scalar.activation(z_h[:, tt, :], ps[:, 4 + tt % 4, :], ACT.Copy).then_inc(z_hi, 1)
                for j in range(STEPS):
                    if j + 1 < STEPS:
                        split_high(o, j + 1)
                    if j < KT:
                        act.wait_ge(y_ok, o * KT + j + 1)
                        nc.scalar.activation(y_h[:, j, :, :], ytmp[:, :, :], ACT.Copy).then_inc(y_hi, 1)

        @block.vector
        def _(dve):
            v = nc.vector
            ch = Chain(dve, chain_s)
            dve.sem_inc(spec_used, 2)
            dve.sem_inc(raw_used, 1)

            def short(dst, src, wcol, bcol):
                ch.link(v.tensor_scalar(dst, src, wcol(1), bcol, ALU.mult, ALU.add))
                ch.link(v.scalar_tensor_tensor(out=dst[:, 1:SEQ], in0=src[:, 0:SEQ - 1], scalar=wcol(0),
                                               in1=dst[:, 1:SEQ], op0=ALU.mult, op1=ALU.add))
                return v.scalar_tensor_tensor(out=dst[:, 0:SEQ - 1], in0=src[:, 1:SEQ], scalar=wcol(2),
                                              in1=dst[:, 0:SEQ - 1], op0=ALU.mult, op1=ALU.add)

            dve.wait_ge(small_in, 48)
            dve.wait_ge(v_in, 64)
            for c in range(4):
                short(yh[:, c, :], xg[:, c, :], lambda a: cw[:, c, a:a + 1], cb[:, c:c + 1]).then_inc(z_ok, 1)
            dve.wait_ge(z_ok, 4)
            with dve.Fori(0, 2) as o:
                ch.loop(o, 4 * 2 + KT * 5 + 4)
                for tt in range(KT):
                    dve.wait_ge(z_hi, o * KT + tt + 1)
                    v.tensor_tensor(z_l[:, tt, :], ps[:, 4 + tt % 4, :], z_h[:, tt, :].bitcast(F32),
                                    ALU.subtract).then_inc(z_lo, 1)
                for j in range(KT):
                    s = j % 2
                    if j < 4:
                        tile = o * 4 + 4 + j
                        dve.wait_ge(raw_in, 16 * (o * 4 + j + 1))
                        short(xg[:, j, :], raw[:, :], lambda a: cw[:, bass.ds(tile, 1), a:a + 1][:, 0, :],
                              cb[:, bass.ds(tile, 1)]).then_inc(raw_used, 1)
                    dve.wait_ge(fwd, o * STEPS + 2 * j + 2)
                    dve.wait_ge(spec_in[s], 16 * (o * 4 + j // 2 + 1))
                    zr, zs, kr, ks = ps[:, 2 * s, :], ps[:, 2 * s + 1, :], spec[:, s, 0, :], spec[:, s, 1, :]
                    ch.link(v.tensor_tensor(prod[:, :, :], ps[:, 2 * s:2 * s + 2, :], spec[:, s, :, :], ALU.mult))
                    dve.wait_ge(y_lo, o * KT + j + 1)
                    ch.link(v.tensor_tensor(ytmp[:, 0, :], prod[:, 0, :], prod[:, 1, :], ALU.subtract))
                    ch.link(v.tensor_tensor(prod[:, 0, :], zr, ks, ALU.mult))
                    ch.link(v.tensor_tensor(prod[:, 1, :], zs, kr, ALU.mult))
                    ch.link(v.tensor_tensor(ytmp[:, 1, :], prod[:, 0, :], prod[:, 1, :], ALU.add))
                    v.sem_inc(spec_used, 1)
                    v.sem_inc(y_ok, 1)
                for c in range(4):
                    dve.wait_ge(inv, 4 * o + c + 2)
                    z = yh[:, c, :]
                    ch.link(v.scalar_tensor_tensor(out=z, in0=z, scalar=bias[:, bass.ds(o, 1), c:c + 1][:, 0, :],
                                                   in1=ps[:, 2 * c:2 * c + 2, :].rearrange("p a b -> p (a b)"),
                                                   op0=ALU.mult, op1=ALU.add))
                    v.tensor_tensor(z, z, xg[:, c, :], ALU.mult).then_inc(z_ok, 1)
                hold(dve, K, z_ok, o * 4 + 8)
            ch.done(2)


def stage_rotary(nc, S, K, T):
    ctx = ExitStack()
    with ctx:
        sb = lambda n, s, d=F32: ctx.enter_context(nc.sbuf_tensor("ro_" + n, s, d))
        sem = lambda n: ctx.enter_context(nc.semaphore("ro_" + n))
        rows = sb("rows", [P, 2, 2 * HEADS, HD])
        tmp = sb("tmp", [P, 4, 2 * HEADS, ROPE])
        ps = ctx.enter_context(nc.psum_tensor("ro_ps", [HD, 6, HALF], F32))
        rows_in = [sem(f"rows_in{k}") for k in range(2)]
        chain_s, rot, tp, act_out, dve_out = sem("chain"), sem("rot"), sem("tp"), sem("act_out"), sem("dve_out")
        block = ctx.enter_context(nc.Block())

        @block.sync
        def _(sp):
            with sp.Fori(0, KT // 2) as i:
                for s in range(2):
                    tt = 2 * i + s
                    sp.wait_ge(tp, 6 * tt + 1)
                    sp.dma_start(rows[:, s, :, :], S["qkv"].rearrange("(a p) n -> a p n", p=P)[bass.ds(tt, 1)][0]
                                 [:, 0:2 * HEADS * HD].rearrange("p (h e) -> p h e", e=HD)).then_inc(rows_in[s], 16)

        @block.tensor
        def _(pe):
            pe.sem_inc(tp, 7)
            with pe.Fori(0, KT // 2) as i:
                for s in range(2):
                    tt = 2 * i + s
                    hold(pe, K, rot, tt + 1)
                    for b in range(6):
                        hold(pe, K, act_out if b % 2 == 0 else dve_out, 3 * tt + b // 2 + 1)
                        for h in range(4):
                            last = nc.tensor.transpose(ps[:, b, h * P:(h + 1) * P], rows[:, s, 4 * b + h, :], K["ident"][:, :])
                        last.then_inc(tp, 1)

        def evacuate(eng, copy, done, parity, s, tt):
            for b in range(parity, 6, 2):
                eng.wait_ge(tp, 6 * tt + b + 8)
                copy(K["qk"][:, 4 * b:4 * b + 4, bass.ds(tt * P, P)],
                     ps[:, b, :].rearrange("p (h t) -> p h t", t=P)).then_inc(done, 1)

        @block.scalar
        def _(act):
            act.sem_inc(act_out, 3)
            with act.Fori(0, KT // 2) as i:
                for s in range(2):
                    evacuate(act, lambda o, x: nc.scalar.activation(o, x, ACT.Copy), act_out, 0, s, 2 * i + s)

        @block.vector
        def _(dve):
            v = nc.vector
            ch = Chain(dve, chain_s)
            dve.sem_inc(dve_out, 3)
            with dve.Fori(0, KT // 2) as i:
                for s in range(2):
                    tt = 2 * i + s
                    dve.wait_ge(rows_in[s], 16 * (i + 1))
                    wide = lambda t: t[:, bass.ds(tt, 1), :].to_broadcast([P, 2 * HEADS, ROPE])
                    cos, sin = wide(K["cos"]), wide(K["sin"])
                    a, b = rows[:, s, :, 0:ROPE], rows[:, s, :, ROPE:2 * ROPE]
                    v.tensor_tensor(tmp[:, 0, :, :], a, cos, ALU.mult).then_inc(chain_s, 1)
                    v.tensor_tensor(tmp[:, 1, :, :], b, sin, ALU.mult).then_inc(chain_s, 1)
                    v.tensor_tensor(tmp[:, 2, :, :], b, cos, ALU.mult).then_inc(chain_s, 1)
                    v.tensor_tensor(tmp[:, 3, :, :], a, sin, ALU.mult).then_inc(chain_s, 1)
                    dve.wait_ge(chain_s, 6 * tt + 4)
                    v.tensor_tensor(a, tmp[:, 0, :, :], tmp[:, 1, :, :], ALU.subtract).then_inc(chain_s, 1)
                    v.tensor_tensor(b, tmp[:, 2, :, :], tmp[:, 3, :, :], ALU.add).then_inc(chain_s, 1)
                    dve.wait_ge(chain_s, 6 * tt + 6)
                    v.sem_inc(rot, 1)
                    evacuate(dve, v.tensor_copy, dve_out, 1, s, tt)


KEYS = 256 + 256 + 640


def stage_attention(nc, S, K, T):
    ctx = ExitStack()
    with ctx:
        sb = lambda n, s, d=F32: ctx.enter_context(nc.sbuf_tensor("at_" + n, s, d))
        sem = lambda n: ctx.enter_context(nc.semaphore("at_" + n))
        qk, ya = K["qk"], K["ya"]
        mask = sb("mask", [P, 2, KEYS])
        v_near = sb("v_near", [P, KT, SLOTS * HD])
        v_class = sb("v_class", [P, 4, 2, 2 * SLOTS * HD])
        qr = sb("qr", [HD, HEADS, 256])
        score, prob_t = sb("score", [P, 2, KEYS]), sb("prob_t", [P, 2, KEYS])
        prob = score
        top, den, rden = sb("top", [P, 2, 2]), sb("den", [P, 8]), sb("rden", [P, 8])
        y = sb("y", [P, 2, SLOTS * HD])
        sps = ctx.enter_context(nc.psum_tensor("at_sps", [P, 3 * HALF], F32))
        tps = ctx.enter_context(nc.psum_tensor("at_tps", [P, 3 * HALF], F32))
        yps = ctx.enter_context(nc.psum_tensor("at_yps", [P, 2, HALF], F32))
        ytps = yps[:, 1, :]
        v_in, q_ok, s_mm, s_used, s_ok = sem("v_in"), sem("q_ok"), sem("s_mm"), sem("s_used"), sem("s_ok")
        mask_in = [sem(f"mask_in{k}") for k in range(2)]
        p_ok, t_mm, t_act, t_dve, pv_mm, y_ok, yt_mm, yt_ok = (sem(n) for n in (
            "p_ok", "t_mm", "t_act", "t_dve", "pv_mm", "y_ok", "yt_mm", "yt_ok"))
        rd, rd2 = sem("top_ok"), sem("rden_ok")
        block = ctx.enter_context(nc.Block())
        U = 2 * SLOTS
        CUT = 512

        @block.sync
        def _(sp):
            vcol = 2 * HEADS * HD
            sp.dma_start(v_near[:, :, :], S["qkv"].rearrange("(a p) n -> p a n", p=P)[:, :, vcol:vcol + 256]).then_inc(v_in, 16)
            for r in range(4):
                sp.dma_start(v_class[:, r, :, :],
                             S["qkv"].rearrange("(a p r) n -> r p a n", p=P, r=4)[r][:, :, vcol + 256:]).then_inc(v_in, 16)
            with sp.Fori(0, 4) as r:
                for b in range(2):
                    sp.wait_ge(s_used, U * r + 4 * b + 4)
                    sp.dma_start(mask[:, b, :], T["mask"][bass.ds(r, 1), b][0]).then_inc(mask_in[b], 16)

        @block.tensor
        def _(pe):
            pe.sem_inc(s_mm, 1)
            pe.sem_inc(t_mm, 2)
            pe.sem_inc(pv_mm, 2)

            def scores(r, u):
                b, hs = divmod(u, SLOTS)
                hold(pe, K, s_used, U * r + u + 8)
                cls = bass.ds(r, 256, 4)
                q = lambda g: qr[:, 4 * g + hs, b * P:(b + 1) * P]
                keys = lambda g, cut: qk[:, HEADS + 4 * g + hs, cut]
                nc.tensor.matmul(sps[:, 0:256], q(2), keys(2, cls), start=True, stop=True)
                nc.tensor.matmul(sps[:, 256:512], q(1), keys(1, cls), start=True, stop=True)
                nc.tensor.matmul(sps[:, 512:1024], q(0), keys(0, slice(384 * b, 384 * b + 512)), start=True, stop=True)
                nc.tensor.matmul(sps[:, 1024:KEYS], q(0), keys(0, slice(384 * b + 512, 384 * b + 640)),
                                 start=True, stop=True).then_inc(s_mm, 1)

            def turn_y(r, b):
                hold(pe, K, y_ok, U * r + 4 * b + 6)
                for c in range(2):
                    last = nc.tensor.transpose(ytps[:, c * P:(c + 1) * P], y[:, b, c * P:(c + 1) * P], K["ident"][:, :])
                last.then_inc(yt_mm, 1)

            def yt_read(r, u):
                if u % SLOTS == 1:
                    hold(pe, K, yt_ok, 2 * r + u // SLOTS + 2)

            pe.wait_ge(v_in, 80)
            with pe.Fori(0, 4) as r:
                pe.wait_ge(q_ok, r + 1)
                scores(r, 0)
                for u in range(U):
                    b, hs = divmod(u, SLOTS)
                    n = U * r + u
                    if u + 1 < U:
                        scores(r, u + 1)
                    hold(pe, K, p_ok, n + 3)
                    hold(pe, K, t_act, n + 1)
                    hold(pe, K, t_dve, n + 1)
                    for i in range(KEYS // P):
                        last = nc.tensor.transpose(tps[:, i * P:(i + 1) * P], prob[:, u % 2, i * P:(i + 1) * P], K["ident"][:, :])
                    last.then_inc(t_mm, 1)
                    hold(pe, K, t_act, n + 2)
                    hold(pe, K, t_dve, n + 2)
                    hold(pe, K, y_ok, n + 1)
                    yt_read(r, u)
                    for i in range(KEYS // P):
                        if i < 4:
                            g = 1 - i // 2
                            val = v_class[:, bass.ds(r, 1), i % 2, (g * SLOTS + hs) * HD:(g * SLOTS + hs + 1) * HD][:, 0, :]
                        else:
                            val = v_near[:, 3 * b + i - 4, hs * HD:(hs + 1) * HD]
                        last = nc.tensor.matmul(yps[:, u % 2, 0:HD], prob_t[:, u % 2, i * P:(i + 1) * P], val,
                                                start=(i == 0), stop=(i == KEYS // P - 1))
                    last.then_inc(pv_mm, 1)
                    if u == SLOTS:
                        turn_y(r, 0)
                turn_y(r, 1)

        @block.scalar
        def _(act):
            act.sem_inc(p_ok, 2)
            act.sem_inc(t_act, 1)
            act.sem_inc(yt_ok, 2)

            def expo(r, u):
                n = U * r + u
                act.wait_ge(s_ok, n + 1)
                nc.scalar.activation(prob[:, u % 2, :], score[:, u % 2, :], ACT.Exp, bias=top[:, u % 2, 1:2],
                                     scale=HD ** -0.5, accum_out=den[:, u:u + 1]).then_inc(p_ok, 1)

            def put_y(r, b):
                act.wait_ge(yt_mm, 2 * r + b + 1)
                nc.scalar.activation(ya.rearrange("p c (b m r) -> p r b c m", b=2, r=4)[:, bass.ds(r, 1), b, :, :][:, 0],
                                     ytps[:, 0:256].rearrange("p (c m) -> p c m", c=2), ACT.Copy).then_inc(yt_ok, 1)

            with act.Fori(0, 4) as r:
                act.wait_ge(s_mm, U * r + 1)
                nc.scalar.activation(qr[:, :, :], qk[:, 0:HEADS, bass.ds(r, 256, 4)], ACT.Copy).then_inc(q_ok, 1)
                expo(r, 0)
                for u in range(U):
                    n = U * r + u
                    if u + 1 < U:
                        expo(r, u + 1)
                    act.wait_ge(t_mm, n + 3)
                    act.wait_ge(pv_mm, n + 1)
                    nc.scalar.activation(prob_t[:, u % 2, CUT:], tps[:, CUT:KEYS], ACT.Copy).then_inc(t_act, 1)
                    if u == 4:
                        put_y(r, 0)
                put_y(r, 1)

        @block.vector
        def _(dve):
            v = nc.vector
            dve.sem_inc(s_used, 8)
            dve.sem_inc(t_dve, 1)
            dve.sem_inc(y_ok, 2)

            def mask_max(r, u):
                n, b, s = U * r + u, u // SLOTS, u % 2
                dve.wait_ge(s_mm, n + 2)
                dve.wait_ge(t_mm, n + 1)
                if u % SLOTS == 0:
                    dve.wait_ge(mask_in[b], 16 * (r + 1))
                v.tensor_tensor(score[:, s, :], sps[:, 0:KEYS], mask[:, b, :], ALU.add).then_inc(s_used, 1)
                hold(dve, K, s_used, n + 9)
                v.tensor_reduce(top[:, s, 0:1], score[:, s, :], AX, ALU.max).then_inc(rd, 1)
                dve.wait_ge(rd, n + 1)
                v.tensor_scalar(top[:, s, 1:2], top[:, s, 0:1], -HD ** -0.5, None, ALU.mult).then_inc(s_ok, 1)

            def normalise(r, u):
                n, (b, hs) = U * r + u, divmod(u, SLOTS)
                hold(dve, K, pv_mm, n + 3)
                v.reciprocal(rden[:, u:u + 1], den[:, u:u + 1]).then_inc(rd2, 1)
                dve.wait_ge(rd2, n + 1)
                if hs == 0:
                    dve.wait_ge(yt_ok, 2 * r + b + 1)
                v.tensor_scalar(y[:, b, hs * HD:(hs + 1) * HD], yps[:, u % 2, 0:HD], rden[:, u:u + 1], None,
                                ALU.mult).then_inc(y_ok, 1)

            with dve.Fori(0, 4) as r:
                mask_max(r, 0)
                for u in range(U):
                    n = U * r + u
                    if u + 1 < U:
                        mask_max(r, u + 1)
                    dve.wait_ge(t_mm, n + 3)
                    dve.wait_ge(pv_mm, n + 1)
                    v.tensor_copy(prob_t[:, u % 2, 0:CUT], tps[:, 0:CUT]).then_inc(t_dve, 1)
                    if u >= 1:
                        normalise(r, u - 1)
                normalise(r, U - 1)


def stage_merge(nc, S, K, T):
    ctx = ExitStack()
    with ctx:
        sb = lambda n, s, d=F32: ctx.enter_context(nc.sbuf_tensor("me_" + n, s, d))
        sem = lambda n: ctx.enter_context(nc.semaphore("me_" + n))
        NH, NY = 4, 6
        y_h, y_l = sb("y_h", [P, NY, SEQ], F32R), sb("y_l", [P, NY, SEQ], F32R)
        w = sb("w", [P, 2, NY, P])
        w_h, w_l = sb("w_h", [P, 2, NY, P], F32R), sb("w_l", [P, 2, NY, P], F32R)
        gate = sb("gate", [P, 2, 2, SEQ])
        tmp = sb("tmp", [P, 2, SEQ])
        ps = ctx.enter_context(nc.psum_tensor("me_ps", [P, 8, HALF], F32))
        w_in = [sem(f"w_in{k}") for k in range(2)]
        g_in = [sem(f"g_in{k}") for k in range(2)]
        y_hi, y_lo, w_hi, w_ok, mm, g_ok, m_ok, chain_s = (sem(n) for n in (
            "y_hi", "y_lo", "w_hi", "w_ok", "mm", "g_ok", "m_ok", "chain"))
        block = ctx.enter_context(nc.Block())
        src = [K["yh"][:, c, :] for c in range(NH)] + [K["ya"][:, c, :] for c in range(NY - NH)]

        @block.sync
        def _(sp):
            with sp.Fori(0, KT // 2) as i:
                for s in range(2):
                    n = 2 * i + s
                    sp.wait_ge(w_ok, n + 1)
                    sp.dma_start(w[:, s, 0:NH, :], T["w_bh"][bass.ds(n, 1)][0]).then_inc(w_in[s], 16)
                    sp.dma_start(w[:, s, NH:NY, :], T["w_ba"][bass.ds(n, 1)][0]).then_inc(w_in[s], 16)
                    sp.wait_ge(m_ok, n + 1)
                    sp.dma_start(gate[:, s, 0, :], S["cm"][bass.ds(HY_TILES + n, 1)][0]).then_inc(g_in[s], 16)
                    sp.dma_start(gate[:, s, 1, :], S["cm"][bass.ds(HY_TILES + KT + n, 1)][0]).then_inc(g_in[s], 16)

        @block.gpsimd
        def _(pool):
            pool.sem_inc(w_ok, 2)
            with pool.Fori(0, KT // 2) as i:
                for s in range(2):
                    pool.wait_ge(w_hi, 2 * i + s + 1)
                    nc.gpsimd.tensor_tensor(w_l[:, s, :, :], w[:, s, :, :], w_h[:, s, :, :].bitcast(F32),
                                            ALU.subtract).then_inc(w_ok, 1)

        @block.tensor
        def _(pe):
            pe.sem_inc(mm, 4)
            pe.wait_ge(y_lo, NY)
            with pe.Fori(0, KT // 2) as i:
                for s in range(2):
                    n = 2 * i + s
                    pe.wait_ge(w_ok, n + 3)
                    pe.wait_ge(m_ok, n + 1)
                    for a, (lo, hi) in enumerate(((0, NH), (NH, NY))):
                        for h in range(2):
                            cut = slice(h * HALF, (h + 1) * HALF)
                            for c in range(lo, hi):
                                last = product3(nc, ps[:, 4 * s + 2 * a + h, :], (w_h[:, s, c, :], w_l[:, s, c, :]),
                                                (y_h[:, c, cut], y_l[:, c, cut]), c == lo, c == hi - 1)
                        last.then_inc(mm, 1)

        @block.scalar
        def _(act):
            for c in range(NY):
                nc.scalar.activation(y_h[:, c, :], src[c], ACT.Copy).then_inc(y_hi, 1)
            with act.Fori(0, KT // 2) as i:
                for s in range(2):
                    n = 2 * i + s
                    act.wait_ge(w_in[s], 32 * (i + 1))
                    act.wait_ge(mm, 2 * n + 2)
                    nc.scalar.activation(w_h[:, s, :, :], w[:, s, :, :], ACT.Copy).then_inc(w_hi, 1)
                    act.wait_ge(g_in[s], 32 * (i + 1))
                    nc.scalar.activation(gate[:, s, :, :], gate[:, s, :, :], ACT.Sigmoid).then_inc(g_ok, 1)

        @block.vector
        def _(dve):
            v = nc.vector
            ch = Chain(dve, chain_s)
            dve.sem_inc(m_ok, 2)
            for c in range(NY):
                dve.wait_ge(y_hi, c + 1)
                v.tensor_tensor(y_l[:, c, :], src[c], y_h[:, c, :].bitcast(F32), ALU.subtract).then_inc(y_lo, 1)
            with dve.Fori(0, KT // 2) as i:
                ch.loop(i, 2 * 3)
                for s in range(2):
                    n = 2 * i + s
                    dve.wait_ge(g_ok, n + 1)
                    for a in range(2):
                        dve.wait_ge(mm, 2 * n + 5 + a)
                        ch.link(v.tensor_tensor(tmp[:, a, :], ps[:, 4 * s + 2 * a:4 * s + 2 * a + 2, :].rearrange("p a b -> p (a b)"),
                                                gate[:, s, a, :], ALU.mult))
                    ch.link(v.tensor_tensor(K["merged"][:, bass.ds(n, 1), :][:, 0, :], tmp[:, 0, :], tmp[:, 1, :], ALU.add))
                    v.sem_inc(m_ok, 1)
            ch.done(KT // 2)


def layer_norm(nc, ch, K, sq, norm, row, stats, gain, base):
    v = nc.vector
    for h in range(2):
        v.bn_stats(stats[:, 6 * h:6 * h + 6], row[:, h * HALF:(h + 1) * HALF]).then_inc(ch.sem, 1)
        ch.n += 1
    hold(ch.eng, K, ch.sem, ch.base + ch.n)
    v.bn_aggr(stats[:, 12:14], stats[:, 0:12]).then_inc(ch.sem, 1)
    ch.n += 1
    ch.eng.wait_ge(ch.sem, ch.base + ch.n)
    v.tensor_scalar(stats[:, 13:14], stats[:, 13:14], EPS, None, ALU.add).then_inc(sq, 1)
    ch.eng.wait_ge(*norm)
    ch.link(v.reciprocal(stats[:, 15:16], stats[:, 14:15]))
    ch.link(v.tensor_scalar(row, row, stats[:, 12:13], stats[:, 15:16], ALU.subtract, ALU.mult))
    ch.link(v.tensor_tensor(row, row, gain, ALU.mult))
    return v.tensor_tensor(row, row, base, ALU.add)


def stage_out(nc, S, K, T):
    ctx = ExitStack()
    with ctx:
        sb = lambda n, s, d=F32: ctx.enter_context(nc.sbuf_tensor("ou_" + n, s, d))
        sem = lambda n: ctx.enter_context(nc.semaphore("ou_" + n))
        raw = sb("raw", [P, 2, D])
        w_h, w_l = sb("w_h", [P, KT, D], F32R), sb("w_l", [P, KT, D], F32R)
        m_h, m_l = sb("m_h", [P, 2, KT, P], F32R), sb("m_l", [P, 2, KT, P], F32R)
        ln = sb("ln", [P, 2, D])
        x, row = sb("x", [P, 2, D]), sb("row", [P, 2, D])
        stats = sb("stats", [P, 16])
        ps = ctx.enter_context(nc.psum_tensor("ou_ps", [P, 4, HALF], F32))
        tps = ctx.enter_context(nc.psum_tensor("ou_tps", [P, 4, HALF], F32))
        raw_in = [sem(f"raw_in{k}") for k in range(2)]
        x_in = [sem(f"x_in{k}") for k in range(2)]
        stored = [sem(f"stored{k}") for k in range(2)]
        ln_in, w_hi, w_lo, m_hi, m_lo, mm, chain_s = (sem(n) for n in ("ln_in", "w_hi", "w_lo", "m_hi", "m_lo", "mm", "chain"))
        x_used, var_ok, root_ok, row_ok, turned, u_ok = (sem(n) for n in ("x_used", "var_ok", "root_ok", "row_ok", "turned", "u_ok"))
        block = ctx.enter_context(nc.Block())

        @block.sync
        def _(sp):
            for k in range(KT):
                if k >= 2:
                    sp.wait_ge(w_lo, k - 1)
                sp.dma_start(raw[:, k % 2, :], T["w_out"][:, k, :]).then_inc(raw_in[k % 2], 16)
            sp.dma_start(ln[:, :, :], T["ln"][0:2, :].partition_broadcast(P)).then_inc(ln_in, 16)
            with sp.Fori(0, KT // 2) as i:
                for s in range(2):
                    n = 2 * i + s
                    sp.wait_ge(x_used, n + 1)
                    sp.dma_start(x[:, s, :], T["x"].rearrange("(a p) n -> a p n", p=P)[bass.ds(n, 1)][0]).then_inc(x_in[s], 16)

        @block.gpsimd
        def _(pool):
            with pool.Fori(0, KT // 2) as i:
                for s in range(2):
                    n = 2 * i + s
                    pool.wait_ge(m_hi, n + 1)
                    nc.gpsimd.tensor_tensor(m_l[:, s, :, :], K["merged"][:, :, bass.ds(n * P, P)], m_h[:, s, :, :].bitcast(F32),
                                            ALU.subtract).then_inc(m_lo, 1)

        @block.tensor
        def _(pe):
            pe.sem_inc(mm, 2)

            def turn(s, n):
                hold(pe, K, row_ok, n + 1)
                hold(pe, K, u_ok, n + 1)
                for k in range(KT):
                    last = nc.tensor.transpose(tps[:, 2 * s + k // 4, (k % 4) * P:(k % 4 + 1) * P],
                                               row[:, s, k * P:(k + 1) * P], K["ident"][:, :])
                last.then_inc(turned, 1)

            pe.sem_inc(turned, 2)
            pe.wait_ge(w_lo, KT)
            with pe.Fori(0, KT // 2) as i:
                for s in range(2):
                    n = 2 * i + s
                    pe.wait_ge(m_lo, n + 1)
                    pe.wait_ge(x_used, n + 1)
                    for h in range(2):
                        for k in range(KT):
                            last = product3(nc, ps[:, 2 * s + h, :], (m_h[:, s, k, :], m_l[:, s, k, :]),
                                            (w_h[:, k, h * HALF:(h + 1) * HALF], w_l[:, k, h * HALF:(h + 1) * HALF]),
                                            k == 0, k == KT - 1)
                    last.then_inc(mm, 1)
                    if s == 1:
                        turn(0, 2 * i)
                turn(1, 2 * i + 1)

        @block.scalar
        def _(act):
            act.sem_inc(u_ok, 2)
            for s in range(2):
                act.sem_inc(stored[s], 16)

            def root_and_u2(s, n):
                act.wait_ge(var_ok, n + 1)
                nc.scalar.activation(stats[:, 14:15], stats[:, 13:14], ACT.Sqrt).then_inc(root_ok, 1)
                act.wait_ge(row_ok, n + 1)
                act.dma_start(S["x1"].rearrange("(a p) n -> a p n", p=P)[bass.ds(n, 1)][0], row[:, s, :]).then_inc(stored[s], 16)
                hold(act, K, turned, n + 3)
                for k in range(KT):
                    last = nc.scalar.activation(K["u2"][:, k, bass.ds(n * P, P)],
                                                tps[:, 2 * s + k // 4, (k % 4) * P:(k % 4 + 1) * P], ACT.Identity,
                                                bias=K["ada_col"][:, 2 * KT + k:2 * KT + k + 1],
                                                scale=K["ada_col"][:, 3 * KT + k:3 * KT + k + 1])
                last.then_inc(u_ok, 1)

            for k in range(KT):
                act.wait_ge(raw_in[k % 2], 16 * (k // 2 + 1))
                nc.scalar.activation(w_h[:, k, :], raw[:, k % 2, :], ACT.Copy).then_inc(w_hi, 1)
            with act.Fori(0, KT // 2) as i:
                for s in range(2):
                    n = 2 * i + s
                    act.wait_ge(mm, n + 1)
                    nc.scalar.activation(m_h[:, s, :, :], K["merged"][:, :, bass.ds(n * P, P)], ACT.Copy).then_inc(m_hi, 1)
                for s in range(2):
                    root_and_u2(s, 2 * i + s)
            for s in range(2):
                act.wait_ge(stored[s], 16 * (KT // 2 + 1))

        @block.vector
        def _(dve):
            v = nc.vector
            ch = Chain(dve, chain_s)
            dve.sem_inc(x_used, 2)
            for k in range(KT):
                dve.wait_ge(w_hi, k + 1)
                v.tensor_tensor(w_l[:, k, :], raw[:, k % 2, :], w_h[:, k, :].bitcast(F32), ALU.subtract).then_inc(w_lo, 1)
            dve.wait_ge(ln_in, 16)
            with dve.Fori(0, KT // 2) as i:
                ch.loop(i, 2 * 8)
                for s in range(2):
                    n = 2 * i + s
                    r = row[:, s, :]
                    dve.wait_ge(mm, n + 3)
                    dve.wait_ge(turned, n + 1)
                    dve.wait_ge(stored[s], 16 * (i + 1))
                    ch.link(v.tensor_tensor(r, ps[:, 2 * s:2 * s + 2, :].rearrange("p a b -> p (a b)"),
                                            K["ada_row"][:, 0:2, :].rearrange("p a b -> p (a b)"), ALU.mult))
                    dve.wait_ge(x_in[s], 16 * (i + 1))
                    ch.link(v.scalar_tensor_tensor(out=r, in0=x[:, s, :], scalar=ALPHA, in1=r, op0=ALU.mult, op1=ALU.add))
                    v.sem_inc(x_used, 1)
                    layer_norm(nc, ch, K, var_ok, (root_ok, n + 1), r, stats, ln[:, 0, :], ln[:, 1, :]).then_inc(row_ok, 1)
            ch.done(KT // 2)


def stage_query(nc, S, K, T):
    ctx = ExitStack()
    with ctx:
        sb = lambda n, s, d=F32: ctx.enter_context(nc.sbuf_tensor("qu_" + n, s, d))
        sem = lambda n: ctx.enter_context(nc.semaphore("qu_" + n))
        HP = 2 * PH
        u_h, u_l = sb("u_h", [P, KT, SEQ], F32R), sb("u_l", [P, KT, SEQ], F32R)
        w = sb("w", [P, 2, KT, P])
        w_h, w_l = sb("w_h", [P, 2, KT, P], F32R), sb("w_l", [P, 2, KT, P], F32R)
        keys = sb("keys", [P, HP, NK])
        q = sb("q", [P, 2, SEQ])
        sc = sb("sc", [P, 2, KT, NK])
        qps = ctx.enter_context(nc.psum_tensor("qu_qps", [P, 4, HALF], F32))
        sps = ctx.enter_context(nc.psum_tensor("qu_sps", [P, 4, HALF], F32))
        w_in = [sem(f"w_in{k}") for k in range(2)]
        stored = [sem(f"stored{k}") for k in range(2)]
        keys_in, u_hi, u_lo, w_hi, w_ok, mm, q_act, q_dve, s_mm, s_act, s_dve = (sem(n) for n in (
            "keys_in", "u_hi", "u_lo", "w_hi", "w_ok", "mm", "q_act", "q_dve", "s_mm", "s_act", "s_dve"))
        block = ctx.enter_context(nc.Block())

        @block.sync
        def _(sp):
            sp.dma_start(keys[:, :, :], T["keysT"].rearrange("h e k -> e h k")).then_inc(keys_in, 16)
            with sp.Fori(0, HP // 2) as i:
                for s in range(2):
                    sp.wait_ge(w_ok, 2 * i + s + 1)
                    sp.dma_start(w[:, s, :, :], T["wq"][bass.ds(2 * i + s, 1)][0]).then_inc(w_in[s], 16)

        @block.gpsimd
        def _(pool):
            pool.sem_inc(w_ok, 2)
            with pool.Fori(0, HP // 2) as i:
                for s in range(2):
                    pool.wait_ge(w_hi, 2 * i + s + 1)
                    nc.gpsimd.tensor_tensor(w_l[:, s, :, :], w[:, s, :, :], w_h[:, s, :, :].bitcast(F32),
                                            ALU.subtract).then_inc(w_ok, 1)

        @block.tensor
        def _(pe):
            pe.sem_inc(mm, 4)
            pe.sem_inc(s_mm, 2)

            def project(s, n):
                hold(pe, K, w_ok, n + 3)
                hold(pe, K, q_act, n + 1)
                hold(pe, K, q_dve, n + 1)
                for h in range(2):
                    cut = slice(h * HALF, (h + 1) * HALF)
                    for k in range(KT):
                        last = product3(nc, qps[:, 2 * s + h, :], (w_h[:, s, k, :], w_l[:, s, k, :]),
                                        (u_h[:, k, cut], u_l[:, k, cut]), k == 0, k == KT - 1)
                    last.then_inc(mm, 1)

            def match(s, n):
                hold(pe, K, q_act, n + 3)
                hold(pe, K, q_dve, n + 3)
                hold(pe, K, s_act, n + 1)
                hold(pe, K, s_dve, n + 1)
                for tt in range(KT):
                    last = nc.tensor.matmul(sps[:, 2 * s + tt // 4, (tt % 4) * P:(tt % 4 + 1) * P],
                                            q[:, s, tt * P:(tt + 1) * P], keys[:, bass.ds(n, 1), :][:, 0, :],
                                            start=True, stop=True)
                last.then_inc(s_mm, 1)

            pe.wait_ge(keys_in, 16)
            pe.wait_ge(u_lo, KT)
            with pe.Fori(0, HP // 2) as i:
                project(0, 2 * i)
                project(1, 2 * i + 1)
                match(0, 2 * i)
                match(1, 2 * i + 1)

        @block.scalar
        def _(act):
            act.sem_inc(q_act, 2)
            act.sem_inc(s_act, 2)
            for s in range(2):
                act.sem_inc(stored[s], 16)
            for k in range(KT):
                nc.scalar.activation(u_h[:, k, :], K["u2"][:, k, :], ACT.Copy).then_inc(u_hi, 1)

            def high(s, n, i):
                act.wait_ge(w_in[s], 16 * (i + 1))
                act.wait_ge(mm, 2 * n + 2)
                nc.scalar.activation(w_h[:, s, :, :], w[:, s, :, :], ACT.Copy).then_inc(w_hi, 1)

            with act.Fori(0, HP // 2) as i:
                for s in range(2):
                    high(s, 2 * i + s, i)
                for s in range(2):
                    n = 2 * i + s
                    act.wait_ge(mm, 2 * n + 5)
                    act.wait_ge(s_mm, n + 1)
                    nc.scalar.activation(q[:, s, 0:HALF], qps[:, 2 * s, :], ACT.Copy).then_inc(q_act, 1)
                for s in range(2):
                    n = 2 * i + s
                    hold(act, K, s_mm, n + 3)
                    act.wait_ge(stored[s], 16 * (i + 1))
                    nc.scalar.activation(sc[:, s, 0:4, :], sps[:, 2 * s, :].rearrange("p (a k) -> p a k", k=NK),
                                         ACT.Copy).then_inc(s_act, 1)
                    act.wait_ge(s_act, n + 3)
                    act.wait_ge(s_dve, n + 3)
                    act.dma_start(S["scores"].rearrange("a p h k -> p a h k")[:, :, bass.ds(n, 1), :][:, :, 0, :],
                                  sc[:, s, :, :]).then_inc(stored[s], 16)
            for s in range(2):
                act.wait_ge(stored[s], 16 * (HP // 2 + 1))

        @block.vector
        def _(dve):
            v = nc.vector
            dve.sem_inc(q_dve, 2)
            dve.sem_inc(s_dve, 2)
            for k in range(KT):
                dve.wait_ge(u_hi, k + 1)
                v.tensor_tensor(u_l[:, k, :], K["u2"][:, k, :], u_h[:, k, :].bitcast(F32), ALU.subtract).then_inc(u_lo, 1)
            with dve.Fori(0, HP // 2) as i:
                for s in range(2):
                    n = 2 * i + s
                    dve.wait_ge(mm, 2 * n + 6)
                    dve.wait_ge(s_mm, n + 1)
                    v.tensor_copy(q[:, s, HALF:SEQ], qps[:, 2 * s + 1, :]).then_inc(q_dve, 1)
                for s in range(2):
                    n = 2 * i + s
                    hold(dve, K, s_mm, n + 3)
                    dve.wait_ge(stored[s], 16 * (i + 1))
                    v.tensor_copy(sc[:, s, 4:8, :], sps[:, 2 * s + 1, :].rearrange("p (a k) -> p a k", k=NK)).then_inc(s_dve, 1)


PICKS = PH * TOPK


def stage_select(nc, S, K, T):
    ctx = ExitStack()
    with ctx:
        sb = lambda n, s, d=F32: ctx.enter_context(nc.sbuf_tensor("se_" + n, s, d))
        sem = lambda n: ctx.enter_context(nc.semaphore("se_" + n))
        HP = 2 * PH
        sc, sc2 = sb("sc", [P, 2, HP, NK]), sb("sc2", [P, HP, NK])
        kv, ki, kf = sb("kv", [P, HP, TOPK]), sb("ki", [P, HP, TOPK], U32), sb("kf", [P, HP, TOPK])
        cand, cand2 = sb("cand", [P, PH, TOPK, TOPK]), sb("cand2", [P, PH, TOPK, TOPK])
        cv, ci = sb("cv", [P, PH, TOPK]), sb("ci", [P, PH, TOPK], U32)
        ab_i, ab = sb("ab_i", [P, 2, PICKS], U32), sb("ab", [P, 2, PICKS])
        iota = sb("iota", [P, TOPK])
        hit = sb("hit", [P, 2, PICKS, TOPK])
        e, tot = sb("e", [P, PH, TOPK]), sb("tot", [P, 2, PH])
        sel = sb("sel", [P, 2, 3, PICKS])
        tps = ctx.enter_context(nc.psum_tensor("se_tps", [P, 3 * P], F32))
        sc_in = [sem(f"sc_in{k}") for k in range(2)]
        small, chain_s, e_in, e_ok, sel_ok, t_mm, t_ok = (sem(n) for n in (
            "small", "chain", "e_in", "e_ok", "sel_ok", "t_mm", "t_ok"))
        block = ctx.enter_context(nc.Block())
        sc_used = sem("sc_used")

        @block.sync
        def _(sp):
            sp.dma_start(iota[:, :], T["iota"][0:TOPK].partition_broadcast(P)).then_inc(small, 16)
            with sp.Fori(0, KT // 2) as i:
                for s in range(2):
                    sp.wait_ge(sc_used, 2 * i + s + 1)
                    sp.dma_start(sc[:, s, :, :], S["scores"][bass.ds(2 * i + s, 1)][0]).then_inc(sc_in[s], 16)

        @block.tensor
        def _(pe):
            with pe.Fori(0, KT // 2) as i:
                for s in range(2):
                    n = 2 * i + s
                    hold(pe, K, sel_ok, n + 1)
                    hold(pe, K, t_ok, n + 2)
                    for a in range(3):
                        last = nc.tensor.transpose(tps[:, a * P:(a + 1) * P], sel[:, s, a, :], K["ident"][:, :])
                    last.then_inc(t_mm, 1)

        @block.scalar
        def _(act):
            act.sem_inc(t_ok, 2)
            with act.Fori(0, KT // 2) as i:
                for s in range(2):
                    n = 2 * i + s
                    act.wait_ge(e_in, n + 1)
                    nc.scalar.activation(e[:, :, :], e[:, :, :], ACT.Exp).then_inc(e_ok, 1)
                    hold(act, K, t_mm, n + 1)
                    nc.scalar.activation(K["sel"][:, :, bass.ds(n * P, P)],
                                         tps[:, :].rearrange("p (a t) -> p a t", t=P), ACT.Copy).then_inc(t_ok, 1)

        @block.vector
        def _(dve):
            v = nc.vector
            ch = Chain(dve, chain_s)
            dve.sem_inc(sc_used, 2)

            def top16(src, spare, vals, idx, rows):
                for r in range(rows):
                    last = v.max(vals(r, 0), src(r))
                ch.link(last, K)
                for r in range(rows):
                    v.max_index(idx(r, 0), vals(r, 0), src(r))
                    last = v.match_replace(spare(r), vals(r, 0), src(r), -3.0e38)
                ch.link(last, K)
                for r in range(rows):
                    last = v.max(vals(r, 1), spare(r))
                ch.link(last, K)
                for r in range(rows):
                    last = v.max_index(idx(r, 1), vals(r, 1), spare(r))
                ch.link(last, K)

            dve.wait_ge(small, 16)
            with dve.Fori(0, KT // 2) as i:
                ch.loop(i, 2 * 21)
                for s in range(2):
                    n = 2 * i + s
                    hold(dve, K, sc_in[s], 16 * (i + 1))
                    part = lambda t, r, a: t[:, r, 8 * a:8 * a + 8]
                    top16(lambda r: sc[:, s, r, :], lambda r: sc2[:, r, :], lambda r, a: part(kv, r, a),
                          lambda r, a: part(ki, r, a), HP)
                    v.sem_inc(sc_used, 1)
                    ch.link(v.tensor_copy(kf[:, :, :], ki[:, :, :]))
                    halves = lambda t: (t[:, :, :].rearrange("p (h two) k -> p h two k", two=2)[:, :, 0, :],
                                        t[:, :, :].rearrange("p (h two) k -> p h two k", two=2)[:, :, 1, :])
                    v0, v1 = halves(kv)
                    wide = [P, PH, TOPK, TOPK]
                    ch.link(v.tensor_tensor(cand[:, :, :, :], v0.unsqueeze(3).to_broadcast(wide),
                                            v1.unsqueeze(2).to_broadcast(wide), ALU.add), K)
                    flat = lambda t, r: t[:, r, :, :].rearrange("p a b -> p (a b)")
                    top16(lambda r: flat(cand, r), lambda r: flat(cand2, r), lambda r, a: part(cv, r, a),
                          lambda r, a: part(ci, r, a), PH)
                    first = cv[:, :, 0:1].to_broadcast([P, PH, TOPK])
                    v.tensor_tensor(e[:, :, :], cv[:, :, :], first, ALU.subtract).then_inc(e_in, 1)
                    cif = ci[:, :, :].rearrange("p h k -> p (h k)")
                    v.tensor_scalar(ab_i[:, 0, :], cif, 4, None, ALU.logical_shift_right)
                    ch.link(v.tensor_scalar(ab_i[:, 1, :], cif, 15, None, ALU.bitwise_and))
                    ch.link(v.tensor_copy(ab[:, :, :], ab_i[:, :, :]))
                    for a in range(2):
                        ch.link(v.tensor_tensor(hit[:, a, :, :], ab[:, a, :].unsqueeze(2).to_broadcast([P, PICKS, TOPK]),
                                                iota[:, :].unsqueeze(1).to_broadcast([P, PICKS, TOPK]), ALU.is_equal))
                    for a in range(2):
                        h4 = hit[:, a, :, :].rearrange("p (h k) j -> p h k j", h=PH)
                        ch.link(v.tensor_tensor(h4, h4, halves(kf)[a].unsqueeze(2).to_broadcast(wide), ALU.mult))
                    dve.wait_ge(t_ok, n + 1)
                    for a in range(2):
                        ch.link(v.tensor_reduce(sel[:, s, a, :], hit[:, a, :, :], AX, ALU.add))
                    dve.wait_ge(e_ok, n + 1)
                    ch.link(v.tensor_reduce(tot[:, 0, :], e[:, :, :], AX, ALU.add))
                    ch.link(v.reciprocal(tot[:, 1, :], tot[:, 0, :]))
                    ch.link(v.tensor_tensor(sel[:, s, 2, :].rearrange("p (h k) -> p h k", h=PH), e[:, :, :],
                                            tot[:, 1, :].unsqueeze(2).to_broadcast([P, PH, TOPK]), ALU.mult))
                    v.sem_inc(sel_ok, 1)
            ch.done(KT // 2)


GATE_SCALE = 2.0 ** 15


def stage_gates(nc, S, K, T):
    ctx = ExitStack()
    with ctx:
        sb = lambda n, s, d=F32: ctx.enter_context(nc.sbuf_tensor("ga_" + n, s, d))
        sem = lambda n: ctx.enter_context(nc.semaphore("ga_" + n))
        G = 4
        iota32 = sb("iota32", [P, NK])
        iota = sb("iota", [P, NK], F16)
        gh16 = sb("gh16", [P, SEQ], F16)
        gs = sb("gs", [P, 2, SEQ])
        first = sb("first", [P, 2, 2, G, NK], F16)
        second = sb("second", [P, 2, G, NK], F16)
        wide = sb("wide", [P, 2, NK, P])
        ps = ctx.enter_context(nc.psum_tensor("ga_ps", [P, 4, HALF], F32))
        small, chain_s, f_ok, mm, act_out = (sem(n) for n in ("small", "chain", "f_ok", "mm", "act_out"))
        stored = [sem(f"stored{k}") for k in range(2)]
        block = ctx.enter_context(nc.Block())
        GROUPS = P // G

        @block.sync
        def _(sp):
            sp.dma_start(iota32[:, :], T["iota"][0:NK].partition_broadcast(P)).then_inc(small, 16)
            for s in range(2):
                sp.sem_inc(stored[s], 16)
            with sp.Fori(0, KT // 2) as i:
                for s in range(2):
                    n = 2 * i + s
                    sp.wait_ge(act_out, (n + 1) * GROUPS + 4)
                    sp.dma_start(S["gates"].rearrange("i j t -> j i t")[:, :, bass.ds(n * P, P)],
                                 wide[:, s, :, :]).then_inc(stored[s], 16)
            for s in range(2):
                sp.wait_ge(stored[s], 16 * (KT // 2 + 1))

        @block.tensor
        def _(pe):
            pe.sem_inc(mm, 2)
            with pe.Fori(0, KT * GROUPS // 4) as g:
                for b in range(4):
                    m = 4 * g + b
                    pe.wait_ge(f_ok, m + 1)
                    pe.wait_ge(act_out, m + 1)
                    for t in range(G):
                        for part in range(2):
                            last = nc.tensor.matmul(ps[:, b, t * NK:(t + 1) * NK], second[:, b % 2, t, :],
                                                    first[:, b % 2, part, t, :], start=part == 0, stop=part == 1)
                    last.then_inc(mm, 1)

        @block.scalar
        def _(act):
            act.sem_inc(act_out, 4)
            with act.Fori(0, KT // 2) as i:
                for s in range(2):
                    hold(act, K, stored[s], 16 * (i + 1))
                    with act.Fori(0, GROUPS // 4) as g:
                        for b in range(4):
                            hold(act, K, mm, (2 * i + s) * GROUPS + 4 * g + b + 3)
                            nc.scalar.activation(wide[:, s, :, bass.ds((4 * g + b) * G, G)],
                                                 ps[:, b, :].rearrange("p (t i) -> p i t", i=NK), ACT.Copy,
                                                 scale=1.0 / GATE_SCALE).then_inc(act_out, 1)

        @block.vector
        def _(dve):
            v = nc.vector
            ch = Chain(dve, chain_s)
            dve.wait_ge(small, 16)
            w = K["sel"][:, 2, :]
            ch.link(v.tensor_copy(iota[:, :], iota32[:, :]))
            ch.link(v.tensor_scalar(gs[:, 1, :], w, GATE_SCALE, None, ALU.mult))
            ch.link(v.tensor_copy(gh16[:, :], gs[:, 1, :]))
            ch.link(v.tensor_copy(gs[:, 0, :], gh16[:, :]))
            ch.link(v.tensor_tensor(gs[:, 1, :], gs[:, 1, :], gs[:, 0, :], ALU.subtract))
            with dve.Fori(0, KT * GROUPS // 4) as g:
                for b in range(4):
                    m = 4 * g + b
                    dve.wait_ge(mm, m + 1)
                    for t in range(G):
                        at = bass.ds(m * G + t, 1)
                        v.tensor_scalar(second[:, b % 2, t, :], iota[:, :], K["sel"][:, 1, at], None, ALU.is_equal)
                        for part in range(2):
                            last = v.tensor_scalar(first[:, b % 2, part, t, :], iota[:, :], K["sel"][:, 0, at],
                                                   gs[:, part, at], ALU.is_equal, ALU.mult)
                    last.then_inc(f_ok, 1)


def stage_experts(nc, S, K, T):
    ctx = ExitStack()
    with ctx:
        sb = lambda n, s, d=F32: ctx.enter_context(nc.sbuf_tensor("ex_" + n, s, d))
        sem = lambda n: ctx.enter_context(nc.semaphore("ex_" + n))
        sums = K["sums"]
        u_h, u_l = sb("u_h", [P, KT, SEQ], F32R), sb("u_l", [P, KT, SEQ], F32R)
        ut = sb("ut", [P, 2, KT, P])
        ut_h, ut_l = sb("ut_h", [P, 2, KT, P], F32R), sb("ut_l", [P, 2, KT, P], F32R)
        vt = sb("vt", [P, 2, D])
        vt_h, vt_l = sb("vt_h", [P, 2, D], F32R), sb("vt_l", [P, 2, D], F32R)
        wt = sb("wt", [P, 2, SEQ])
        act_a = sb("act_a", [P, 2, SEQ])
        c_h, c_l = sb("c_h", [P, 2, SEQ], F32R), sb("c_l", [P, 2, SEQ], F32R)
        aps = ctx.enter_context(nc.psum_tensor("ex_aps", [P, 4, HALF], F32))
        fps = ctx.enter_context(nc.psum_tensor("ex_fps", [P, 4, HALF], F32))
        pair = lambda n: [sem(f"{n}{k}") for k in range(2)]
        ut_in, vt_in, wt_in = pair("ut_in"), pair("vt_in"), pair("wt_in")
        u_hi, u_lo, ut_hi, ut_ok, vt_hi, vt_ok = (sem(n) for n in ("u_hi", "u_lo", "ut_hi", "ut_ok", "vt_hi", "vt_ok"))
        a_mm, gelu_ok, c_ok, c_hi, c_lo, f_mm, f_ok = (sem(n) for n in ("a_mm", "gelu_ok", "c_ok", "c_hi", "c_lo", "f_mm", "f_ok"))
        zeroed = sem("zeroed")
        LAST = NK - 2
        HT = KT // 2
        half = lambda h: slice(h * HALF, (h + 1) * HALF)
        block = ctx.enter_context(nc.Block())

        @block.sync
        def _(sp):
            with sp.Fori(0, NK // 2) as i:
                for s in range(2):
                    n = 2 * i + s
                    sp.wait_ge(ut_ok, n + 1)
                    sp.dma_start(ut[:, s, :, :], T["utab"][bass.ds(n, 1)][0]).then_inc(ut_in[s], 16)
                    sp.wait_ge(c_lo, 2 * n + 2)
                    sp.dma_start(wt[:, s, :], S["gates"][bass.ds(n, 1)][0]).then_inc(wt_in[s], 16)
                    sp.wait_ge(vt_ok, n + 1)
                    sp.dma_start(vt[:, s, :], T["vtab"][bass.ds(n, 1)][0]).then_inc(vt_in[s], 16)

        @block.gpsimd
        def _(pool):
            pool.sem_inc(ut_ok, 2)
            pool.sem_inc(vt_ok, 2)
            with pool.Fori(0, NK // 2) as i:
                for s in range(2):
                    n = 2 * i + s
                    pool.wait_ge(ut_hi, n + 1)
                    nc.gpsimd.tensor_tensor(ut_l[:, s, :, :], ut[:, s, :, :], ut_h[:, s, :, :].bitcast(F32),
                                            ALU.subtract).then_inc(ut_ok, 1)
                    pool.wait_ge(vt_hi, n + 1)
                    nc.gpsimd.tensor_tensor(vt_l[:, s, :], vt[:, s, :], vt_h[:, s, :].bitcast(F32),
                                            ALU.subtract).then_inc(vt_ok, 1)

        @block.tensor
        def _(pe):
            pe.sem_inc(a_mm, 4)
            pe.sem_inc(f_mm, 2 * KT)

            def activations(s, n, h):
                pe.wait_ge(ut_ok, n + 3)
                pe.wait_ge(gelu_ok, 2 * n + h + 1)
                for k in range(KT):
                    last = product3(nc, aps[:, 2 * s + h, :], (ut_h[:, s, k, :], ut_l[:, s, k, :]),
                                    (u_h[:, k, half(h)], u_l[:, k, half(h)]), k == 0, k == KT - 1)
                last.then_inc(a_mm, 1)

            def sums_of(s, n, h):
                pe.wait_ge(vt_ok, n + 3)
                pe.wait_ge(c_lo, 2 * n + h + 5)
                for tt in range(h * HT, (h + 1) * HT):
                    b = tt % 2
                    pe.wait_ge(f_ok, KT * n + tt + 1)
                    cut = slice(tt * P, (tt + 1) * P)
                    for dd in range(2):
                        last = product3(nc, fps[:, 2 * b + dd, :], (c_h[:, s, cut], c_l[:, s, cut]),
                                        (vt_h[:, s, half(dd)], vt_l[:, s, half(dd)]), True, True)
                    last.then_inc(f_mm, 1)

            pe.wait_ge(u_lo, KT)
            for h in range(2):
                activations(0, 0, h)
            with pe.Fori(0, LAST // 2) as i:
                for s in range(2):
                    n = 2 * i + s
                    for h in range(2):
                        activations(1 - s, n + 1, h)
                        sums_of(s, n, h)
            for h in range(2):
                activations(1, NK - 1, h)
                sums_of(0, NK - 2, h)
            for h in range(2):
                sums_of(1, NK - 1, h)

        @block.scalar
        def _(act):
            act.sem_inc(gelu_ok, 4)
            for k in range(KT):
                nc.scalar.activation(u_h[:, k, :], K["u2"][:, k, :], ACT.Copy).then_inc(u_hi, 1)

            def split_tables(s, n, i):
                act.wait_ge(ut_in[s], 16 * (i + 1))
                act.wait_ge(a_mm, 2 * n + 2)
                nc.scalar.activation(ut_h[:, s, :, :], ut[:, s, :, :], ACT.Copy).then_inc(ut_hi, 1)

            def split_values(s, n, i):
                act.wait_ge(vt_in[s], 16 * (i + 1))
                act.wait_ge(f_mm, KT * n + KT)
                nc.scalar.activation(vt_h[:, s, :], vt[:, s, :], ACT.Copy).then_inc(vt_hi, 1)

            def gelu(s, n, h):
                act.wait_ge(a_mm, 2 * n + h + 5)
                act.wait_ge(c_lo, 2 * n + h + 1)
                nc.scalar.activation(act_a[:, s, half(h)], aps[:, 2 * s + h, :], ACT.Gelu).then_inc(gelu_ok, 1)

            def coef_high(s, n, h):
                act.wait_ge(c_ok, 2 * n + h + 1)
                act.wait_ge(f_mm, KT * n + HT * (h + 1))
                nc.scalar.activation(c_h[:, s, half(h)], act_a[:, s, half(h)], ACT.Copy).then_inc(c_hi, 1)

            split_tables(0, 0, 0)
            split_tables(1, 1, 0)
            split_values(0, 0, 0)
            for h in range(2):
                gelu(0, 0, h)
                coef_high(0, 0, h)
            with act.Fori(0, LAST // 2) as i:
                for s in range(2):
                    n = 2 * i + s
                    o = 1 - s
                    split_tables(s, n + 2, i + 1)
                    gelu(o, n + 1, 0)
                    coef_high(o, n + 1, 0)
                    split_values(o, n + 1, i + s)
                    gelu(o, n + 1, 1)
                    coef_high(o, n + 1, 1)
            gelu(1, NK - 1, 0)
            coef_high(1, NK - 1, 0)
            split_values(1, NK - 1, NK // 2 - 1)
            gelu(1, NK - 1, 1)
            coef_high(1, NK - 1, 1)

        @block.vector
        def _(dve):
            v = nc.vector
            dve.sem_inc(c_lo, 4)
            dve.sem_inc(f_ok, 2)
            for k in range(KT):
                dve.wait_ge(u_hi, k + 1)
                v.tensor_tensor(u_l[:, k, :], K["u2"][:, k, :], u_h[:, k, :].bitcast(F32), ALU.subtract).then_inc(u_lo, 1)
            dve.wait_ge(u_lo, KT)
            v.memset(sums[:, :, :], 0.0).then_inc(zeroed, 1)
            dve.wait_ge(zeroed, 1)

            def coefficients(s, n, i, h):
                dve.wait_ge(gelu_ok, 2 * n + h + 5)
                dve.wait_ge(wt_in[s], 16 * (i + 1))
                a = act_a[:, s, half(h)]
                v.tensor_tensor(a, a, wt[:, s, half(h)], ALU.mult).then_inc(c_ok, 1)

            def coef_low(s, n, h):
                dve.wait_ge(c_hi, 2 * n + h + 1)
                v.tensor_tensor(c_l[:, s, half(h)], act_a[:, s, half(h)], c_h[:, s, half(h)].bitcast(F32),
                                ALU.subtract).then_inc(c_lo, 1)

            def add_sums(n, tt):
                b = tt % 2
                hold(dve, K, f_mm, KT * n + tt + 1 + 2 * KT)
                row = sums[:, tt, :]
                v.tensor_tensor(row, row, fps[:, 2 * b:2 * b + 2, :].rearrange("p a b -> p (a b)"), ALU.add).then_inc(f_ok, 1)

            def turn(s, n, i):
                for h in range(2):
                    add_sums(n, HT * h)
                    coefficients(1 - s, n + 1, i + s, h)
                    add_sums(n, HT * h + 1)
                    coef_low(1 - s, n + 1, h)
                    add_sums(n, HT * h + 2)
                    add_sums(n, HT * h + 3)

            for h in range(2):
                coefficients(0, 0, 0, h)
                coef_low(0, 0, h)
            with dve.Fori(0, LAST // 2) as i:
                for s in range(2):
                    turn(s, 2 * i + s, i)
            turn(0, NK - 2, NK // 2 - 1)
            for tt in range(KT):
                add_sums(NK - 1, tt)


def stage_final(nc, S, K, T, out):
    ctx = ExitStack()
    with ctx:
        sb = lambda n, s, d=F32: ctx.enter_context(nc.sbuf_tensor("fi_" + n, s, d))
        sem = lambda n: ctx.enter_context(nc.semaphore("fi_" + n))
        x1, ln = sb("x1", [P, KT, D]), sb("ln", [P, 2, D])
        stats = sb("stats", [P, KT, 16])
        ln_in, var_ok, root_ok, row_ok, stored, chain_s = (sem(n) for n in (
            "ln_in", "var_ok", "root_ok", "row_ok", "stored", "chain"))
        xin = [sem(f"x_in{k}") for k in range(KT)]
        block = ctx.enter_context(nc.Block())
        rows = lambda t, n: t.rearrange("(a p) n -> a p n", p=P)[n]

        @block.sync
        def _(sp):
            for n in range(KT):
                sp.dma_start(x1[:, n, :], rows(S["x1"], n)).then_inc(xin[n], 16)
            sp.dma_start(ln[:, :, :], T["ln"][2:4, :].partition_broadcast(P)).then_inc(ln_in, 16)
            for n in range(KT):
                sp.wait_ge(row_ok, n + 1)
                sp.dma_start(rows(out[0], n), K["sums"][:, n, :]).then_inc(stored, 16)
            sp.wait_ge(stored, 16 * KT)

        @block.scalar
        def _(act):
            for n in range(KT):
                act.wait_ge(var_ok, n + 1)
                nc.scalar.activation(stats[:, n, 14:15], stats[:, n, 13:14], ACT.Sqrt).then_inc(root_ok, 1)

        @block.vector
        def _(dve):
            v = nc.vector
            ch = Chain(dve, chain_s)
            dve.wait_ge(ln_in, 16)
            for n in range(KT):
                r = K["sums"][:, n, :]
                ch.link(v.tensor_tensor(r, r, K["ada_row"][:, 2:4, :].rearrange("p a b -> p (a b)"), ALU.mult))
                dve.wait_ge(xin[n], 16)
                ch.link(v.scalar_tensor_tensor(out=r, in0=x1[:, n, :], scalar=ALPHA, in1=r, op0=ALU.mult, op1=ALU.add))
                layer_norm(nc, ch, K, var_ok, (root_ok, n + 1), r, stats[:, n, :], ln[:, 0, :], ln[:, 1, :]).then_inc(row_ok, 1)


def build(nc, T, out, stages=None):
    S = {}

    def dram(name, shape, dt=F32):
        S[name] = nc.dram_tensor("scratch_" + name, shape, dt, kind="Internal").ap()

    dram("spec", (2, KT, P, 2, HW))
    dram("cm", (CM_TILES, P, SEQ))
    dram("qkv", (SEQ, QKV))
    dram("x1", (SEQ, D))
    dram("scores", (KT, P, 2 * PH, NK))
    dram("gates", (NK, NK, SEQ))
    ctx = ExitStack()
    with ctx:
        K = {}

        def keep(name, shape, dt=F32):
            K[name] = ctx.enter_context(nc.sbuf_tensor("k_" + name, shape, dt))

        K["passed"] = ctx.enter_context(nc.semaphore("passed"))
        keep("ident", [P, P])
        keep("cos", [P, KT, ROPE])
        keep("sin", [P, KT, ROPE])
        keep("ada_col", [P, 4 * KT])
        keep("ada_row", [P, 4, HALF])
        early = ExitStack()
        with early:
            K["h2"] = early.enter_context(nc.sbuf_tensor("k_h2", [64, SEQ], F32))
            K["f3w"] = early.enter_context(nc.sbuf_tensor("k_f3w", [64, 4 * HW], F32))
            K["silu"] = early.enter_context(nc.sbuf_tensor("k_silu", [P, KT], F32))
            K["silu_wide"] = early.enter_context(nc.sbuf_tensor("k_silu_wide", [P, KT, P], F32))
            stage_setup(nc, S, K, T)
            stage_spectra(nc, S, K, T)
        stage_project(nc, S, K, T)
        keep("big", [P, KT, SEQ])
        K["yh"], K["ya"] = K["big"][:, 0:4, :], K["big"][:, 4:6, :]
        K["merged"] = K["u2"] = K["sums"] = K["big"]
        stage_hyena(nc, S, K, T)
        with nc.sbuf_tensor("k_qk", [HD, 2 * HEADS, SEQ], F32) as qk:
            K["qk"] = qk
            stage_rotary(nc, S, K, T)
            stage_attention(nc, S, K, T)
        stage_merge(nc, S, K, T)
        stage_out(nc, S, K, T)
        stage_query(nc, S, K, T)
        with nc.sbuf_tensor("k_sel", [P, 3, SEQ], F32) as sel:
            K["sel"] = sel
            stage_select(nc, S, K, T)
            stage_gates(nc, S, K, T)
        stage_experts(nc, S, K, T)
        stage_final(nc, S, K, T, out)


def layouts(x, c, positions, w_ada, b_ada, w_in, hy_conv_w, hy_conv_b, hy_f1_w, hy_f1_b, hy_f1_freq,
            hy_f2_w, hy_f2_b, hy_f2_freq, hy_f3_w, hy_bias, w_branch_hyena, w_branch_attn, w_out,
            ln1_g, ln1_b, peer_wq, peer_keys, peer_u, peer_v, ln2_g, ln2_b):
    f = np.float32

    def tiles(w, cols):
        k, n = w.shape
        return w.reshape(k // P, P, n // cols, cols).transpose(2, 1, 0, 3)

    def col(vec):
        return vec.reshape(-1, P).T

    wa, ba, win = w_ada[0], b_ada[0], w_in[0]
    hyc, att = 3 * HW, 3 * HEADS * HD
    col_at, row_at = (0, 1024, 3072, 4096), (2048, 2560, 5120, 5632)
    ada = [np.concatenate([wa[:, a:a + D], wa[:, b:b + HALF]], 1) for a, b in zip(col_at, row_at)]
    t = np.arange(SEQ, dtype=np.float64)
    mid = 2 * t + 1
    sym = np.pi * np.outer(mid, mid) / (4 * SEQ)
    lag = np.pi * np.outer(t, mid) / (2 * SEQ)

    def table_cols(a):
        both = np.stack([np.cos(a), np.sin(a)]).astype(f)
        return both.reshape(2, KT, P, KT, P).transpose(3, 2, 0, 1, 4)

    lin = np.linspace(0, 1, SEQ, dtype=f)[:, None]
    w = (2.0 * math.pi * np.arange(SEQ, dtype=f)[:, None] / SEQ).astype(f)
    band = np.linspace(1e-4, 15, 16, dtype=f)[None, :]
    arg = (band * w).astype(f).astype(np.float64)
    feats = np.concatenate([lin, np.cos(arg), -np.sin(arg)], 1).astype(f)
    deltas = np.linspace(math.log(1e-2) / 1.5, math.log(1e-2) / 0.3, HW, dtype=f)
    decay = np.exp(-lin.astype(np.float64) * np.abs(deltas)[None, :].astype(np.float64)).astype(f)
    r, b, p, j = np.ogrid[0:4, 0:2, 0:P, 0:640]
    key, mid_q = np.arange(256)[None, None, None, :], b * P + p
    full = np.broadcast_to((key - mid_q) % 4 == 0, (4, 2, P, 256))
    near = np.broadcast_to(np.abs(key - mid_q) <= 64, (4, 2, P, 256))
    local = np.abs(384 * b + j - (r + 4 * mid_q)) <= 64
    mask = np.where(np.concatenate([full, near, local], 3), f(0), f(NEG)).astype(f)
    return {
        "feats": feats.T, "f1_w": hy_f1_w[0], "f2_w": hy_f2_w[0], "f3_w": hy_f3_w[0],
        "fvec": np.stack([hy_f1_b[0], hy_f1_freq[0], hy_f2_b[0], hy_f2_freq[0]], 1),
        "positions": positions[0].reshape(KT, P).T,
        "inv": (500000.0 ** (-np.arange(0, 16, 2, dtype=np.float64) / 16)).astype(f),
        "c": col(c[0]), "ident": np.eye(P, dtype=f),
        "b_col": np.concatenate([col(ba[a:a + D]) for a in col_at], 1),
        "b_row": np.stack([ba[a:a + HALF] for a in row_at]),
        "decay": decay.reshape(KT, P, HW).transpose(1, 0, 2),
        "tab0": table_cols(lag), "tab1": table_cols(sym),
        "tab1_rows": np.stack([np.cos(sym), np.sin(sym)]).astype(f).reshape(2, KT, P, SEQ).transpose(1, 2, 0, 3),
        "w_ada": np.concatenate([tiles(a, 256) for a in ada]),
        "xT": x[0].T.reshape(KT, P, SEQ).transpose(1, 0, 2), "x": x[0],
        "w_cm": tiles(np.concatenate([win[:, :hyc], win[:, hyc + att:]], 1), P),
        "w_qkv": tiles(win[:, hyc:hyc + att], QC),
        "conv_w": hy_conv_w[0].reshape(3, HY_TILES, P).transpose(2, 1, 0),
        "conv_b": col(hy_conv_b[0]),
        "hy_bias": hy_bias[0].reshape(2, 4, P).transpose(2, 0, 1),
        "mask": mask,
        "w_bh": tiles(w_branch_hyena[0], P), "w_ba": tiles(w_branch_attn[0], P),
        "w_out": w_out[0].reshape(KT, P, D).transpose(1, 0, 2),
        "ln": np.stack([ln1_g[0], ln1_b[0], ln2_g[0], ln2_b[0]]),
        "wq": tiles(peer_wq[0], P), "keysT": peer_keys[0].reshape(2 * PH, NK, P).transpose(0, 2, 1),
        "iota": np.arange(256, dtype=f),
        "utab": peer_u[0].reshape(NK, NK, KT, P).transpose(0, 3, 2, 1),
        "vtab": peer_v[0].reshape(NK, NK, D),
    }


def kernel(**inputs):
    import concourse.bacc as bacc
    from concourse.bass_utils import run_bass_kernel_spmd

    nc = bacc.Bacc("TRN2", target_bir_lowering=False, num_devices=1)
    arrays, T = {}, {}
    for name, a in layouts(**{k: np.asarray(v) for k, v in inputs.items()}).items():
        a = np.ascontiguousarray(a)
        arrays["in_" + name] = a
        T[name] = nc.dram_tensor("in_" + name, a.shape, mybir.dt.from_np(a.dtype), kind="ExternalInput").ap()
    out = nc.dram_tensor("out", (1, SEQ, D), F32, kind="ExternalOutput").ap()
    build(nc, T, out)
    return run_bass_kernel_spmd(nc, [arrays], core_ids=[0]).results[0]["out"]
```

```python
import math
from contextlib import ExitStack

import numpy as np

import concourse.bass as bass
from concourse import mybir

F32 = mybir.dt.float32
F32R = mybir.dt.float32r
F16 = mybir.dt.float16
I32 = mybir.dt.int32
U32 = mybir.dt.uint32
ALU = mybir.AluOpType
ACT = mybir.ActivationFunctionType
AX = mybir.AxisListType.X

P = 128
SEQ = 1024
D = 1024
KT = D // P
HALF = 512
HW = 512
HEADS = 12
HD = 64
SLOTS = 4
ROPE = 8
PH = 8
NK = 128
TOPK = 16
ALPHA = 2.0 ** 0.25
EPS = 1e-5
NEG = -1e30
CM_TILES = (3 * HW + 2 * D) // P
HY_TILES = 3 * HW // P
QKV = 3 * HEADS * HD
QC = 384

MAGIC = 1.5 * 2.0 ** 23
TWO_PI = (6.28125, 0.0019340515136718750, 1.2556659146443102e-06)


class Chain:

    def __init__(self, eng, sem):
        self.eng, self.sem, self.base, self.n = eng, sem, 0, 0

    def link(self, ins, K=None):
        self.n += 1
        ins.then_inc(self.sem, 1)
        if K is None:
            self.eng.wait_ge(self.sem, self.base + self.n)
        else:
            hold(self.eng, K, self.sem, self.base + self.n)

    def loop(self, i, per):
        self.start, self.per = self.base + self.n, per
        self.base, self.n = self.start + i * per, 0

    def done(self, times):
        assert self.n == self.per, (self.n, self.per)
        self.base, self.n = self.start + times * self.per, 0


def hold(eng, K, sem, value):
    eng.wait_ge(sem, value)
    eng.sem_inc(K["passed"], 1)


def product3(nc, out, w, x, first, last):
    nc.tensor.matmul(out, w[0], x[0], start=first, stop=False)
    nc.tensor.matmul(out, w[0], x[1], start=False, stop=False)
    return nc.tensor.matmul(out, w[1], x[0], start=False, stop=last)


def cleared_sems(nc, ctx, prefix):
    used = []

    def clear():
        nc.clear_and_free_semaphores(used)
        nc.all_engine_barrier()

    def sem(name):
        used.append(nc.alloc_semaphore(name=prefix + name))
        return used[-1]

    ctx.callback(clear)
    return sem




def sine_prepare(nc, chain, out, turns, src, bias, freq):
    v = nc.vector
    chain.link(v.tensor_scalar(out, src, bias, freq, ALU.add, ALU.mult))
    wrap(nc, chain, out, turns)


def wrap(nc, chain, x, turns):
    v = nc.vector
    chain.link(v.tensor_scalar(turns, x, 1.0 / (2.0 * math.pi), MAGIC, ALU.mult, ALU.add))
    chain.link(v.tensor_scalar(turns, turns, -MAGIC, None, ALU.add))
    for part in TWO_PI:
        chain.link(v.scalar_tensor_tensor(out=x, in0=turns, scalar=-part, in1=x, op0=ALU.mult, op1=ALU.add))
    chain.link(v.tensor_scalar(x, x, -3.1415925, 3.1415925, ALU.max, ALU.min))


def stage_setup(nc, S, K, T):
    ctx = ExitStack()
    with ctx:
        sb = lambda n, s, d=F32: ctx.enter_context(nc.sbuf_tensor("su_" + n, s, d))
        sem = cleared_sems(nc, ctx, "su_")
        feats = sb("feats", [33, SEQ])
        f1w, f2w = sb("f1w", [33, 64]), sb("f2w", [64, 64])
        fvec = sb("fvec", [64, 4])
        arg, turns = sb("arg", [64, SEQ]), sb("turns", [64, SEQ])
        h1 = sb("h1", [64, SEQ])
        pos_i, pos = sb("pos_i", [P, KT], I32), sb("pos", [P, KT])
        inv = sb("inv", [P, ROPE])
        ang = sb("ang", [P, 2, KT, ROPE])
        ang_turns = sb("ang_turns", [P, 2, KT, ROPE])
        cc = sb("cc", [P, KT])
        ps = ctx.enter_context(nc.psum_tensor("su_ps", [64, 2, HALF], F32))
        loads, ready, layer, args_ok, hid = sem("loads"), sem("silu"), sem("layer"), sem("args"), sem("hidden")
        chain_s = sem("chain")
        act_s = sem("act")
        block = ctx.enter_context(nc.Block())

        @block.sync
        def _(sp):
            small = [
                (feats[:, :], T["feats"]), (f1w[:, :], T["f1_w"]), (f2w[:, :], T["f2_w"]),
                (K["f3w"][:, :], T["f3_w"]), (fvec[:, :], T["fvec"]), (pos_i[:, :], T["positions"]),
                (inv[:, :], T["inv"].partition_broadcast(P)), (cc[:, :], T["c"]), (K["ident"][:, :], T["ident"]),
                (K["ada_col"][:, :], T["b_col"]),
                (K["ada_row"][:, :, :], T["b_row"].partition_broadcast(P)),
            ]
            for dst, src in small:
                sp.dma_start(dst, src).then_inc(loads, 16)
            sp.wait_ge(loads, 16 * len(small))
            sp.sem_inc(ready, 1)

        @block.tensor
        def _(pe):
            pe.wait_ge(ready, 1)
            for h in range(2):
                last = nc.tensor.matmul(ps[:, h, :], f1w[:, :], feats[:, h * HALF:(h + 1) * HALF], start=True, stop=True)
            last.then_inc(layer, 1)
            pe.wait_ge(hid, 1)
            for h in range(2):
                last = nc.tensor.matmul(ps[:, h, :], f2w[:, :], h1[:, h * HALF:(h + 1) * HALF], start=True, stop=True)
            last.then_inc(layer, 1)

        @block.vector
        def _(dve):
            ch = Chain(dve, chain_s)
            flat = ps[:, :, :].rearrange("p a b -> p (a b)")
            dve.wait_ge(layer, 1)
            sine_prepare(nc, ch, arg[:, :], turns[:, :], flat, fvec[:, 0:1], fvec[:, 1:2])
            nc.vector.tensor_copy(pos[:, :], pos_i[:, :]).then_inc(args_ok, 1)
            dve.wait_ge(args_ok, 1)
            ch.link(nc.vector.tensor_tensor(ang[:, 1, :, :], pos[:, :].unsqueeze(2).to_broadcast([P, KT, ROPE]),
                                            inv[:, :].unsqueeze(1).to_broadcast([P, KT, ROPE]), ALU.mult))
            ch.link(nc.vector.tensor_scalar(ang[:, 0, :, :], ang[:, 1, :, :], 0.5, None, ALU.mult))
            wrap(nc, ch, ang[:, :, :, :].rearrange("p a b c -> p (a b c)"),
                 ang_turns[:, :, :, :].rearrange("p a b c -> p (a b c)"))
            nc.vector.tensor_copy(pos[:, :], pos_i[:, :]).then_inc(args_ok, 1)
            dve.wait_ge(layer, 2)
            dve.wait_ge(hid, 1)
            sine_prepare(nc, ch, arg[:, :], turns[:, :], flat, fvec[:, 2:3], fvec[:, 3:4])
            nc.vector.tensor_copy(pos[:, :], pos_i[:, :]).then_inc(args_ok, 1)
            dve.wait_ge(act_s, 2)
            sc = K["cos"][:, :, :].rearrange("p a b -> p (a b)")
            ch.link(nc.vector.tensor_tensor(sc, sc, sc, ALU.mult))
            ch.link(nc.vector.tensor_scalar(sc, sc, -2.0, 1.0, ALU.mult, ALU.add))
            ch.link(nc.vector.tensor_copy(K["silu_wide"][:, :, :], K["silu"][:, :].unsqueeze(2).to_broadcast([P, KT, P])))

        @block.scalar
        def _(act):
            act.wait_ge(args_ok, 1)
            nc.scalar.activation(h1[:, :], arg[:, :], ACT.Sin).then_inc(hid, 1)
            act.wait_ge(args_ok, 2)
            nc.scalar.activation(K["cos"][:, :, :], ang[:, 0, :, :], ACT.Sin)
            nc.scalar.activation(K["sin"][:, :, :], ang[:, 1, :, :], ACT.Sin)
            act.wait_ge(args_ok, 3)
            nc.scalar.activation(K["h2"][:, :], arg[:, :], ACT.Sin).then_inc(hid, 1)
            nc.scalar.activation(K["silu"][:, :], cc[:, :], ACT.Silu).then_inc(act_s, 2)


def stage_spectra(nc, S, K, T):
    ctx = ExitStack()
    with ctx:
        sb = lambda n, s, d=F32: ctx.enter_context(nc.sbuf_tensor("sp_" + n, s, d))
        sem = cleared_sems(nc, ctx, "sp_")
        decay = sb("decay", [P, KT, HW])
        fb = sb("fb", [P, 2, HW])
        pm = sb("pm", [P, 2, 2, HW])
        taps_h = sb("taps_h", [P, 2, KT, HW], F32R)
        taps_l = sb("taps_l", [P, 2, KT, HW], F32R)
        tab = sb("tab", [P, 2, 2, KT, P])
        tab_h = sb("tab_h", [P, 2, 2, KT, P], F32R)
        tab_l = sb("tab_l", [P, 2, 2, KT, P], F32R)
        spec = sb("spec", [P, 2, 2, HW])
        wada = sb("wada", [P, 2, KT, 256])
        hps = ctx.enter_context(nc.psum_tensor("sp_hps", [P, 2, HALF], F32))
        sps = ctx.enter_context(nc.psum_tensor("sp_sps", [P, 4, HALF], F32))
        aps = ctx.enter_context(nc.psum_tensor("sp_aps", [P, 2, HALF], F32))
        decay_in, taps_mm, pm_ok, hi_ok, lo_ok = sem("decay_in"), sem("taps_mm"), sem("pm_ok"), sem("hi_ok"), sem("lo_ok")
        tab_hi, tab_ok, spec_mm = sem("tab_hi"), sem("tab_ok"), sem("spec_mm")
        tab_in = [sem(f"tab_in{k}") for k in range(2)]
        stored = [sem(f"stored{k}") for k in range(2)]
        ada_in = [sem(f"ada_in{k}") for k in range(2)]
        cos_out, sin_out = sem("cos_out"), sem("sin_out")
        ada_mm, ada_out, chain_s = sem("ada_mm"), sem("ada_out"), sem("chain")
        block = ctx.enter_context(nc.Block())

        @block.sync
        def _(sp):
            sp.dma_start(decay[:, :, :], T["decay"]).then_inc(decay_in, 16)
            with sp.Fori(0, 2) as o:
                with sp.Fori(0, 2) as h:
                    for q in range(4):
                        n = o * KT + h * 4 + q
                        sp.wait_ge(tab_ok, n + 1)
                        sp.dma_start(tab[:, q % 2, :, :, :], T["tab0"][bass.ds(h * 4 + q, 1)][0]).then_inc(tab_in[q % 2], 16)
                        if q < 3:
                            m = (o * 2 + h) * 3 + q
                            sp.wait_ge(ada_mm, m + 1)
                            for c in range(2):
                                sp.dma_start(wada[:, c, :, :], T["w_ada"][bass.ds(m * 2 + c, 1)][0]).then_inc(ada_in[c], 16)

        @block.gpsimd
        def _(pool):
            pool.sem_inc(lo_ok, 2)
            pool.sem_inc(tab_ok, 2)
            with pool.Fori(0, 2) as o:
                for lt in range(KT):
                    n = o * KT + lt
                    pool.wait_ge(hi_ok, n + 1)
                    for j in range(2):
                        last = nc.gpsimd.tensor_tensor(taps_l[:, j, lt, :], pm[:, lt % 2, j, :],
                                                       taps_h[:, j, lt, :].bitcast(F32), ALU.subtract)
                    last.then_inc(lo_ok, 1)
                with pool.Fori(0, 2) as h:
                    for q in range(4):
                        n = o * KT + h * 4 + q
                        s = q % 2
                        pool.wait_ge(tab_hi, n + 1)
                        nc.gpsimd.tensor_tensor(tab_l[:, s, :, :, :], tab[:, s, :, :, :],
                                                tab_h[:, s, :, :, :].bitcast(F32), ALU.subtract).then_inc(tab_ok, 1)

        @block.tensor
        def _(pe):
            pe.sem_inc(spec_mm, 4)
            pe.sem_inc(ada_mm, 1)
            with pe.Fori(0, 2) as o:
                for lt in range(KT):
                    hold(pe, K, chain_s, o * (KT + 1) + lt + 1 + (lt > 0))
                    for j in range(2):
                        last = nc.tensor.matmul(hps[:, j, :], K["h2"][:, lt * P:(lt + 1) * P],
                                                K["f3w"][:, bass.ds(o * HW + j * 2 * HW, HW)], start=True, stop=True)
                    last.then_inc(taps_mm, 1)
                hold(pe, K, lo_ok, (o + 1) * KT + 2)
                with pe.Fori(0, 2) as h:
                    for q in range(4):
                        n = o * KT + h * 4 + q
                        pe.wait_ge(tab_ok, n + 3)
                        pe.wait_ge(cos_out, n + 1)
                        pe.wait_ge(sin_out, n + 1)
                        for j in range(2):
                            for lt in range(KT):
                                last = product3(nc, sps[:, 2 * (q % 2) + j, :],
                                                (tab_h[:, q % 2, j, lt, :], tab_l[:, q % 2, j, lt, :]),
                                                (taps_h[:, j, lt, :], taps_l[:, j, lt, :]), lt == 0, lt == KT - 1)
                            last.then_inc(spec_mm, 1)
                        if q < 3:
                            m = (o * 2 + h) * 3 + q
                            pe.wait_ge(ada_out, m + 1)
                            for c in range(2):
                                pe.wait_ge(ada_in[c], 16 * (m + 1))
                                for ct in range(2 if q < 2 else 1):
                                    for k in range(KT):
                                        flags = dict(start=k == 0, stop=k == KT - 1)
                                        if q < 2:
                                            last = nc.tensor.matmul(aps[:, q % 2, 2 * c + ct:2 * c + ct + 1],
                                                                    wada[:, c, k, ct * P:(ct + 1) * P],
                                                                    K["silu"][:, k:k + 1], **flags)
                                        else:
                                            last = nc.tensor.matmul(aps[:, q % 2, c * 256:(c + 1) * 256],
                                                                    K["silu_wide"][:, k, :], wada[:, c, k, :], **flags)
                            last.then_inc(ada_mm, 1)

        @block.scalar
        def _(act):
            act.sem_inc(cos_out, 2)
            for s in range(2):
                act.sem_inc(stored[s], 16)

            def split_high(o, q):
                act.wait_ge(tab_in[q % 2], 16 * (o * 4 + q // 2 + 1))
                act.wait_ge(spec_mm, 2 * (o * KT + q) + 2)
                nc.scalar.activation(tab_h[:, q % 2, :, :, :], tab[:, q % 2, :, :, :], ACT.Copy).then_inc(tab_hi, 1)

            with act.Fori(0, 2) as o:
                for lt in range(KT):
                    n = o * KT + lt
                    act.wait_ge(pm_ok, 2 * n + 2)
                    if lt == 0:
                        act.wait_ge(spec_mm, 2 * KT * o + 4)
                    nc.scalar.activation(taps_h[:, :, lt, :], pm[:, lt % 2, :, :], ACT.Copy).then_inc(hi_ok, 1)
                split_high(o, 0)
                for q in range(KT):
                    n, s = o * KT + q, q % 2
                    if q + 1 < KT:
                        split_high(o, q + 1)
                    act.wait_ge(spec_mm, 2 * n + 5)
                    act.wait_ge(stored[s], 16 * (o * 4 + q // 2 + 1))
                    nc.scalar.activation(spec[:, s, 0, :], sps[:, 2 * s, :], ACT.Copy, scale=1.0 / SEQ).then_inc(cos_out, 1)
                    act.wait_ge(cos_out, n + 3)
                    act.wait_ge(sin_out, n + 3)
                    act.dma_start(S["spec"][bass.ds(o, 1), q][0], spec[:, s, :, :]).then_inc(stored[s], 16)
            for s in range(2):
                act.wait_ge(stored[s], 16 * (KT + 1))

        @block.vector
        def _(dve):
            v = nc.vector
            ch = Chain(dve, chain_s)
            dve.sem_inc(chain_s, 1)
            ch.n = 1
            dve.sem_inc(sin_out, 2)
            dve.sem_inc(ada_out, 1)
            dve.wait_ge(decay_in, 16)
            with dve.Fori(0, 2) as o:
                ch.loop(o, KT + 1)
                for lt in range(KT):
                    n = o * KT + lt
                    dve.wait_ge(taps_mm, n + 1)
                    ch.link(v.tensor_tensor(fb[:, :, :], hps[:, :, :], decay[:, lt, :].unsqueeze(1).to_broadcast([P, 2, HW]), ALU.mult))
                    if lt == 0:
                        ch.link(v.memset(fb[0:1, 1, :], 0.0))
                    dve.wait_ge(lo_ok, n + 1)
                    v.tensor_tensor(pm[:, lt % 2, 0, :], fb[:, 0, :], fb[:, 1, :], ALU.add).then_inc(pm_ok, 1)
                    v.tensor_tensor(pm[:, lt % 2, 1, :], fb[:, 0, :], fb[:, 1, :], ALU.subtract).then_inc(pm_ok, 1)
                    hold(dve, K, pm_ok, 2 * n + 2)
                with dve.Fori(0, 2) as h:
                    for q in range(4):
                        n, s = o * KT + h * 4 + q, q % 2
                        dve.wait_ge(spec_mm, 2 * n + 6)
                        dve.wait_ge(stored[s], 16 * (o * 4 + h * 2 + q // 2 + 1))
                        v.tensor_scalar(spec[:, s, 1, :], sps[:, 2 * s + 1, :], 1.0 / SEQ, None, ALU.mult).then_inc(sin_out, 1)
                        if q < 3:
                            g = o * 2 + h
                            m = g * 3 + q
                            dve.wait_ge(ada_mm, m + 2)
                            if q < 2:
                                col = K["ada_col"][:, bass.ds(g * 8 + 4 * q, 4)]
                                v.tensor_tensor(col, aps[:, q % 2, 0:4], col, ALU.add).then_inc(ada_out, 1)
                            else:
                                row = K["ada_row"][:, bass.ds(g, 1), :][:, 0, :]
                                v.scalar_tensor_tensor(out=row, in0=aps[:, q % 2, :], scalar=1.0, in1=row,
                                                       op0=ALU.add, op1=ALU.add).then_inc(ada_out, 1)
            ch.done(2)




def stage_project(nc, S, K, T):
    ctx = ExitStack()
    with ctx:
        sb = lambda n, s, d=F32: ctx.enter_context(nc.sbuf_tensor("pj_" + n, s, d))
        sem = cleared_sems(nc, ctx, "pj_")
        XS = 4
        xk = sb("xk", [P, XS, SEQ])
        u_h, u_l = sb("u_h", [P, KT, SEQ], F32R), sb("u_l", [P, KT, SEQ], F32R)
        w = sb("w", [P, 2, KT, QC])
        w_h, w_l = sb("w_h", [P, 2, KT, QC], F32R), sb("w_l", [P, 2, KT, QC], F32R)
        out_c = sb("out_c", [P, 2, SEQ])
        out_q = sb("out_q", [P, 2, KT, QC])
        cps = ctx.enter_context(nc.psum_tensor("pj_cps", [P, 4, HALF], F32))
        qps = ctx.enter_context(nc.psum_tensor("pj_qps", [P, 4, HALF], F32))
        x_in = [sem(f"x_in{k}") for k in range(XS)]
        w_in = [sem(f"w_in{k}") for k in range(2)]
        stored = [sem(f"stored{k}") for k in range(2)]
        q_stored = [sem(f"q_stored{k}") for k in range(2)]
        chain_s, u_ok, u_hi, u_lo, w_hi, w_ok = sem("chain"), sem("u_ok"), sem("u_hi"), sem("u_lo"), sem("w_hi"), sem("w_ok")
        cmm, act_out, dve_out, qmm, act_q, dve_q = sem("cmm"), sem("act_out"), sem("dve_out"), sem("qmm"), sem("act_q"), sem("dve_q")
        block = ctx.enter_context(nc.Block())
        CN, QN = CM_TILES, QKV // QC

        @block.sync
        def _(sp):
            for k in range(KT):
                if k >= XS:
                    sp.wait_ge(u_lo, k - XS + 1)
                sp.dma_start(xk[:, k % XS, :], T["xT"][:, k, :]).then_inc(x_in[k % XS], 16)
            with sp.Fori(0, CN // 2) as i:
                for s in range(2):
                    sp.wait_ge(w_ok, 2 * i + s + 1)
                    sp.dma_start(w[:, s, :, 0:P], T["w_cm"][bass.ds(2 * i + s, 1)][0]).then_inc(w_in[s], 16)
            with sp.Fori(0, QN // 2) as i:
                for s in range(2):
                    sp.wait_ge(w_ok, 2 * i + s + 1 + CN)
                    sp.dma_start(w[:, s, :, :], T["w_qkv"][bass.ds(2 * i + s, 1)][0]).then_inc(w_in[s], 16)

        @block.gpsimd
        def _(pool):
            pool.sem_inc(w_ok, 2)

            def split(s, n, count, cols, read):
                pool.wait_ge(w_in[s], 16 * (count + 1))
                hold(pool, K, *read)
                nc.gpsimd.tensor_copy(w_h[:, s, :, 0:cols], w[:, s, :, 0:cols]).then_inc(w_hi, 1)
                pool.wait_ge(w_hi, n + 1)
                nc.gpsimd.tensor_tensor(w_l[:, s, :, 0:cols], w[:, s, :, 0:cols],
                                        w_h[:, s, :, 0:cols].bitcast(F32), ALU.subtract).then_inc(w_ok, 1)

            with pool.Fori(0, CN // 2) as i:
                for s in range(2):
                    n = 2 * i + s
                    split(s, n, i, P, (cmm, 2 * n + 2))
            pool.wait_ge(cmm, 4 + 2 * CN)
            with pool.Fori(0, QN // 2) as i:
                for s in range(2):
                    n = 2 * i + s
                    split(s, n + CN, i + CN // 2, QC, (qmm, KT * n + 1))

        @block.tensor
        def _(pe):
            pe.sem_inc(cmm, 4)
            pe.sem_inc(qmm, 1 + KT)
            pe.wait_ge(u_lo, KT)
            with pe.Fori(0, CN // 2) as i:
                for s in range(2):
                    n = 2 * i + s
                    pe.wait_ge(w_ok, n + 3)
                    pe.wait_ge(act_out, n + 1)
                    pe.wait_ge(dve_out, n + 1)
                    for h in range(2):
                        cut = slice(h * HALF, (h + 1) * HALF)
                        for k in range(KT):
                            last = product3(nc, cps[:, 2 * s + h, :], (w_h[:, s, k, 0:P], w_l[:, s, k, 0:P]),
                                            (u_h[:, k, cut], u_l[:, k, cut]), k == 0, k == KT - 1)
                        last.then_inc(cmm, 1)
            with pe.Fori(0, QN // 2) as i:
                for s in range(2):
                    n = 2 * i + s
                    pe.wait_ge(w_ok, n + 3 + CN)
                    for tt in range(KT):
                        done = act_q if tt % 2 == 0 else dve_q
                        pe.wait_ge(done, 4 * n + tt // 2 + 1)
                        cut = slice(tt * P, (tt + 1) * P)
                        for k in range(KT):
                            last = product3(nc, qps[:, tt % 4, 0:QC], (u_h[:, k, cut], u_l[:, k, cut]),
                                            (w_h[:, s, k, :], w_l[:, s, k, :]), k == 0, k == KT - 1)
                        last.then_inc(qmm, 1)

        @block.scalar
        def _(act):
            act.sem_inc(act_out, 2)
            act.sem_inc(act_q, 2)
            for s in range(2):
                act.sem_inc(stored[s], 16)
                act.sem_inc(q_stored[s], 16)
            for k in range(KT):
                act.wait_ge(u_ok, k + 1)
                nc.scalar.activation(u_h[:, k, :], xk[:, k % XS, :], ACT.Copy).then_inc(u_hi, 1)
            with act.Fori(0, CN // 2) as i:
                for s in range(2):
                    n = 2 * i + s
                    act.wait_ge(cmm, 2 * n + 5)
                    act.wait_ge(stored[s], 16 * (i + 1))
                    nc.scalar.activation(out_c[:, s, 0:HALF], cps[:, 2 * s, :], ACT.Copy).then_inc(act_out, 1)
                    act.wait_ge(act_out, n + 3)
                    act.wait_ge(dve_out, n + 3)
                    act.dma_start(S["cm"][bass.ds(n, 1)][0], out_c[:, s, :]).then_inc(stored[s], 16)
            with act.Fori(0, QN // 2) as i:
                for s in range(2):
                    n = 2 * i + s
                    act.wait_ge(q_stored[s], 16 * (i + 1))
                    for tt in range(0, KT, 2):
                        act.wait_ge(qmm, KT * n + tt + 2 + KT)
                        nc.scalar.activation(out_q[:, s, tt, :], qps[:, tt % 4, 0:QC], ACT.Copy).then_inc(act_q, 1)
                    act.wait_ge(act_q, 4 * n + 6)
                    act.wait_ge(dve_q, 4 * n + 6)
                    act.dma_start(S["qkv"].rearrange("(a p) n -> p a n", p=P)[:, :, bass.ds(n * QC, QC)],
                                  out_q[:, s, :, :]).then_inc(q_stored[s], 16)
            for s in range(2):
                act.wait_ge(stored[s], 16 * (CN // 2 + 1))
                act.wait_ge(q_stored[s], 16 * (QN // 2 + 1))

        @block.vector
        def _(dve):
            v = nc.vector
            ch = Chain(dve, chain_s)
            dve.sem_inc(dve_out, 2)
            dve.sem_inc(dve_q, 2)
            for a in (KT, 3 * KT):
                ch.link(v.tensor_scalar(K["ada_col"][:, a:a + KT], K["ada_col"][:, a:a + KT], 1.0, None, ALU.add))

            def low(k):
                dve.wait_ge(u_hi, k + 1)
                v.tensor_tensor(u_l[:, k, :], xk[:, k % XS, :], u_h[:, k, :].bitcast(F32), ALU.subtract).then_inc(u_lo, 1)

            for k in range(KT):
                dve.wait_ge(x_in[k % XS], 16 * (k // XS + 1))
                v.tensor_scalar(xk[:, k % XS, :], xk[:, k % XS, :], K["ada_col"][:, KT + k:KT + k + 1],
                                K["ada_col"][:, k:k + 1], ALU.mult, ALU.add).then_inc(u_ok, 1)
                if k >= 1:
                    low(k - 1)
            low(KT - 1)
            with dve.Fori(0, CN // 2) as i:
                for s in range(2):
                    n = 2 * i + s
                    dve.wait_ge(cmm, 2 * n + 6)
                    dve.wait_ge(stored[s], 16 * (i + 1))
                    v.tensor_copy(out_c[:, s, HALF:SEQ], cps[:, 2 * s + 1, :]).then_inc(dve_out, 1)
            with dve.Fori(0, QN // 2) as i:
                for s in range(2):
                    n = 2 * i + s
                    dve.wait_ge(q_stored[s], 16 * (i + 1))
                    for tt in range(1, KT, 2):
                        dve.wait_ge(qmm, KT * n + tt + 2 + KT)
                        v.tensor_copy(out_q[:, s, tt, :], qps[:, tt % 4, 0:QC]).then_inc(dve_q, 1)


def stage_hyena(nc, S, K, T):
    ctx = ExitStack()
    with ctx:
        sb = lambda n, s, d=F32: ctx.enter_context(nc.sbuf_tensor("hy_" + n, s, d))
        sem = cleared_sems(nc, ctx, "hy_")
        yh = K["yh"]
        cw, cb, bias = sb("cw", [P, HY_TILES, 3]), sb("cb", [P, HY_TILES]), sb("bias", [P, 2, 4])
        raw = sb("raw", [P, SEQ])
        xg = K["big"][:, 4:8, :]
        z_h, z_l = sb("z_h", [P, KT, HW], F32R), sb("z_l", [P, KT, HW], F32R)
        y_h, y_l = sb("y_h", [P, KT, 2, HW], F32R), sb("y_l", [P, KT, 2, HW], F32R)
        tab = sb("tab", [P, 2, 2, SEQ])
        tab_h, tab_l = sb("tab_h", [P, 2, 2, SEQ], F32R), sb("tab_l", [P, 2, 2, SEQ], F32R)
        spec = sb("spec", [P, 2, 2, HW])
        prod, ytmp = sb("prod", [P, 2, HW]), sb("ytmp", [P, 2, HW])
        ps = ctx.enter_context(nc.psum_tensor("hy_ps", [P, 8, HALF], F32))
        small_in, v_in, raw_in, raw_used = sem("small_in"), sem("v_in"), sem("raw_in"), sem("raw_used")
        tab_in = [sem(f"tab_in{k}") for k in range(2)]
        spec_in = [sem(f"spec_in{k}") for k in range(2)]
        tab_hi, tab_ok, spec_used = sem("tab_hi"), sem("tab_ok"), sem("spec_used")
        z_ok, z_hi, z_lo, tp, fwd = sem("z_ok"), sem("z_hi"), sem("z_lo"), sem("tp"), sem("fwd")
        y_ok, y_hi, y_lo, inv, slab, chain_s = sem("y_ok"), sem("y_hi"), sem("y_lo"), sem("inv"), sem("slab"), sem("chain")
        block = ctx.enter_context(nc.Block())
        STEPS = 2 * KT

        @block.sync
        def _(sp):
            sp.dma_start(cw[:, :, :], T["conv_w"]).then_inc(small_in, 16)
            sp.dma_start(cb[:, :], T["conv_b"]).then_inc(small_in, 16)
            sp.dma_start(bias[:, :, :], T["hy_bias"]).then_inc(small_in, 16)
            for c in range(4):
                sp.dma_start(xg[:, c, :], S["cm"][c]).then_inc(v_in, 16)
            with sp.Fori(0, 2) as o:
                for j in range(STEPS):
                    sp.wait_ge(tab_ok, o * STEPS + j + 1)
                    src = T["tab1"][j].rearrange("p a b c -> p a (b c)") if j < KT else T["tab1_rows"][j - KT]
                    sp.dma_start(tab[:, j % 2, :, :], src).then_inc(tab_in[j % 2], 16)
                    if j < KT:
                        sp.wait_ge(spec_used, o * KT + j + 1)
                        sp.dma_start(spec[:, j % 2, :, :], S["spec"][bass.ds(o, 1), j][0]).then_inc(spec_in[j % 2], 16)
                    if j < 4:
                        sp.wait_ge(raw_used, o * 4 + j + 1)
                        sp.dma_start(raw[:, :], S["cm"][bass.ds(o * 4 + 4 + j, 1)][0]).then_inc(raw_in, 16)

        @block.gpsimd
        def _(pool):
            pool.sem_inc(tab_ok, 2)
            pool.sem_inc(y_lo, 1)

            def split_low(o, j):
                pool.wait_ge(tab_hi, o * STEPS + j + 1)
                nc.gpsimd.tensor_tensor(tab_l[:, j % 2, :, :], tab[:, j % 2, :, :],
                                        tab_h[:, j % 2, :, :].bitcast(F32), ALU.subtract).then_inc(tab_ok, 1)

            with pool.Fori(0, 2) as o:
                split_low(o, 0)
                for j in range(STEPS):
                    if j + 1 < STEPS:
                        split_low(o, j + 1)
                    if j < KT:
                        pool.wait_ge(y_hi, o * KT + j + 1)
                        nc.gpsimd.tensor_tensor(y_l[:, j, :, :], ytmp[:, :, :], y_h[:, j, :, :].bitcast(F32),
                                                ALU.subtract).then_inc(y_lo, 1)

        @block.tensor
        def _(pe):
            pe.sem_inc(slab, 2)
            with pe.Fori(0, 2) as o:
                pe.wait_ge(z_ok, o * 4 + 4)
                for tt in range(KT):
                    if tt >= 4:
                        pe.wait_ge(z_lo, o * KT + tt - 3)
                    for c in range(4):
                        last = nc.tensor.transpose(ps[:, 4 + tt % 4, c * P:(c + 1) * P],
                                                   yh[:, c, tt * P:(tt + 1) * P], K["ident"][:, :])
                    last.then_inc(tp, 1)
                hold(pe, K, z_lo, o * KT + KT)
                for j in range(KT):
                    s = j % 2
                    pe.wait_ge(tab_ok, o * STEPS + j + 3)
                    if j >= 2:
                        pe.wait_ge(y_ok, o * KT + j - 1)
                    for a in range(2):
                        for tt in range(KT):
                            cut = slice(tt * P, (tt + 1) * P)
                            last = product3(nc, ps[:, 2 * s + a, :], (tab_h[:, s, a, cut], tab_l[:, s, a, cut]),
                                            (z_h[:, tt, :], z_l[:, tt, :]), tt == 0, tt == KT - 1)
                        last.then_inc(fwd, 1)
                pe.wait_ge(y_ok, o * KT + KT)
                for j in range(KT):
                    s = j % 2
                    pe.wait_ge(tab_ok, o * STEPS + KT + j + 3)
                    pe.wait_ge(y_lo, o * KT + j + 2)
                    for c in range(4):
                        cc = slice(c * P, (c + 1) * P)
                        for h in range(2):
                            cut = slice(h * HALF, (h + 1) * HALF)
                            for a in range(2):
                                last = product3(nc, ps[:, 2 * c + h, :], (y_h[:, j, a, cc], y_l[:, j, a, cc]),
                                                (tab_h[:, s, a, cut], tab_l[:, s, a, cut]),
                                                j == 0 and a == 0, j == KT - 1 and a == 1)
                        if j == KT - 1 and c < 3:
                            last.then_inc(inv, 1)
                    last.then_inc(inv if j == KT - 1 else slab, 1)

        @block.scalar
        def _(act):
            def split_high(o, j):
                act.wait_ge(tab_in[j % 2], 16 * (o * KT + j // 2 + 1))
                if j < 2:
                    act.wait_ge(inv, 4 * o + 1)
                elif j <= KT + 1:
                    act.wait_ge(fwd, o * STEPS + 2 * (j - 1))
                else:
                    act.wait_ge(slab, o * (KT - 1) + j - KT - 1 + 2)
                nc.scalar.activation(tab_h[:, j % 2, :, :], tab[:, j % 2, :, :], ACT.Copy).then_inc(tab_hi, 1)

            act.sem_inc(inv, 1)
            with act.Fori(0, 2) as o:
                split_high(o, 0)
                for tt in range(KT):
                    act.wait_ge(tp, o * KT + tt + 1)
                    nc.scalar.activation(z_h[:, tt, :], ps[:, 4 + tt % 4, :], ACT.Copy).then_inc(z_hi, 1)
                for j in range(STEPS):
                    if j + 1 < STEPS:
                        split_high(o, j + 1)
                    if j < KT:
                        act.wait_ge(y_ok, o * KT + j + 1)
                        nc.scalar.activation(y_h[:, j, :, :], ytmp[:, :, :], ACT.Copy).then_inc(y_hi, 1)

        @block.vector
        def _(dve):
            v = nc.vector
            ch = Chain(dve, chain_s)
            dve.sem_inc(spec_used, 2)
            dve.sem_inc(raw_used, 1)

            def short(dst, src, wcol, bcol):
                ch.link(v.tensor_scalar(dst, src, wcol(1), bcol, ALU.mult, ALU.add))
                ch.link(v.scalar_tensor_tensor(out=dst[:, 1:SEQ], in0=src[:, 0:SEQ - 1], scalar=wcol(0),
                                               in1=dst[:, 1:SEQ], op0=ALU.mult, op1=ALU.add))
                return v.scalar_tensor_tensor(out=dst[:, 0:SEQ - 1], in0=src[:, 1:SEQ], scalar=wcol(2),
                                              in1=dst[:, 0:SEQ - 1], op0=ALU.mult, op1=ALU.add)

            dve.wait_ge(small_in, 48)
            dve.wait_ge(v_in, 64)
            for c in range(4):
                short(yh[:, c, :], xg[:, c, :], lambda a: cw[:, c, a:a + 1], cb[:, c:c + 1]).then_inc(z_ok, 1)
            dve.wait_ge(z_ok, 4)
            with dve.Fori(0, 2) as o:
                ch.loop(o, 4 * 2 + KT * 5 + 4)
                for tt in range(KT):
                    dve.wait_ge(z_hi, o * KT + tt + 1)
                    v.tensor_tensor(z_l[:, tt, :], ps[:, 4 + tt % 4, :], z_h[:, tt, :].bitcast(F32),
                                    ALU.subtract).then_inc(z_lo, 1)
                for j in range(KT):
                    s = j % 2
                    if j < 4:
                        tile = o * 4 + 4 + j
                        dve.wait_ge(raw_in, 16 * (o * 4 + j + 1))
                        short(xg[:, j, :], raw[:, :], lambda a: cw[:, bass.ds(tile, 1), a:a + 1][:, 0, :],
                              cb[:, bass.ds(tile, 1)]).then_inc(raw_used, 1)
                    dve.wait_ge(fwd, o * STEPS + 2 * j + 2)
                    dve.wait_ge(spec_in[s], 16 * (o * 4 + j // 2 + 1))
                    zr, zs, kr, ks = ps[:, 2 * s, :], ps[:, 2 * s + 1, :], spec[:, s, 0, :], spec[:, s, 1, :]
                    ch.link(v.tensor_tensor(prod[:, :, :], ps[:, 2 * s:2 * s + 2, :], spec[:, s, :, :], ALU.mult))
                    dve.wait_ge(y_lo, o * KT + j + 1)
                    ch.link(v.tensor_tensor(ytmp[:, 0, :], prod[:, 0, :], prod[:, 1, :], ALU.subtract))
                    ch.link(v.tensor_tensor(prod[:, 0, :], zr, ks, ALU.mult))
                    ch.link(v.tensor_tensor(prod[:, 1, :], zs, kr, ALU.mult))
                    ch.link(v.tensor_tensor(ytmp[:, 1, :], prod[:, 0, :], prod[:, 1, :], ALU.add))
                    v.sem_inc(spec_used, 1)
                    v.sem_inc(y_ok, 1)
                for c in range(4):
                    dve.wait_ge(inv, 4 * o + c + 2)
                    z = yh[:, c, :]
                    ch.link(v.scalar_tensor_tensor(out=z, in0=z, scalar=bias[:, bass.ds(o, 1), c:c + 1][:, 0, :],
                                                   in1=ps[:, 2 * c:2 * c + 2, :].rearrange("p a b -> p (a b)"),
                                                   op0=ALU.mult, op1=ALU.add))
                    v.tensor_tensor(z, z, xg[:, c, :], ALU.mult).then_inc(z_ok, 1)
                hold(dve, K, z_ok, o * 4 + 8)
            ch.done(2)


def stage_rotary(nc, S, K, T):
    ctx = ExitStack()
    with ctx:
        sb = lambda n, s, d=F32: ctx.enter_context(nc.sbuf_tensor("ro_" + n, s, d))
        sem = cleared_sems(nc, ctx, "ro_")
        rows = sb("rows", [P, 2, 2 * HEADS, HD])
        tmp = sb("tmp", [P, 4, 2 * HEADS, ROPE])
        ps = ctx.enter_context(nc.psum_tensor("ro_ps", [HD, 6, HALF], F32))
        rows_in = [sem(f"rows_in{k}") for k in range(2)]
        chain_s, rot, tp, act_out, dve_out = sem("chain"), sem("rot"), sem("tp"), sem("act_out"), sem("dve_out")
        block = ctx.enter_context(nc.Block())

        @block.sync
        def _(sp):
            with sp.Fori(0, KT // 2) as i:
                for s in range(2):
                    tt = 2 * i + s
                    sp.wait_ge(tp, 6 * tt + 1)
                    sp.dma_start(rows[:, s, :, :], S["qkv"].rearrange("(a p) n -> a p n", p=P)[bass.ds(tt, 1)][0]
                                 [:, 0:2 * HEADS * HD].rearrange("p (h e) -> p h e", e=HD)).then_inc(rows_in[s], 16)

        @block.tensor
        def _(pe):
            pe.sem_inc(tp, 7)
            with pe.Fori(0, KT // 2) as i:
                for s in range(2):
                    tt = 2 * i + s
                    hold(pe, K, rot, tt + 1)
                    for b in range(6):
                        hold(pe, K, act_out if b % 2 == 0 else dve_out, 3 * tt + b // 2 + 1)
                        for h in range(4):
                            last = nc.tensor.transpose(ps[:, b, h * P:(h + 1) * P], rows[:, s, 4 * b + h, :], K["ident"][:, :])
                        last.then_inc(tp, 1)

        def evacuate(eng, copy, done, parity, s, tt):
            for b in range(parity, 6, 2):
                eng.wait_ge(tp, 6 * tt + b + 8)
                copy(K["qk"][:, 4 * b:4 * b + 4, bass.ds(tt * P, P)],
                     ps[:, b, :].rearrange("p (h t) -> p h t", t=P)).then_inc(done, 1)

        @block.scalar
        def _(act):
            act.sem_inc(act_out, 3)
            with act.Fori(0, KT // 2) as i:
                for s in range(2):
                    evacuate(act, lambda o, x: nc.scalar.activation(o, x, ACT.Copy), act_out, 0, s, 2 * i + s)

        @block.vector
        def _(dve):
            v = nc.vector
            ch = Chain(dve, chain_s)
            dve.sem_inc(dve_out, 3)
            with dve.Fori(0, KT // 2) as i:
                for s in range(2):
                    tt = 2 * i + s
                    dve.wait_ge(rows_in[s], 16 * (i + 1))
                    wide = lambda t: t[:, bass.ds(tt, 1), :].to_broadcast([P, 2 * HEADS, ROPE])
                    cos, sin = wide(K["cos"]), wide(K["sin"])
                    a, b = rows[:, s, :, 0:ROPE], rows[:, s, :, ROPE:2 * ROPE]
                    v.tensor_tensor(tmp[:, 0, :, :], a, cos, ALU.mult).then_inc(chain_s, 1)
                    v.tensor_tensor(tmp[:, 1, :, :], b, sin, ALU.mult).then_inc(chain_s, 1)
                    v.tensor_tensor(tmp[:, 2, :, :], b, cos, ALU.mult).then_inc(chain_s, 1)
                    v.tensor_tensor(tmp[:, 3, :, :], a, sin, ALU.mult).then_inc(chain_s, 1)
                    dve.wait_ge(chain_s, 6 * tt + 4)
                    v.tensor_tensor(a, tmp[:, 0, :, :], tmp[:, 1, :, :], ALU.subtract).then_inc(chain_s, 1)
                    v.tensor_tensor(b, tmp[:, 2, :, :], tmp[:, 3, :, :], ALU.add).then_inc(chain_s, 1)
                    dve.wait_ge(chain_s, 6 * tt + 6)
                    v.sem_inc(rot, 1)
                    evacuate(dve, v.tensor_copy, dve_out, 1, s, tt)


KEYS = 256 + 256 + 640


def stage_attention(nc, S, K, T):
    ctx = ExitStack()
    with ctx:
        sb = lambda n, s, d=F32: ctx.enter_context(nc.sbuf_tensor("at_" + n, s, d))
        sem = cleared_sems(nc, ctx, "at_")
        qk, ya = K["qk"], K["ya"]
        mask = sb("mask", [P, 2, KEYS])
        v_near = sb("v_near", [P, KT, SLOTS * HD])
        v_class = sb("v_class", [P, 4, 2, 2 * SLOTS * HD])
        qr = sb("qr", [HD, HEADS, 256])
        score, prob_t = sb("score", [P, 2, KEYS]), sb("prob_t", [P, 2, KEYS])
        prob = score
        top, den, rden = sb("top", [P, 2, 2]), sb("den", [P, 8]), sb("rden", [P, 8])
        y = sb("y", [P, 2, SLOTS * HD])
        sps = ctx.enter_context(nc.psum_tensor("at_sps", [P, 3 * HALF], F32))
        tps = ctx.enter_context(nc.psum_tensor("at_tps", [P, 3 * HALF], F32))
        yps = ctx.enter_context(nc.psum_tensor("at_yps", [P, 2, HALF], F32))
        ytps = yps[:, 1, :]
        v_in, q_ok, s_mm, s_used, s_ok = sem("v_in"), sem("q_ok"), sem("s_mm"), sem("s_used"), sem("s_ok")
        mask_in = [sem(f"mask_in{k}") for k in range(2)]
        p_ok, t_mm, t_act, t_dve, pv_mm, y_ok, yt_mm, yt_ok = (sem(n) for n in (
            "p_ok", "t_mm", "t_act", "t_dve", "pv_mm", "y_ok", "yt_mm", "yt_ok"))
        rd, rd2 = sem("top_ok"), sem("rden_ok")
        block = ctx.enter_context(nc.Block())
        U = 2 * SLOTS
        CUT = 512

        @block.sync
        def _(sp):
            vcol = 2 * HEADS * HD
            sp.dma_start(v_near[:, :, :], S["qkv"].rearrange("(a p) n -> p a n", p=P)[:, :, vcol:vcol + 256]).then_inc(v_in, 16)
            for r in range(4):
                sp.dma_start(v_class[:, r, :, :],
                             S["qkv"].rearrange("(a p r) n -> r p a n", p=P, r=4)[r][:, :, vcol + 256:]).then_inc(v_in, 16)
            with sp.Fori(0, 4) as r:
                for b in range(2):
                    sp.wait_ge(s_used, U * r + 4 * b + 4)
                    sp.dma_start(mask[:, b, :], T["mask"][bass.ds(r, 1), b][0]).then_inc(mask_in[b], 16)

        @block.tensor
        def _(pe):
            pe.sem_inc(s_mm, 1)
            pe.sem_inc(t_mm, 2)
            pe.sem_inc(pv_mm, 2)

            def scores(r, u):
                b, hs = divmod(u, SLOTS)
                hold(pe, K, s_used, U * r + u + 8)
                cls = bass.ds(r, 256, 4)
                q = lambda g: qr[:, 4 * g + hs, b * P:(b + 1) * P]
                keys = lambda g, cut: qk[:, HEADS + 4 * g + hs, cut]
                nc.tensor.matmul(sps[:, 0:256], q(2), keys(2, cls), start=True, stop=True)
                nc.tensor.matmul(sps[:, 256:512], q(1), keys(1, cls), start=True, stop=True)
                nc.tensor.matmul(sps[:, 512:1024], q(0), keys(0, slice(384 * b, 384 * b + 512)), start=True, stop=True)
                nc.tensor.matmul(sps[:, 1024:KEYS], q(0), keys(0, slice(384 * b + 512, 384 * b + 640)),
                                 start=True, stop=True).then_inc(s_mm, 1)

            def turn_y(r, b):
                hold(pe, K, y_ok, U * r + 4 * b + 6)
                for c in range(2):
                    last = nc.tensor.transpose(ytps[:, c * P:(c + 1) * P], y[:, b, c * P:(c + 1) * P], K["ident"][:, :])
                last.then_inc(yt_mm, 1)

            def yt_read(r, u):
                if u % SLOTS == 1:
                    hold(pe, K, yt_ok, 2 * r + u // SLOTS + 2)

            pe.wait_ge(v_in, 80)
            with pe.Fori(0, 4) as r:
                pe.wait_ge(q_ok, r + 1)
                scores(r, 0)
                for u in range(U):
                    b, hs = divmod(u, SLOTS)
                    n = U * r + u
                    if u + 1 < U:
                        scores(r, u + 1)
                    hold(pe, K, p_ok, n + 3)
                    hold(pe, K, t_act, n + 1)
                    hold(pe, K, t_dve, n + 1)
                    for i in range(KEYS // P):
                        last = nc.tensor.transpose(tps[:, i * P:(i + 1) * P], prob[:, u % 2, i * P:(i + 1) * P], K["ident"][:, :])
                    last.then_inc(t_mm, 1)
                    hold(pe, K, t_act, n + 2)
                    hold(pe, K, t_dve, n + 2)
                    hold(pe, K, y_ok, n + 1)
                    yt_read(r, u)
                    for i in range(KEYS // P):
                        if i < 4:
                            g = 1 - i // 2
                            val = v_class[:, bass.ds(r, 1), i % 2, (g * SLOTS + hs) * HD:(g * SLOTS + hs + 1) * HD][:, 0, :]
                        else:
                            val = v_near[:, 3 * b + i - 4, hs * HD:(hs + 1) * HD]
                        last = nc.tensor.matmul(yps[:, u % 2, 0:HD], prob_t[:, u % 2, i * P:(i + 1) * P], val,
                                                start=(i == 0), stop=(i == KEYS // P - 1))
                    last.then_inc(pv_mm, 1)
                    if u == SLOTS:
                        turn_y(r, 0)
                turn_y(r, 1)

        @block.scalar
        def _(act):
            act.sem_inc(p_ok, 2)
            act.sem_inc(t_act, 1)
            act.sem_inc(yt_ok, 2)

            def expo(r, u):
                n = U * r + u
                act.wait_ge(s_ok, n + 1)
                nc.scalar.activation(prob[:, u % 2, :], score[:, u % 2, :], ACT.Exp, bias=top[:, u % 2, 1:2],
                                     scale=HD ** -0.5, accum_out=den[:, u:u + 1]).then_inc(p_ok, 1)

            def put_y(r, b):
                act.wait_ge(yt_mm, 2 * r + b + 1)
                nc.scalar.activation(ya.rearrange("p c (b m r) -> p r b c m", b=2, r=4)[:, bass.ds(r, 1), b, :, :][:, 0],
                                     ytps[:, 0:256].rearrange("p (c m) -> p c m", c=2), ACT.Copy).then_inc(yt_ok, 1)

            with act.Fori(0, 4) as r:
                act.wait_ge(s_mm, U * r + 1)
                nc.scalar.activation(qr[:, :, :], qk[:, 0:HEADS, bass.ds(r, 256, 4)], ACT.Copy).then_inc(q_ok, 1)
                expo(r, 0)
                for u in range(U):
                    n = U * r + u
                    act.wait_ge(t_mm, n + 3)
                    act.wait_ge(pv_mm, n + 1)
                    nc.scalar.activation(prob_t[:, u % 2, CUT:], tps[:, CUT:KEYS], ACT.Copy).then_inc(t_act, 1)
                    if u + 1 < U:
                        expo(r, u + 1)
                    if u == 4:
                        put_y(r, 0)
                put_y(r, 1)

        @block.vector
        def _(dve):
            v = nc.vector
            dve.sem_inc(s_used, 8)
            dve.sem_inc(t_dve, 1)
            dve.sem_inc(y_ok, 2)

            def mask_scores(r, u):
                n, b, s = U * r + u, u // SLOTS, u % 2
                dve.wait_ge(s_mm, n + 2)
                dve.wait_ge(t_mm, n + 1)
                if u % SLOTS == 0:
                    dve.wait_ge(mask_in[b], 16 * (r + 1))
                v.tensor_tensor(score[:, s, :], sps[:, 0:KEYS], mask[:, b, :], ALU.add).then_inc(s_used, 1)

            def maximum(r, u):
                n, s = U * r + u, u % 2
                hold(dve, K, s_used, n + 9)
                v.tensor_reduce(top[:, s, 0:1], score[:, s, :], AX, ALU.max).then_inc(rd, 1)
                dve.wait_ge(rd, n + 1)
                v.tensor_scalar(top[:, s, 1:2], top[:, s, 0:1], -HD ** -0.5, None, ALU.mult).then_inc(s_ok, 1)

            def normalise(r, u):
                n, (b, hs) = U * r + u, divmod(u, SLOTS)
                hold(dve, K, pv_mm, n + 3)
                v.reciprocal(rden[:, u:u + 1], den[:, u:u + 1]).then_inc(rd2, 1)
                dve.wait_ge(rd2, n + 1)
                if hs == 0:
                    dve.wait_ge(yt_ok, 2 * r + b + 1)
                v.tensor_scalar(y[:, b, hs * HD:(hs + 1) * HD], yps[:, u % 2, 0:HD], rden[:, u:u + 1], None,
                                ALU.mult).then_inc(y_ok, 1)

            with dve.Fori(0, 4) as r:
                mask_scores(r, 0)
                maximum(r, 0)
                for u in range(U):
                    n = U * r + u
                    if u + 1 < U:
                        mask_scores(r, u + 1)
                    dve.wait_ge(t_mm, n + 3)
                    dve.wait_ge(pv_mm, n + 1)
                    v.tensor_copy(prob_t[:, u % 2, 0:CUT], tps[:, 0:CUT]).then_inc(t_dve, 1)
                    if u + 1 < U:
                        maximum(r, u + 1)
                    if u >= 1:
                        normalise(r, u - 1)
                normalise(r, U - 1)


def stage_merge(nc, S, K, T):
    ctx = ExitStack()
    with ctx:
        sb = lambda n, s, d=F32: ctx.enter_context(nc.sbuf_tensor("me_" + n, s, d))
        sem = cleared_sems(nc, ctx, "me_")
        NH, NY = 4, 6
        y_h, y_l = sb("y_h", [P, NY, SEQ], F32R), sb("y_l", [P, NY, SEQ], F32R)
        w = sb("w", [P, 2, NY, P])
        w_h, w_l = sb("w_h", [P, 2, NY, P], F32R), sb("w_l", [P, 2, NY, P], F32R)
        gate = sb("gate", [P, 2, 2, SEQ])
        tmp = sb("tmp", [P, 2, SEQ])
        ps = ctx.enter_context(nc.psum_tensor("me_ps", [P, 8, HALF], F32))
        w_in = [sem(f"w_in{k}") for k in range(2)]
        g_in = [sem(f"g_in{k}") for k in range(2)]
        y_hi, y_lo, w_hi, w_ok, mm, g_ok, m_ok, chain_s = (sem(n) for n in (
            "y_hi", "y_lo", "w_hi", "w_ok", "mm", "g_ok", "m_ok", "chain"))
        block = ctx.enter_context(nc.Block())
        src = [K["yh"][:, c, :] for c in range(NH)] + [K["ya"][:, c, :] for c in range(NY - NH)]

        @block.sync
        def _(sp):
            with sp.Fori(0, KT // 2) as i:
                for s in range(2):
                    n = 2 * i + s
                    sp.wait_ge(w_ok, n + 1)
                    sp.dma_start(w[:, s, 0:NH, :], T["w_bh"][bass.ds(n, 1)][0]).then_inc(w_in[s], 16)
                    sp.dma_start(w[:, s, NH:NY, :], T["w_ba"][bass.ds(n, 1)][0]).then_inc(w_in[s], 16)
                    sp.wait_ge(m_ok, n + 1)
                    sp.dma_start(gate[:, s, 0, :], S["cm"][bass.ds(HY_TILES + n, 1)][0]).then_inc(g_in[s], 16)
                    sp.dma_start(gate[:, s, 1, :], S["cm"][bass.ds(HY_TILES + KT + n, 1)][0]).then_inc(g_in[s], 16)

        @block.gpsimd
        def _(pool):
            pool.sem_inc(w_ok, 2)
            with pool.Fori(0, KT // 2) as i:
                for s in range(2):
                    pool.wait_ge(w_hi, 2 * i + s + 1)
                    nc.gpsimd.tensor_tensor(w_l[:, s, :, :], w[:, s, :, :], w_h[:, s, :, :].bitcast(F32),
                                            ALU.subtract).then_inc(w_ok, 1)

        @block.tensor
        def _(pe):
            pe.sem_inc(mm, 4)
            pe.wait_ge(y_lo, NY)
            with pe.Fori(0, KT // 2) as i:
                for s in range(2):
                    n = 2 * i + s
                    pe.wait_ge(w_ok, n + 3)
                    pe.wait_ge(m_ok, n + 1)
                    for a, (lo, hi) in enumerate(((0, NH), (NH, NY))):
                        for h in range(2):
                            cut = slice(h * HALF, (h + 1) * HALF)
                            for c in range(lo, hi):
                                last = product3(nc, ps[:, 4 * s + 2 * a + h, :], (w_h[:, s, c, :], w_l[:, s, c, :]),
                                                (y_h[:, c, cut], y_l[:, c, cut]), c == lo, c == hi - 1)
                        last.then_inc(mm, 1)

        @block.scalar
        def _(act):
            for c in range(NY):
                nc.scalar.activation(y_h[:, c, :], src[c], ACT.Copy).then_inc(y_hi, 1)
            with act.Fori(0, KT // 2) as i:
                for s in range(2):
                    n = 2 * i + s
                    act.wait_ge(w_in[s], 32 * (i + 1))
                    act.wait_ge(mm, 2 * n + 2)
                    nc.scalar.activation(w_h[:, s, :, :], w[:, s, :, :], ACT.Copy).then_inc(w_hi, 1)
                    act.wait_ge(g_in[s], 32 * (i + 1))
                    nc.scalar.activation(gate[:, s, :, :], gate[:, s, :, :], ACT.Sigmoid).then_inc(g_ok, 1)

        @block.vector
        def _(dve):
            v = nc.vector
            ch = Chain(dve, chain_s)
            dve.sem_inc(m_ok, 2)
            for c in range(NY):
                dve.wait_ge(y_hi, c + 1)
                v.tensor_tensor(y_l[:, c, :], src[c], y_h[:, c, :].bitcast(F32), ALU.subtract).then_inc(y_lo, 1)
            with dve.Fori(0, KT // 2) as i:
                ch.loop(i, 2 * 3)
                for s in range(2):
                    n = 2 * i + s
                    dve.wait_ge(g_ok, n + 1)
                    for a in range(2):
                        dve.wait_ge(mm, 2 * n + 5 + a)
                        ch.link(v.tensor_tensor(tmp[:, a, :], ps[:, 4 * s + 2 * a:4 * s + 2 * a + 2, :].rearrange("p a b -> p (a b)"),
                                                gate[:, s, a, :], ALU.mult))
                    ch.link(v.tensor_tensor(K["merged"][:, bass.ds(n, 1), :][:, 0, :], tmp[:, 0, :], tmp[:, 1, :], ALU.add))
                    v.sem_inc(m_ok, 1)
            ch.done(KT // 2)


def layer_norm(nc, ch, K, sq, norm, row, stats, gain, base):
    v = nc.vector
    for h in range(2):
        v.bn_stats(stats[:, 6 * h:6 * h + 6], row[:, h * HALF:(h + 1) * HALF]).then_inc(ch.sem, 1)
        ch.n += 1
    hold(ch.eng, K, ch.sem, ch.base + ch.n)
    v.bn_aggr(stats[:, 12:14], stats[:, 0:12]).then_inc(ch.sem, 1)
    ch.n += 1
    ch.eng.wait_ge(ch.sem, ch.base + ch.n)
    v.tensor_scalar(stats[:, 13:14], stats[:, 13:14], EPS, None, ALU.add).then_inc(sq, 1)
    ch.eng.wait_ge(*norm)
    ch.link(v.reciprocal(stats[:, 15:16], stats[:, 14:15]))
    ch.link(v.scalar_tensor_tensor(out=row, in0=row, scalar=stats[:, 12:13], in1=gain, op0=ALU.subtract, op1=ALU.mult))
    return v.scalar_tensor_tensor(out=row, in0=row, scalar=stats[:, 15:16], in1=base, op0=ALU.mult, op1=ALU.add)


def stage_out(nc, S, K, T):
    ctx = ExitStack()
    with ctx:
        sb = lambda n, s, d=F32: ctx.enter_context(nc.sbuf_tensor("ou_" + n, s, d))
        sem = cleared_sems(nc, ctx, "ou_")
        raw = sb("raw", [P, 2, D])
        w_h, w_l = sb("w_h", [P, KT, D], F32R), sb("w_l", [P, KT, D], F32R)
        m_h, m_l = sb("m_h", [P, 2, KT, P], F32R), sb("m_l", [P, 2, KT, P], F32R)
        ln = sb("ln", [P, 2, D])
        x, row = sb("x", [P, 2, D]), sb("row", [P, 2, D])
        stats = sb("stats", [P, 16])
        ps = ctx.enter_context(nc.psum_tensor("ou_ps", [P, 4, HALF], F32))
        tps = ctx.enter_context(nc.psum_tensor("ou_tps", [P, 4, HALF], F32))
        raw_in = [sem(f"raw_in{k}") for k in range(2)]
        x_in = [sem(f"x_in{k}") for k in range(2)]
        stored = [sem(f"stored{k}") for k in range(2)]
        ln_in, w_hi, w_lo, m_hi, m_lo, mm, chain_s = (sem(n) for n in ("ln_in", "w_hi", "w_lo", "m_hi", "m_lo", "mm", "chain"))
        x_used, var_ok, root_ok, row_ok, turned, u_ok = (sem(n) for n in ("x_used", "var_ok", "root_ok", "row_ok", "turned", "u_ok"))
        block = ctx.enter_context(nc.Block())

        @block.sync
        def _(sp):
            for k in range(KT):
                if k >= 2:
                    sp.wait_ge(w_lo, k - 1)
                sp.dma_start(raw[:, k % 2, :], T["w_out"][:, k, :]).then_inc(raw_in[k % 2], 16)
            sp.dma_start(ln[:, :, :], T["ln"][0:2, :].partition_broadcast(P)).then_inc(ln_in, 16)
            with sp.Fori(0, KT // 2) as i:
                for s in range(2):
                    n = 2 * i + s
                    sp.wait_ge(x_used, n + 1)
                    sp.dma_start(x[:, s, :], T["x"].rearrange("(a p) n -> a p n", p=P)[bass.ds(n, 1)][0]).then_inc(x_in[s], 16)

        @block.gpsimd
        def _(pool):
            with pool.Fori(0, KT // 2) as i:
                for s in range(2):
                    n = 2 * i + s
                    pool.wait_ge(m_hi, n + 1)
                    nc.gpsimd.tensor_tensor(m_l[:, s, :, :], K["merged"][:, :, bass.ds(n * P, P)], m_h[:, s, :, :].bitcast(F32),
                                            ALU.subtract).then_inc(m_lo, 1)

        @block.tensor
        def _(pe):
            pe.sem_inc(mm, 2)

            def turn(s, n):
                hold(pe, K, row_ok, n + 1)
                hold(pe, K, u_ok, n + 1)
                for k in range(KT):
                    last = nc.tensor.transpose(tps[:, 2 * s + k // 4, (k % 4) * P:(k % 4 + 1) * P],
                                               row[:, s, k * P:(k + 1) * P], K["ident"][:, :])
                last.then_inc(turned, 1)

            pe.sem_inc(turned, 2)
            pe.wait_ge(w_lo, KT)
            with pe.Fori(0, KT // 2) as i:
                for s in range(2):
                    n = 2 * i + s
                    pe.wait_ge(m_lo, n + 1)
                    pe.wait_ge(x_used, n + 1)
                    for h in range(2):
                        for k in range(KT):
                            last = product3(nc, ps[:, 2 * s + h, :], (m_h[:, s, k, :], m_l[:, s, k, :]),
                                            (w_h[:, k, h * HALF:(h + 1) * HALF], w_l[:, k, h * HALF:(h + 1) * HALF]),
                                            k == 0, k == KT - 1)
                    last.then_inc(mm, 1)
                    if s == 1:
                        turn(0, 2 * i)
                turn(1, 2 * i + 1)

        @block.scalar
        def _(act):
            act.sem_inc(u_ok, 2)
            for s in range(2):
                act.sem_inc(stored[s], 16)

            def root_and_u2(s, n):
                act.wait_ge(var_ok, n + 1)
                nc.scalar.activation(stats[:, 14:15], stats[:, 13:14], ACT.Sqrt).then_inc(root_ok, 1)
                act.wait_ge(row_ok, n + 1)
                act.dma_start(S["x1"].rearrange("(a p) n -> a p n", p=P)[bass.ds(n, 1)][0], row[:, s, :]).then_inc(stored[s], 16)
                hold(act, K, turned, n + 3)
                for k in range(KT):
                    last = nc.scalar.activation(K["u2"][:, k, bass.ds(n * P, P)],
                                                tps[:, 2 * s + k // 4, (k % 4) * P:(k % 4 + 1) * P], ACT.Identity,
                                                bias=K["ada_col"][:, 2 * KT + k:2 * KT + k + 1],
                                                scale=K["ada_col"][:, 3 * KT + k:3 * KT + k + 1])
                last.then_inc(u_ok, 1)

            for k in range(KT):
                act.wait_ge(raw_in[k % 2], 16 * (k // 2 + 1))
                nc.scalar.activation(w_h[:, k, :], raw[:, k % 2, :], ACT.Copy).then_inc(w_hi, 1)
            with act.Fori(0, KT // 2) as i:
                for s in range(2):
                    n = 2 * i + s
                    act.wait_ge(mm, n + 1)
                    nc.scalar.activation(m_h[:, s, :, :], K["merged"][:, :, bass.ds(n * P, P)], ACT.Copy).then_inc(m_hi, 1)
                for s in range(2):
                    root_and_u2(s, 2 * i + s)
            for s in range(2):
                act.wait_ge(stored[s], 16 * (KT // 2 + 1))

        @block.vector
        def _(dve):
            v = nc.vector
            ch = Chain(dve, chain_s)
            dve.sem_inc(x_used, 2)
            for k in range(KT):
                dve.wait_ge(w_hi, k + 1)
                v.tensor_tensor(w_l[:, k, :], raw[:, k % 2, :], w_h[:, k, :].bitcast(F32), ALU.subtract).then_inc(w_lo, 1)
            dve.wait_ge(ln_in, 16)
            with dve.Fori(0, KT // 2) as i:
                ch.loop(i, 2 * 7)
                for s in range(2):
                    n = 2 * i + s
                    r = row[:, s, :]
                    dve.wait_ge(mm, n + 3)
                    dve.wait_ge(turned, n + 1)
                    dve.wait_ge(stored[s], 16 * (i + 1))
                    ch.link(v.tensor_tensor(r, ps[:, 2 * s:2 * s + 2, :].rearrange("p a b -> p (a b)"),
                                            K["ada_row"][:, 0:2, :].rearrange("p a b -> p (a b)"), ALU.mult))
                    dve.wait_ge(x_in[s], 16 * (i + 1))
                    ch.link(v.scalar_tensor_tensor(out=r, in0=x[:, s, :], scalar=ALPHA, in1=r, op0=ALU.mult, op1=ALU.add))
                    v.sem_inc(x_used, 1)
                    layer_norm(nc, ch, K, var_ok, (root_ok, n + 1), r, stats, ln[:, 0, :], ln[:, 1, :]).then_inc(row_ok, 1)
            ch.done(KT // 2)


def stage_query(nc, S, K, T):
    ctx = ExitStack()
    with ctx:
        sb = lambda n, s, d=F32: ctx.enter_context(nc.sbuf_tensor("qu_" + n, s, d))
        sem = lambda n: ctx.enter_context(nc.semaphore("qu_" + n))
        HP = 2 * PH
        u_h, u_l = K["u_h"], K["u_l"]
        w = sb("w", [P, 2, KT, P])
        w_h, w_l = sb("w_h", [P, 2, KT, P], F32R), sb("w_l", [P, 2, KT, P], F32R)
        keys = sb("keys", [P, HP, NK])
        q = sb("q", [P, 2, SEQ])
        sc = sb("sc", [P, 2, KT, NK])
        qps = ctx.enter_context(nc.psum_tensor("qu_qps", [P, 4, HALF], F32))
        sps = ctx.enter_context(nc.psum_tensor("qu_sps", [P, 4, HALF], F32))
        w_in = [sem(f"w_in{k}") for k in range(2)]
        stored = [sem(f"stored{k}") for k in range(2)]
        keys_in, u_hi, u_lo, w_hi, w_ok, mm, q_act, q_dve, s_mm, s_act, s_dve = (sem(n) for n in (
            "keys_in", "u_hi", "u_lo", "w_hi", "w_ok", "mm", "q_act", "q_dve", "s_mm", "s_act", "s_dve"))
        block = ctx.enter_context(nc.Block())

        @block.sync
        def _(sp):
            sp.dma_start(keys[:, :, :], T["keysT"].rearrange("h e k -> e h k")).then_inc(keys_in, 16)
            with sp.Fori(0, HP // 2) as i:
                for s in range(2):
                    sp.wait_ge(w_ok, 2 * i + s + 1)
                    sp.dma_start(w[:, s, :, :], T["wq"][bass.ds(2 * i + s, 1)][0]).then_inc(w_in[s], 16)

        @block.gpsimd
        def _(pool):
            pool.sem_inc(w_ok, 2)
            with pool.Fori(0, HP // 2) as i:
                for s in range(2):
                    pool.wait_ge(w_hi, 2 * i + s + 1)
                    nc.gpsimd.tensor_tensor(w_l[:, s, :, :], w[:, s, :, :], w_h[:, s, :, :].bitcast(F32),
                                            ALU.subtract).then_inc(w_ok, 1)

        @block.tensor
        def _(pe):
            pe.sem_inc(mm, 4)
            pe.sem_inc(s_mm, 2)

            def project(s, n):
                hold(pe, K, w_ok, n + 3)
                hold(pe, K, q_act, n + 1)
                hold(pe, K, q_dve, n + 1)
                for h in range(2):
                    cut = slice(h * HALF, (h + 1) * HALF)
                    for k in range(KT):
                        last = product3(nc, qps[:, 2 * s + h, :], (w_h[:, s, k, :], w_l[:, s, k, :]),
                                        (u_h[:, k, cut], u_l[:, k, cut]), k == 0, k == KT - 1)
                    last.then_inc(mm, 1)

            def match(s, n):
                hold(pe, K, q_act, n + 3)
                hold(pe, K, q_dve, n + 3)
                hold(pe, K, s_act, n + 1)
                hold(pe, K, s_dve, n + 1)
                for tt in range(KT):
                    last = nc.tensor.matmul(sps[:, 2 * s + tt // 4, (tt % 4) * P:(tt % 4 + 1) * P],
                                            q[:, s, tt * P:(tt + 1) * P], keys[:, bass.ds(n, 1), :][:, 0, :],
                                            start=True, stop=True)
                last.then_inc(s_mm, 1)

            pe.wait_ge(keys_in, 16)
            pe.wait_ge(u_lo, KT)
            with pe.Fori(0, HP // 2) as i:
                project(0, 2 * i)
                project(1, 2 * i + 1)
                match(0, 2 * i)
                match(1, 2 * i + 1)

        @block.scalar
        def _(act):
            act.sem_inc(q_act, 2)
            act.sem_inc(s_act, 2)
            for s in range(2):
                act.sem_inc(stored[s], 16)
            for k in range(KT):
                nc.scalar.activation(u_h[:, k, :], K["u2"][:, k, :], ACT.Copy).then_inc(u_hi, 1)

            def high(s, n, i):
                act.wait_ge(w_in[s], 16 * (i + 1))
                act.wait_ge(mm, 2 * n + 2)
                nc.scalar.activation(w_h[:, s, :, :], w[:, s, :, :], ACT.Copy).then_inc(w_hi, 1)

            with act.Fori(0, HP // 2) as i:
                for s in range(2):
                    high(s, 2 * i + s, i)
                for s in range(2):
                    n = 2 * i + s
                    act.wait_ge(mm, 2 * n + 5)
                    act.wait_ge(s_mm, n + 1)
                    nc.scalar.activation(q[:, s, 0:HALF], qps[:, 2 * s, :], ACT.Copy).then_inc(q_act, 1)
                for s in range(2):
                    n = 2 * i + s
                    hold(act, K, s_mm, n + 3)
                    act.wait_ge(stored[s], 16 * (i + 1))
                    nc.scalar.activation(sc[:, s, 0:4, :], sps[:, 2 * s, :].rearrange("p (a k) -> p a k", k=NK),
                                         ACT.Copy).then_inc(s_act, 1)
                    act.wait_ge(s_act, n + 3)
                    act.wait_ge(s_dve, n + 3)
                    act.dma_start(S["scores"].rearrange("a p h k -> p a h k")[:, :, bass.ds(n, 1), :][:, :, 0, :],
                                  sc[:, s, :, :]).then_inc(stored[s], 16)
            for s in range(2):
                act.wait_ge(stored[s], 16 * (HP // 2 + 1))

        @block.vector
        def _(dve):
            v = nc.vector
            dve.sem_inc(q_dve, 2)
            dve.sem_inc(s_dve, 2)
            for k in range(KT):
                dve.wait_ge(u_hi, k + 1)
                v.tensor_tensor(u_l[:, k, :], K["u2"][:, k, :], u_h[:, k, :].bitcast(F32), ALU.subtract).then_inc(u_lo, 1)
            with dve.Fori(0, HP // 2) as i:
                for s in range(2):
                    n = 2 * i + s
                    dve.wait_ge(mm, 2 * n + 6)
                    dve.wait_ge(s_mm, n + 1)
                    v.tensor_copy(q[:, s, HALF:SEQ], qps[:, 2 * s + 1, :]).then_inc(q_dve, 1)
                for s in range(2):
                    n = 2 * i + s
                    hold(dve, K, s_mm, n + 3)
                    dve.wait_ge(stored[s], 16 * (i + 1))
                    v.tensor_copy(sc[:, s, 4:8, :], sps[:, 2 * s + 1, :].rearrange("p (a k) -> p a k", k=NK)).then_inc(s_dve, 1)


PICKS = PH * TOPK
AT = 5
FIRST = AT * KT
BESIDE = NK // 2
AHEAD = FIRST + BESIDE


def stage_select(nc, S, K, T):
    ctx = ExitStack()
    with ctx:
        sb = lambda n, s, d=F32: ctx.enter_context(nc.sbuf_tensor("se_" + n, s, d))
        sem = lambda n: ctx.enter_context(nc.semaphore("se_" + n))
        HP = 2 * PH
        sc, sc2 = sb("sc", [P, 2, HP, NK]), sb("sc2", [P, HP, NK])
        kv, ki, kf = sb("kv", [P, HP, TOPK]), sb("ki", [P, HP, TOPK], U32), sb("kf", [P, HP, TOPK])
        big = K["big"]
        sums16 = lambda x: x.rearrange("p a (b c d) -> p (a b) c d", c=TOPK, d=TOPK)
        cand, cand2 = sums16(big[:, 0:2, :]), sums16(big[:, 2:4, :])
        cv, ci = sb("cv", [P, PH, TOPK]), sb("ci", [P, PH, TOPK], U32)
        ab_i, ab = sb("ab_i", [P, 2, PICKS], U32), sb("ab", [P, 2, PICKS])
        iota = sb("iota", [P, TOPK])
        hit = big[:, 4:8, :].rearrange("p (a x) (b c) -> p a (x b) c", a=2, c=TOPK)
        e, tot = sb("e", [P, PH, TOPK]), sb("tot", [P, 2, PH])
        sel = sb("sel", [P, 2, 3, PICKS])
        u_h, u_l = K["u_h"], K["u_l"]
        ut = sb("ut", [P, 2, KT, P])
        ut_h, ut_l = sb("ut_h", [P, 2, KT, P], F32R), sb("ut_l", [P, 2, KT, P], F32R)
        gelu_a = sb("gelu_a", [P, 2, SEQ])
        aps = ctx.enter_context(nc.psum_tensor("se_aps", [P, 4, HALF], F32))
        tps = ctx.enter_context(nc.psum_tensor("se_tps", [P, 3 * P], F32))
        sc_in = [sem(f"sc_in{k}") for k in range(2)]
        small, chain_s, e_in, e_ok, sel_ok, t_mm, t_ok = (sem(n) for n in (
            "small", "chain", "e_in", "e_ok", "sel_ok", "t_mm", "t_ok"))
        sc_used, ut_hi, ut_ok, a_mm, gelu_ok = (sem(n) for n in ("sc_used", "ut_hi", "ut_ok", "a_mm", "gelu_ok"))
        ut_in = [sem(f"ut_in{k}") for k in range(2)]
        act_stored = [sem(f"act_stored{k}") for k in range(2)]
        block = ctx.enter_context(nc.Block())

        @block.sync
        def _(sp):
            sp.dma_start(iota[:, :], T["iota"][0:TOPK].partition_broadcast(P)).then_inc(small, 16)
            with sp.Fori(0, KT // 2) as i:
                for s in range(2):
                    sp.wait_ge(sc_used, 2 * i + s + 1)
                    sp.dma_start(sc[:, s, :, :], S["scores"][bass.ds(2 * i + s, 1)][0]).then_inc(sc_in[s], 16)
                    for c in range(AT * s, AT * s + AT):
                        sp.wait_ge(ut_ok, 2 * AT * i + c + 1)
                        sp.dma_start(ut[:, c % 2, :, :], T["utab"][bass.ds(2 * AT * i + c, 1)][0]).then_inc(ut_in[c % 2], 16)
            sp.wait_ge(ut_ok, AT * KT + 1)
            sp.dma_start(ut[:, 0, :, :], T["utab"][AT * KT]).then_inc(ut_in[0], 16)

        @block.gpsimd
        def _(pool):
            pool.sem_inc(ut_ok, 2)

            def low(s, n):
                pool.wait_ge(ut_hi, n + 1)
                nc.gpsimd.tensor_tensor(ut_l[:, s, :, :], ut[:, s, :, :], ut_h[:, s, :, :].bitcast(F32),
                                        ALU.subtract).then_inc(ut_ok, 1)

            with pool.Fori(0, AT * KT // 2) as i:
                for s in range(2):
                    low(s, 2 * i + s)
            low(0, AT * KT)

        @block.tensor
        def _(pe):
            pe.sem_inc(a_mm, 4)
            with pe.Fori(0, KT // 2) as i:
                for s in range(2):
                    for c in range(AT * s, AT * s + AT):
                        a = 2 * AT * i + c
                        pe.wait_ge(ut_ok, a + 3)
                        for h in range(2):
                            pe.wait_ge(gelu_ok, 2 * a + h + 1)
                            cut = slice(h * HALF, (h + 1) * HALF)
                            for k in range(KT):
                                last = product3(nc, aps[:, 2 * (c % 2) + h, :], (ut_h[:, c % 2, k, :], ut_l[:, c % 2, k, :]),
                                                (u_h[:, k, cut], u_l[:, k, cut]), k == 0, k == KT - 1)
                            last.then_inc(a_mm, 1)
                    n = 2 * i + s
                    hold(pe, K, sel_ok, n + 1)
                    hold(pe, K, t_ok, n + 2)
                    for a in range(3):
                        last = nc.tensor.transpose(tps[:, a * P:(a + 1) * P], sel[:, s, a, :], K["ident"][:, :])
                    last.then_inc(t_mm, 1)

        @block.scalar
        def _(act):
            act.sem_inc(t_ok, 2)
            act.sem_inc(gelu_ok, 4)
            for s in range(2):
                act.sem_inc(act_stored[s], 16)

            def split(s, a, count):
                act.wait_ge(ut_in[s], 16 * (count + 1))
                act.wait_ge(a_mm, 2 * a + 2)
                nc.scalar.activation(ut_h[:, s, :, :], ut[:, s, :, :], ACT.Copy).then_inc(ut_hi, 1)

            split(0, 0, 0)
            with act.Fori(0, KT // 2) as i:
                for s in range(2):
                    n = 2 * i + s
                    for j in range(AT):
                        c = AT * s + j
                        a, slot = 2 * AT * i + c, c % 2
                        split(1 - slot, a + 1, AT * i + (c + 1) // 2)
                        act.wait_ge(act_stored[slot], 16 * (AT * i + c // 2 + 1))
                        for h in range(2):
                            act.wait_ge(a_mm, 2 * a + h + 5)
                            nc.scalar.activation(gelu_a[:, slot, h * HALF:(h + 1) * HALF], aps[:, 2 * slot + h, :],
                                                 ACT.Gelu).then_inc(gelu_ok, 1)
                        act.wait_ge(gelu_ok, 2 * a + 6)
                        act.dma_start(S["ahead"][bass.ds(a, 1)][0], gelu_a[:, slot, :]).then_inc(act_stored[slot], 16)
                        if j == AT - 2:
                            act.wait_ge(e_in, n + 1)
                            nc.scalar.activation(e[:, :, :], e[:, :, :], ACT.Exp).then_inc(e_ok, 1)
                    hold(act, K, t_mm, n + 1)
                    nc.scalar.activation(K["sel"][:, :, bass.ds(n * P, P)],
                                         tps[:, :].rearrange("p (a t) -> p a t", t=P), ACT.Copy).then_inc(t_ok, 1)
            for s in range(2):
                act.wait_ge(act_stored[s], 16 * (AT * KT // 2 + 1))

        @block.vector
        def _(dve):
            v = nc.vector
            ch = Chain(dve, chain_s)
            dve.sem_inc(sc_used, 2)

            def top16(src, spare, vals, idx, rows):
                for r in range(rows):
                    last = v.max(vals(r, 0), src(r))
                ch.link(last, K)
                for r in range(rows):
                    v.max_index(idx(r, 0), vals(r, 0), src(r))
                    last = v.match_replace(spare(r), vals(r, 0), src(r), -3.0e38)
                ch.link(last, K)
                for r in range(rows):
                    last = v.max(vals(r, 1), spare(r))
                ch.link(last, K)
                for r in range(rows):
                    last = v.max_index(idx(r, 1), vals(r, 1), spare(r))
                ch.link(last, K)

            dve.wait_ge(small, 16)
            with dve.Fori(0, KT // 2) as i:
                ch.loop(i, 2 * 21)
                for s in range(2):
                    n = 2 * i + s
                    hold(dve, K, sc_in[s], 16 * (i + 1))
                    part = lambda t, r, a: t[:, r, 8 * a:8 * a + 8]
                    top16(lambda r: sc[:, s, r, :], lambda r: sc2[:, r, :], lambda r, a: part(kv, r, a),
                          lambda r, a: part(ki, r, a), HP)
                    v.sem_inc(sc_used, 1)
                    ch.link(v.tensor_copy(kf[:, :, :], ki[:, :, :]))
                    halves = lambda t: (t[:, :, :].rearrange("p (h two) k -> p h two k", two=2)[:, :, 0, :],
                                        t[:, :, :].rearrange("p (h two) k -> p h two k", two=2)[:, :, 1, :])
                    v0, v1 = halves(kv)
                    wide = [P, PH, TOPK, TOPK]
                    ch.link(v.tensor_tensor(cand[:, :, :, :], v0.unsqueeze(3).to_broadcast(wide),
                                            v1.unsqueeze(2).to_broadcast(wide), ALU.add), K)
                    flat = lambda t, r: t[:, r, :, :].rearrange("p a b -> p (a b)")
                    top16(lambda r: flat(cand, r), lambda r: flat(cand2, r), lambda r, a: part(cv, r, a),
                          lambda r, a: part(ci, r, a), PH)
                    first = cv[:, :, 0:1].to_broadcast([P, PH, TOPK])
                    v.tensor_tensor(e[:, :, :], cv[:, :, :], first, ALU.subtract).then_inc(e_in, 1)
                    cif = ci[:, :, :].rearrange("p h k -> p (h k)")
                    v.tensor_scalar(ab_i[:, 0, :], cif, 4, None, ALU.logical_shift_right)
                    ch.link(v.tensor_scalar(ab_i[:, 1, :], cif, 15, None, ALU.bitwise_and))
                    ch.link(v.tensor_copy(ab[:, :, :], ab_i[:, :, :]))
                    for a in range(2):
                        ch.link(v.tensor_tensor(hit[:, a, :, :], ab[:, a, :].unsqueeze(2).to_broadcast([P, PICKS, TOPK]),
                                                iota[:, :].unsqueeze(1).to_broadcast([P, PICKS, TOPK]), ALU.is_equal))
                    for a in range(2):
                        h4 = hit[:, a, :, :].rearrange("p (h k) j -> p h k j", h=PH)
                        ch.link(v.tensor_tensor(h4, h4, halves(kf)[a].unsqueeze(2).to_broadcast(wide), ALU.mult))
                    dve.wait_ge(t_ok, n + 1)
                    for a in range(2):
                        ch.link(v.tensor_reduce(sel[:, s, a, :], hit[:, a, :, :], AX, ALU.add))
                    dve.wait_ge(e_ok, n + 1)
                    ch.link(v.tensor_reduce(tot[:, 0, :], e[:, :, :], AX, ALU.add))
                    ch.link(v.reciprocal(tot[:, 1, :], tot[:, 0, :]))
                    ch.link(v.tensor_tensor(sel[:, s, 2, :].rearrange("p (h k) -> p h k", h=PH), e[:, :, :],
                                            tot[:, 1, :].unsqueeze(2).to_broadcast([P, PH, TOPK]), ALU.mult))
                    v.sem_inc(sel_ok, 1)
            ch.done(KT // 2)


GATE_SCALE = 2.0 ** 15


def stage_gates(nc, S, K, T):
    ctx = ExitStack()
    with ctx:
        sb = lambda n, s, d=F32: ctx.enter_context(nc.sbuf_tensor("ga_" + n, s, d))
        sem = lambda n: ctx.enter_context(nc.semaphore("ga_" + n))
        G = 4
        iota32 = sb("iota32", [P, NK])
        iota = sb("iota", [P, NK], F16)
        gh16 = sb("gh16", [P, SEQ], F16)
        gs = sb("gs", [P, 2, SEQ])
        first = sb("first", [P, 2, 2, G, NK], F16)
        second = sb("second", [P, 2, G, NK], F16)
        TW = P // 2
        wide = [sb("wide", [P, NK, TW])[:, :, :], K["big"][:, :, :].rearrange("p a (b t) -> p (a b) t", t=TW)]
        u_h, u_l = K["u_h"], K["u_l"]
        ut = sb("ut", [P, 2, KT, P])
        ut_h, ut_l = sb("ut_h", [P, 2, KT, P], F32R), sb("ut_l", [P, 2, KT, P], F32R)
        gelu_a = sb("gelu_a", [P, 2, SEQ])
        ps = ctx.enter_context(nc.psum_tensor("ga_ps", [P, 4, HALF], F32))
        aps = ctx.enter_context(nc.psum_tensor("ga_aps", [P, 4, HALF], F32))
        small, chain_s, f_ok, mm, act_out = (sem(n) for n in ("small", "chain", "f_ok", "mm", "act_out"))
        ut_hi, ut_ok, a_mm, gelu_ok = (sem(n) for n in ("ut_hi", "ut_ok", "a_mm", "gelu_ok"))
        stored = [sem(f"stored{k}") for k in range(2)]
        ut_in = [sem(f"ut_in{k}") for k in range(2)]
        act_stored = [sem(f"act_stored{k}") for k in range(2)]
        block = ctx.enter_context(nc.Block())
        GROUPS = P // G
        SG = TW // G
        assert KT * GROUPS == 4 * BESIDE

        @block.sync
        def _(sp):
            sp.dma_start(iota32[:, :], T["iota"][0:NK].partition_broadcast(P)).then_inc(small, 16)

            def load(s, n):
                sp.wait_ge(ut_ok, n + 1)
                sp.dma_start(ut[:, s, :, :], T["utab"][bass.ds(n + FIRST, 1)][0]).then_inc(ut_in[s], 16)

            with sp.Fori(0, BESIDE // 2) as i:
                for s in range(2):
                    load(s, 2 * i + s)
            load(0, BESIDE)

        @block.gpsimd
        def _(pool):
            pool.sem_inc(ut_ok, 2)

            def low(s, n):
                pool.wait_ge(ut_hi, n + 1)
                nc.gpsimd.tensor_tensor(ut_l[:, s, :, :], ut[:, s, :, :], ut_h[:, s, :, :].bitcast(F32),
                                        ALU.subtract).then_inc(ut_ok, 1)

            with pool.Fori(0, BESIDE // 2) as i:
                for s in range(2):
                    low(s, 2 * i + s)
            low(0, BESIDE)

        @block.tensor
        def _(pe):
            pe.sem_inc(mm, 2)
            pe.sem_inc(a_mm, 4)
            with pe.Fori(0, BESIDE // 2) as q:
                for s in range(2):
                    n = 2 * q + s
                    for b in range(4):
                        m = 4 * n + b
                        pe.wait_ge(f_ok, m + 1)
                        pe.wait_ge(act_out, m + 1)
                        for t in range(G):
                            for part in range(2):
                                last = nc.tensor.matmul(ps[:, b, t * NK:(t + 1) * NK], second[:, b % 2, t, :],
                                                        first[:, b % 2, part, t, :], start=part == 0, stop=part == 1)
                        last.then_inc(mm, 1)
                        if b == 0:
                            pe.wait_ge(ut_ok, n + 3)
                        h = b // 2
                        if b % 2 == 0:
                            pe.wait_ge(gelu_ok, 2 * n + h + 1)
                        cut = slice(h * HALF, (h + 1) * HALF)
                        for k in range(KT // 2 * (b % 2), KT // 2 * (b % 2 + 1)):
                            last = product3(nc, aps[:, 2 * s + h, :], (ut_h[:, s, k, :], ut_l[:, s, k, :]),
                                            (u_h[:, k, cut], u_l[:, k, cut]), k == 0, k == KT - 1)
                        if b % 2 == 1:
                            last.then_inc(a_mm, 1)

        @block.scalar
        def _(act):
            act.sem_inc(act_out, 4)
            act.sem_inc(gelu_ok, 4)
            for s in range(2):
                act.sem_inc(stored[s], 16)
                act.sem_inc(act_stored[s], 16)

            def split(s, n, i):
                act.wait_ge(ut_in[s], 16 * (i + 1))
                act.wait_ge(a_mm, 2 * n + 2)
                nc.scalar.activation(ut_h[:, s, :, :], ut[:, s, :, :], ACT.Copy).then_inc(ut_hi, 1)

            def scatter_out(s, g, m, b):
                hold(act, K, mm, m + 3)
                nc.scalar.activation(wide[s][:, :, bass.ds((8 * g + b) * G, G)],
                                     ps[:, b % 4, :].rearrange("p (t i) -> p i t", i=NK), ACT.Copy,
                                     scale=1.0 / GATE_SCALE).then_inc(act_out, 1)

            def gelu(a, n, h):
                act.wait_ge(a_mm, 2 * n + h + 5)
                nc.scalar.activation(gelu_a[:, a, h * HALF:(h + 1) * HALF], aps[:, 2 * a + h, :], ACT.Gelu).then_inc(gelu_ok, 1)

            split(0, 0, 0)
            def tile(i, last):
                for s in range(2):
                    hold(act, K, stored[s], 16 * (i + 1))
                    with act.Fori(0, SG // 8) as g:
                        for a in range(2):
                            q = i * 4 + s * 2 + g
                            n = 2 * q + a
                            split(1 - a, n + 1, q + a)
                            m = 4 * n
                            for b in range(3):
                                scatter_out(s, g, m + b, 4 * a + b)
                            act.wait_ge(act_stored[a], 16 * (q + 1))
                            gelu(a, n, 0)
                            scatter_out(s, g, m + 3, 4 * a + 3)
                            gelu(a, n, 1)
                            act.wait_ge(gelu_ok, 2 * n + 6)
                            act.dma_start(S["ahead"][bass.ds(n + FIRST, 1)][0], gelu_a[:, a, :]).then_inc(act_stored[a], 16)
                    act.wait_ge(act_out, (2 * i + s + 1) * SG + 4)
                    act.dma_start(S["gates"].rearrange("i j t -> j i t")[:, :, bass.ds(i * P + s * TW, TW)],
                                  wide[s]).then_inc(stored[s] if s == 0 or not last else K["last_gates"], 16)

            with act.Fori(0, KT - 1) as i:
                tile(i, False)
            tile(KT - 1, True)
            act.wait_ge(stored[0], 16 * (KT + 1))
            for s in range(2):
                act.wait_ge(act_stored[s], 16 * (BESIDE // 2 + 1))

        @block.vector
        def _(dve):
            v = nc.vector
            ch = Chain(dve, chain_s)
            dve.wait_ge(small, 16)
            w = K["sel"][:, 2, :]
            ch.link(v.tensor_copy(iota[:, :], iota32[:, :]))
            ch.link(v.tensor_scalar(gs[:, 1, :], w, GATE_SCALE, None, ALU.mult))
            ch.link(v.tensor_copy(gh16[:, :], gs[:, 1, :]))
            ch.link(v.tensor_copy(gs[:, 0, :], gh16[:, :]))
            ch.link(v.tensor_tensor(gs[:, 1, :], gs[:, 1, :], gs[:, 0, :], ALU.subtract))
            with dve.Fori(0, KT * GROUPS // 4) as g:
                for b in range(4):
                    m = 4 * g + b
                    dve.wait_ge(mm, m + 1)
                    for t in range(G):
                        at = bass.ds(m * G + t, 1)
                        v.tensor_scalar(second[:, b % 2, t, :], iota[:, :], K["sel"][:, 1, at], None, ALU.is_equal)
                        for part in range(2):
                            last = v.tensor_scalar(first[:, b % 2, part, t, :], iota[:, :], K["sel"][:, 0, at],
                                                   gs[:, part, at], ALU.is_equal, ALU.mult)
                    last.then_inc(f_ok, 1)


def stage_experts(nc, S, K, T):
    ctx = ExitStack()
    with ctx:
        sb = lambda n, s, d=F32: ctx.enter_context(nc.sbuf_tensor("ex_" + n, s, d))
        sem = lambda n: ctx.enter_context(nc.semaphore("ex_" + n))
        sums = K["sums"]
        u_h, u_l = K["u_h"], K["u_l"]
        N = NK - AHEAD
        ut = sb("ut", [P, 2, KT, P])
        ut_h, ut_l = sb("ut_h", [P, 2, KT, P], F32R), sb("ut_l", [P, 2, KT, P], F32R)
        vt = sb("vt", [P, 2, D])
        vt_h, vt_l = sb("vt_h", [P, 2, D], F32R), sb("vt_l", [P, 2, D], F32R)
        wt = sb("wt", [P, 2, SEQ])
        act_a = sb("act_a", [P, 2, SEQ])
        c_h, c_l = sb("c_h", [P, 2, SEQ], F32R), sb("c_l", [P, 2, SEQ], F32R)
        aps = ctx.enter_context(nc.psum_tensor("ex_aps", [P, 4, HALF], F32))
        fps = ctx.enter_context(nc.psum_tensor("ex_fps", [P, 4, HALF], F32))
        pair = lambda n: [sem(f"{n}{k}") for k in range(2)]
        ut_in, vt_in, wt_in = pair("ut_in"), pair("vt_in"), pair("wt_in")
        ut_hi, ut_ok, vt_hi, vt_ok = (sem(n) for n in ("ut_hi", "ut_ok", "vt_hi", "vt_ok"))
        a_mm, gelu_ok, c_ok, c_hi, c_lo, f_mm, f_ok = (sem(n) for n in ("a_mm", "gelu_ok", "c_ok", "c_hi", "c_lo", "f_mm", "f_ok"))
        zeroed = sem("zeroed")
        LAST = N - 2
        HT = KT // 2
        half = lambda h: slice(h * HALF, (h + 1) * HALF)
        block = ctx.enter_context(nc.Block())

        @block.sync
        def _(sp):
            with sp.Fori(0, N // 2) as i:
                for s in range(2):
                    n = 2 * i + s
                    sp.wait_ge(ut_ok, n + 1)
                    sp.dma_start(ut[:, s, :, :], T["utab"][bass.ds(n + AHEAD, 1)][0]).then_inc(ut_in[s], 16)
                    sp.wait_ge(K["last_gates"], 16)
                    sp.wait_ge(c_lo, 2 * n + 2)
                    sp.dma_start(wt[:, s, :], S["gates"][bass.ds(n + AHEAD, 1)][0]).then_inc(wt_in[s], 16)
                    sp.wait_ge(vt_ok, n + 1)
                    sp.dma_start(vt[:, s, :], T["vtab"][bass.ds(n + AHEAD, 1)][0]).then_inc(vt_in[s], 16)

        @block.gpsimd
        def _(pool):
            pool.sem_inc(ut_ok, 2)
            pool.sem_inc(vt_ok, 2)
            with pool.Fori(0, N // 2) as i:
                for s in range(2):
                    n = 2 * i + s
                    pool.wait_ge(ut_hi, n + 1)
                    nc.gpsimd.tensor_tensor(ut_l[:, s, :, :], ut[:, s, :, :], ut_h[:, s, :, :].bitcast(F32),
                                            ALU.subtract).then_inc(ut_ok, 1)
                    pool.wait_ge(vt_hi, n + 1)
                    nc.gpsimd.tensor_tensor(vt_l[:, s, :], vt[:, s, :], vt_h[:, s, :].bitcast(F32),
                                            ALU.subtract).then_inc(vt_ok, 1)

        @block.tensor
        def _(pe):
            pe.sem_inc(a_mm, 4)
            pe.sem_inc(f_mm, 2 * KT)

            def activations(s, n, h):
                pe.wait_ge(ut_ok, n + 3)
                pe.wait_ge(gelu_ok, 2 * n + h + 1)
                for k in range(KT):
                    last = product3(nc, aps[:, 2 * s + h, :], (ut_h[:, s, k, :], ut_l[:, s, k, :]),
                                    (u_h[:, k, half(h)], u_l[:, k, half(h)]), k == 0, k == KT - 1)
                last.then_inc(a_mm, 1)

            def sums_of(s, n, h):
                pe.wait_ge(vt_ok, n + 3)
                pe.wait_ge(c_lo, 2 * n + h + 5)
                for tt in range(h * HT, (h + 1) * HT):
                    b = tt % 2
                    pe.wait_ge(f_ok, KT * n + tt + 1)
                    cut = slice(tt * P, (tt + 1) * P)
                    for dd in range(2):
                        last = product3(nc, fps[:, 2 * b + dd, :], (c_h[:, s, cut], c_l[:, s, cut]),
                                        (vt_h[:, s, half(dd)], vt_l[:, s, half(dd)]), True, True)
                    last.then_inc(f_mm, 1)

            for h in range(2):
                activations(0, 0, h)
            with pe.Fori(0, LAST // 2) as i:
                for s in range(2):
                    n = 2 * i + s
                    for h in range(2):
                        activations(1 - s, n + 1, h)
                        sums_of(s, n, h)
            for h in range(2):
                activations(1, N - 1, h)
                sums_of(0, N - 2, h)
            for h in range(2):
                sums_of(1, N - 1, h)

        @block.scalar
        def _(act):
            act.sem_inc(gelu_ok, 4)

            def split_tables(s, n, i):
                act.wait_ge(ut_in[s], 16 * (i + 1))
                act.wait_ge(a_mm, 2 * n + 2)
                nc.scalar.activation(ut_h[:, s, :, :], ut[:, s, :, :], ACT.Copy).then_inc(ut_hi, 1)

            def split_values(s, n, i):
                act.wait_ge(vt_in[s], 16 * (i + 1))
                act.wait_ge(f_mm, KT * n + KT)
                nc.scalar.activation(vt_h[:, s, :], vt[:, s, :], ACT.Copy).then_inc(vt_hi, 1)

            def gelu(s, n, h):
                act.wait_ge(a_mm, 2 * n + h + 5)
                act.wait_ge(c_lo, 2 * n + h + 1)
                nc.scalar.activation(act_a[:, s, half(h)], aps[:, 2 * s + h, :], ACT.Gelu).then_inc(gelu_ok, 1)

            def coef_high(s, n, h):
                act.wait_ge(c_ok, 2 * n + h + 1)
                act.wait_ge(f_mm, KT * n + HT * (h + 1))
                nc.scalar.activation(c_h[:, s, half(h)], act_a[:, s, half(h)], ACT.Copy).then_inc(c_hi, 1)

            split_tables(0, 0, 0)
            split_tables(1, 1, 0)
            split_values(0, 0, 0)
            for h in range(2):
                gelu(0, 0, h)
                coef_high(0, 0, h)
            with act.Fori(0, LAST // 2) as i:
                for s in range(2):
                    n = 2 * i + s
                    o = 1 - s
                    split_tables(s, n + 2, i + 1)
                    gelu(o, n + 1, 0)
                    coef_high(o, n + 1, 0)
                    split_values(o, n + 1, i + s)
                    gelu(o, n + 1, 1)
                    coef_high(o, n + 1, 1)
            gelu(1, N - 1, 0)
            coef_high(1, N - 1, 0)
            split_values(1, N - 1, N // 2 - 1)
            gelu(1, N - 1, 1)
            coef_high(1, N - 1, 1)

        @block.vector
        def _(dve):
            v = nc.vector
            dve.sem_inc(c_lo, 4)
            dve.sem_inc(f_ok, 2)
            def coefficients(s, n, i, h):
                dve.wait_ge(gelu_ok, 2 * n + h + 5)
                dve.wait_ge(wt_in[s], 16 * (i + 1))
                a = act_a[:, s, half(h)]
                v.tensor_tensor(a, a, wt[:, s, half(h)], ALU.mult).then_inc(c_ok, 1)

            def coef_low(s, n, h):
                dve.wait_ge(c_hi, 2 * n + h + 1)
                v.tensor_tensor(c_l[:, s, half(h)], act_a[:, s, half(h)], c_h[:, s, half(h)].bitcast(F32),
                                ALU.subtract).then_inc(c_lo, 1)

            def add_sums(n, tt):
                b = tt % 2
                hold(dve, K, f_mm, KT * n + tt + 1 + 2 * KT)
                row = sums[:, tt, :]
                v.tensor_tensor(row, row, fps[:, 2 * b:2 * b + 2, :].rearrange("p a b -> p (a b)"), ALU.add).then_inc(f_ok, 1)

            def turn(s, n, i):
                for h in range(2):
                    coefficients(1 - s, n + 1, i + s, h)
                    add_sums(n, HT * h)
                    add_sums(n, HT * h + 1)
                    add_sums(n, HT * h + 2)
                    coef_low(1 - s, n + 1, h)
                    add_sums(n, HT * h + 3)

            for h in range(2):
                coefficients(0, 0, 0, h)
                coef_low(0, 0, h)
            dve.wait_ge(K["last_gates"], 16)
            v.memset(sums[:, :, :], 0.0).then_inc(zeroed, 1)
            dve.wait_ge(zeroed, 1)
            with dve.Fori(0, LAST // 2) as i:
                for s in range(2):
                    turn(s, 2 * i + s, i)
            turn(0, N - 2, N // 2 - 1)
            for tt in range(KT):
                add_sums(N - 1, tt)


def stage_values(nc, S, K, T):
    ctx = ExitStack()
    with ctx:
        sb = lambda n, s, d=F32: ctx.enter_context(nc.sbuf_tensor("va_" + n, s, d))
        sem = lambda n: ctx.enter_context(nc.semaphore("va_" + n))
        sums = K["sums"]
        GT = 4
        NG = AHEAD // GT
        vt, wt, c = sb("vt", [P, 2, D]), sb("wt", [P, 2, SEQ]), sb("c", [P, 2, SEQ])
        vt_h, vt_l = sb("vt_h", [P, 2, GT, D], F32R), sb("vt_l", [P, 2, GT, D], F32R)
        c_h, c_l = sb("c_h", [P, 2, GT, SEQ], F32R), sb("c_l", [P, 2, GT, SEQ], F32R)
        fps = ctx.enter_context(nc.psum_tensor("va_fps", [P, 8, HALF], F32))
        BP = 4
        pair = lambda n: [sem(f"{n}{k}") for k in range(2)]
        c_in, wt_in, vt_in = pair("c_in"), pair("wt_in"), pair("vt_in")
        vt_hi, vt_ok, c_ok, c_hi, c_lo, f_mm, f_ok = (sem(n) for n in ("vt_hi", "vt_ok", "c_ok", "c_hi", "c_lo", "f_mm", "f_ok"))
        block = ctx.enter_context(nc.Block())

        @block.sync
        def _(sp):
            with sp.Fori(0, AHEAD // 2) as i:
                for s in range(2):
                    n = 2 * i + s
                    sp.wait_ge(c_lo, n + 1)
                    sp.dma_start(c[:, s, :], S["ahead"][bass.ds(n, 1)][0]).then_inc(c_in[s], 16)
                    sp.dma_start(wt[:, s, :], S["gates"][bass.ds(n, 1)][0]).then_inc(wt_in[s], 16)
                    sp.wait_ge(vt_ok, n + 1)
                    sp.dma_start(vt[:, s, :], T["vtab"][bass.ds(n, 1)][0]).then_inc(vt_in[s], 16)

        @block.gpsimd
        def _(pool):
            pool.sem_inc(vt_ok, 2)
            with pool.Fori(0, NG // 2) as i:
                for s in range(2):
                    for t in range(GT):
                        n = (2 * i + s) * GT + t
                        pool.wait_ge(vt_hi, n + 1)
                        nc.gpsimd.tensor_tensor(vt_l[:, s, t, :], vt[:, t % 2, :], vt_h[:, s, t, :].bitcast(F32),
                                                ALU.subtract).then_inc(vt_ok, 1)

        @block.tensor
        def _(pe):
            pe.sem_inc(f_mm, 2 * KT)
            with pe.Fori(0, NG // 2) as i:
                for s in range(2):
                    g = 2 * i + s
                    pe.wait_ge(vt_ok, GT * g + GT + 2)
                    pe.wait_ge(c_lo, GT * g + GT + 2)
                    for tt in range(KT):
                        b = tt % BP
                        pe.wait_ge(f_ok, KT * g + tt + 1)
                        cut = slice(tt * P, (tt + 1) * P)
                        for h in range(2):
                            dd = slice(h * HALF, (h + 1) * HALF)
                            for t in range(GT):
                                last = product3(nc, fps[:, 2 * b + h, :], (c_h[:, s, t, cut], c_l[:, s, t, cut]),
                                                (vt_h[:, s, t, dd], vt_l[:, s, t, dd]), t == 0, t == GT - 1)
                        last.then_inc(f_mm, 1)

        @block.scalar
        def _(act):
            def split(s, g, t):
                n = GT * g + t
                act.wait_ge(f_mm, KT * g + KT)
                act.wait_ge(vt_in[t % 2], GT // 2 * 16 * g + 16 * (t // 2 + 1))
                nc.scalar.activation(vt_h[:, s, t, :], vt[:, t % 2, :], ACT.Copy).then_inc(vt_hi, 1)
                act.wait_ge(c_ok, n + 1)
                nc.scalar.activation(c_h[:, s, t, :], c[:, t % 2, :], ACT.Copy).then_inc(c_hi, 1)

            with act.Fori(0, NG // 2) as i:
                for s in range(2):
                    for t in range(GT):
                        split(s, 2 * i + s, t)

        @block.vector
        def _(dve):
            v = nc.vector
            dve.sem_inc(c_lo, 2)
            dve.sem_inc(f_ok, BP)

            def coefficients(g, t):
                r = t % 2
                count = GT // 2 * 16 * g + 16 * (t // 2 + 1)
                dve.wait_ge(c_in[r], count)
                dve.wait_ge(wt_in[r], count)
                v.tensor_tensor(c[:, r, :], c[:, r, :], wt[:, r, :], ALU.mult).then_inc(c_ok, 1)

            def coef_low(s, g, t):
                dve.wait_ge(c_hi, GT * g + t + 1)
                v.tensor_tensor(c_l[:, s, t, :], c[:, t % 2, :], c_h[:, s, t, :].bitcast(F32), ALU.subtract).then_inc(c_lo, 1)

            def add_sums(g, tt):
                b = tt % BP
                hold(dve, K, f_mm, KT * g + tt + 1 + 2 * KT)
                row = sums[:, tt, :]
                v.tensor_tensor(row, row, fps[:, 2 * b:2 * b + 2, :].rearrange("p a b -> p (a b)"), ALU.add).then_inc(f_ok, 1)

            def turn(s, g):
                for t in range(GT):
                    coefficients(g + 1, t)
                    add_sums(g, t)
                    coef_low(1 - s, g + 1, t)
                for tt in range(GT, KT):
                    add_sums(g, tt)

            for t in range(GT):
                coefficients(0, t)
                coef_low(0, 0, t)
            with dve.Fori(0, NG // 2 - 1) as i:
                for s in range(2):
                    turn(s, 2 * i + s)
            turn(0, NG - 2)
            for tt in range(KT):
                add_sums(NG - 1, tt)


def stage_final(nc, S, K, T, out):
    ctx = ExitStack()
    with ctx:
        sb = lambda n, s, d=F32: ctx.enter_context(nc.sbuf_tensor("fi_" + n, s, d))
        sem = lambda n: ctx.enter_context(nc.semaphore("fi_" + n))
        x1, ln = sb("x1", [P, KT, D]), sb("ln", [P, 2, D])
        stats = sb("stats", [P, KT, 16])
        ln_in, gated, var_ok, root_ok, row_ok, stored, chain_s = (sem(n) for n in (
            "ln_in", "gated", "var_ok", "root_ok", "row_ok", "stored", "chain"))
        xin = [sem(f"x_in{k}") for k in range(KT)]
        block = ctx.enter_context(nc.Block())
        rows = lambda t, n: t.rearrange("(a p) n -> a p n", p=P)[n]

        @block.sync
        def _(sp):
            for n in range(KT):
                sp.dma_start(x1[:, n, :], rows(S["x1"], n)).then_inc(xin[n], 16)
            sp.dma_start(ln[:, :, :], T["ln"][2:4, :].partition_broadcast(P)).then_inc(ln_in, 16)
            for n in range(KT):
                sp.wait_ge(row_ok, n + 1)
                sp.dma_start(rows(out[0], n), K["sums"][:, n, :]).then_inc(stored, 16)
            sp.wait_ge(stored, 16 * KT)

        @block.scalar
        def _(act):
            for n in range(KT):
                act.wait_ge(var_ok, n + 1)
                nc.scalar.activation(stats[:, n, 14:15], stats[:, n, 13:14], ACT.Sqrt).then_inc(root_ok, 1)

        @block.gpsimd
        def _(pool):
            for n in range(KT):
                r = K["sums"][:, n, :]
                nc.gpsimd.tensor_tensor(r, r, K["ada_row"][:, 2:4, :].rearrange("p a b -> p (a b)"), ALU.mult).then_inc(gated, 1)

        @block.vector
        def _(dve):
            v = nc.vector
            ch = Chain(dve, chain_s)
            dve.wait_ge(ln_in, 16)
            for n in range(KT):
                r = K["sums"][:, n, :]
                dve.wait_ge(gated, n + 1)
                dve.wait_ge(xin[n], 16)
                ch.link(v.scalar_tensor_tensor(out=r, in0=x1[:, n, :], scalar=ALPHA, in1=r, op0=ALU.mult, op1=ALU.add))
                layer_norm(nc, ch, K, var_ok, (root_ok, n + 1), r, stats[:, n, :], ln[:, 0, :], ln[:, 1, :]).then_inc(row_ok, 1)


def build(nc, T, out, stages=None):
    S = {}

    def dram(name, shape, dt=F32):
        S[name] = nc.dram_tensor("scratch_" + name, shape, dt, kind="Internal").ap()

    dram("spec", (2, KT, P, 2, HW))
    dram("cm", (CM_TILES, P, SEQ))
    dram("qkv", (SEQ, QKV))
    dram("x1", (SEQ, D))
    dram("scores", (KT, P, 2 * PH, NK))
    dram("gates", (NK, NK, SEQ))
    dram("ahead", (AHEAD, P, SEQ))
    ctx = ExitStack()
    with ctx:
        K = {}

        def keep(name, shape, dt=F32):
            K[name] = ctx.enter_context(nc.sbuf_tensor("k_" + name, shape, dt))

        K["passed"] = ctx.enter_context(nc.semaphore("passed"))
        K["last_gates"] = ctx.enter_context(nc.semaphore("last_gates"))
        keep("ident", [P, P])
        keep("cos", [P, KT, ROPE])
        keep("sin", [P, KT, ROPE])
        keep("ada_col", [P, 4 * KT])
        keep("ada_row", [P, 4, HALF])
        early = ExitStack()
        with early:
            K["h2"] = early.enter_context(nc.sbuf_tensor("k_h2", [64, SEQ], F32))
            K["f3w"] = early.enter_context(nc.sbuf_tensor("k_f3w", [64, 4 * HW], F32))
            K["silu"] = early.enter_context(nc.sbuf_tensor("k_silu", [P, KT], F32))
            K["silu_wide"] = early.enter_context(nc.sbuf_tensor("k_silu_wide", [P, KT, P], F32))
            stage_setup(nc, S, K, T)
            stage_spectra(nc, S, K, T)
        stage_project(nc, S, K, T)
        keep("big", [P, KT, SEQ])
        K["yh"], K["ya"] = K["big"][:, 0:4, :], K["big"][:, 4:6, :]
        K["merged"] = K["u2"] = K["sums"] = K["big"]
        stage_hyena(nc, S, K, T)
        with nc.sbuf_tensor("k_qk", [HD, 2 * HEADS, SEQ], F32) as qk:
            K["qk"] = qk
            stage_rotary(nc, S, K, T)
            stage_attention(nc, S, K, T)
        stage_merge(nc, S, K, T)
        stage_out(nc, S, K, T)
        with nc.sbuf_tensor("k_u_h", [P, KT, SEQ], F32R) as u_h, nc.sbuf_tensor("k_u_l", [P, KT, SEQ], F32R) as u_l:
            K["u_h"], K["u_l"] = u_h, u_l
            stage_query(nc, S, K, T)
            with nc.sbuf_tensor("k_sel", [P, 3, SEQ], F32) as sel:
                K["sel"] = sel
                stage_select(nc, S, K, T)
                stage_gates(nc, S, K, T)
            stage_experts(nc, S, K, T)
        stage_values(nc, S, K, T)
        stage_final(nc, S, K, T, out)


def layouts(x, c, positions, w_ada, b_ada, w_in, hy_conv_w, hy_conv_b, hy_f1_w, hy_f1_b, hy_f1_freq,
            hy_f2_w, hy_f2_b, hy_f2_freq, hy_f3_w, hy_bias, w_branch_hyena, w_branch_attn, w_out,
            ln1_g, ln1_b, peer_wq, peer_keys, peer_u, peer_v, ln2_g, ln2_b):
    f = np.float32

    def tiles(w, cols):
        k, n = w.shape
        return w.reshape(k // P, P, n // cols, cols).transpose(2, 1, 0, 3)

    def col(vec):
        return vec.reshape(-1, P).T

    wa, ba, win = w_ada[0], b_ada[0], w_in[0]
    hyc, att = 3 * HW, 3 * HEADS * HD
    col_at, row_at = (0, 1024, 3072, 4096), (2048, 2560, 5120, 5632)
    ada = [np.concatenate([wa[:, a:a + D], wa[:, b:b + HALF]], 1) for a, b in zip(col_at, row_at)]
    t = np.arange(SEQ, dtype=np.float64)
    mid = 2 * t + 1
    sym = np.pi * np.outer(mid, mid) / (4 * SEQ)
    lag = np.pi * np.outer(t, mid) / (2 * SEQ)

    def table_cols(a):
        both = np.stack([np.cos(a), np.sin(a)]).astype(f)
        return both.reshape(2, KT, P, KT, P).transpose(3, 2, 0, 1, 4)

    lin = np.linspace(0, 1, SEQ, dtype=f)[:, None]
    w = (2.0 * math.pi * np.arange(SEQ, dtype=f)[:, None] / SEQ).astype(f)
    band = np.linspace(1e-4, 15, 16, dtype=f)[None, :]
    arg = (band * w).astype(f).astype(np.float64)
    feats = np.concatenate([lin, np.cos(arg), -np.sin(arg)], 1).astype(f)
    deltas = np.linspace(math.log(1e-2) / 1.5, math.log(1e-2) / 0.3, HW, dtype=f)
    decay = np.exp(-lin.astype(np.float64) * np.abs(deltas)[None, :].astype(np.float64)).astype(f)
    r, b, p, j = np.ogrid[0:4, 0:2, 0:P, 0:640]
    key, mid_q = np.arange(256)[None, None, None, :], b * P + p
    full = np.broadcast_to((key - mid_q) % 4 == 0, (4, 2, P, 256))
    near = np.broadcast_to(np.abs(key - mid_q) <= 64, (4, 2, P, 256))
    local = np.abs(384 * b + j - (r + 4 * mid_q)) <= 64
    mask = np.where(np.concatenate([full, near, local], 3), f(0), f(NEG)).astype(f)
    return {
        "feats": feats.T, "f1_w": hy_f1_w[0], "f2_w": hy_f2_w[0], "f3_w": hy_f3_w[0],
        "fvec": np.stack([hy_f1_b[0], hy_f1_freq[0], hy_f2_b[0], hy_f2_freq[0]], 1),
        "positions": positions[0].reshape(KT, P).T,
        "inv": (500000.0 ** (-np.arange(0, 16, 2, dtype=np.float64) / 16)).astype(f),
        "c": col(c[0]), "ident": np.eye(P, dtype=f),
        "b_col": np.concatenate([col(ba[a:a + D]) for a in col_at], 1),
        "b_row": np.stack([ba[a:a + HALF] for a in row_at]),
        "decay": decay.reshape(KT, P, HW).transpose(1, 0, 2),
        "tab0": table_cols(lag), "tab1": table_cols(sym),
        "tab1_rows": np.stack([np.cos(sym), np.sin(sym)]).astype(f).reshape(2, KT, P, SEQ).transpose(1, 2, 0, 3),
        "w_ada": np.concatenate([tiles(a, 256) for a in ada]),
        "xT": x[0].T.reshape(KT, P, SEQ).transpose(1, 0, 2), "x": x[0],
        "w_cm": tiles(np.concatenate([win[:, :hyc], win[:, hyc + att:]], 1), P),
        "w_qkv": tiles(win[:, hyc:hyc + att], QC),
        "conv_w": hy_conv_w[0].reshape(3, HY_TILES, P).transpose(2, 1, 0),
        "conv_b": col(hy_conv_b[0]),
        "hy_bias": hy_bias[0].reshape(2, 4, P).transpose(2, 0, 1),
        "mask": mask,
        "w_bh": tiles(w_branch_hyena[0], P), "w_ba": tiles(w_branch_attn[0], P),
        "w_out": w_out[0].reshape(KT, P, D).transpose(1, 0, 2),
        "ln": np.stack([ln1_g[0], ln1_b[0], ln2_g[0], ln2_b[0]]),
        "wq": tiles(peer_wq[0], P), "keysT": peer_keys[0].reshape(2 * PH, NK, P).transpose(0, 2, 1),
        "iota": np.arange(256, dtype=f),
        "utab": peer_u[0].reshape(NK, NK, KT, P).transpose(0, 3, 2, 1),
        "vtab": peer_v[0].reshape(NK, NK, D),
    }


def kernel(**inputs):
    import concourse.bacc as bacc
    from concourse.bass_utils import run_bass_kernel_spmd

    nc = bacc.Bacc("TRN2", target_bir_lowering=False, num_devices=1)
    arrays, T = {}, {}
    for name, a in layouts(**{k: np.asarray(v) for k, v in inputs.items()}).items():
        a = np.ascontiguousarray(a)
        arrays["in_" + name] = a
        T[name] = nc.dram_tensor("in_" + name, a.shape, mybir.dt.from_np(a.dtype), kind="ExternalInput").ap()
    out = nc.dram_tensor("out", (1, SEQ, D), F32, kind="ExternalOutput").ap()
    build(nc, T, out)
    return run_bass_kernel_spmd(nc, [arrays], core_ids=[0]).results[0]["out"]
```
